# Optimizing a Trainium2 kernel written in Bass

```python
import jax, jax.numpy as jnp
from jax import lax
import numpy as np
import math

D_MODEL = 1024
BATCH = 1
SEQ = 512
DEPTH = 1

N_MEM = 256
A_HEADS = 8
HEAD_DIM = 64
A_WIDTH = A_HEADS * HEAD_DIM
IDX_HEADS = 4
IDX_DIM = 64
TOPK_MAX = 256
Q_BLOCK = 128
B_GROUPS = 8
B_WIDTH = D_MODEL - A_WIDTH
CONV_B_WIDTH = 31
MIX_WIDTH = A_WIDTH + B_WIDTH
ROPE_THETA = 500000.0
ROT_DIM = HEAD_DIM // 4
CROSS_HEADS = 4
CROSS_HEAD_DIM = D_MODEL // CROSS_HEADS
D_FF = 2816
FFN_CONV_WIDTH = 3
EPS = 1e-6
IN_SPLITS = (A_WIDTH, HEAD_DIM, HEAD_DIM, IDX_HEADS * IDX_DIM, IDX_DIM, IDX_HEADS, 2 * B_WIDTH)
IN_COLS = sum(IN_SPLITS)


def rmsnorm(x, g):
    xf = x.astype(jnp.float32)
    y = xf * lax.rsqrt(jnp.mean(xf * xf, axis=-1, keepdims=True) + EPS)
    return (y * g.astype(jnp.float32)).astype(x.dtype)

def layernorm(x, g, b):
    xf = x.astype(jnp.float32)
    mu = jnp.mean(xf, axis=-1, keepdims=True)
    var = jnp.mean(jnp.square(xf - mu), axis=-1, keepdims=True)
    y = (xf - mu) * lax.rsqrt(var + EPS)
    return (y * g.astype(jnp.float32) + b.astype(jnp.float32)).astype(x.dtype)

def causal_dwconv(x, w, b):
    width, ch = w.shape
    y = lax.conv_general_dilated(
        x, w.astype(x.dtype)[:, None, :], window_strides=(1,),
        padding=[(width - 1, 0)], dimension_numbers=('NWC', 'WIO', 'NWC'),
        feature_group_count=ch)
    return y + b.astype(x.dtype)

def rope_tables(positions):
    freqs = ROPE_THETA ** (-jnp.arange(0, ROT_DIM, 2, dtype=jnp.float32) / ROT_DIM)
    ang = positions.astype(jnp.float32)[:, :, None, None] * freqs
    return jnp.cos(ang), jnp.sin(ang)

def partial_rope(x, cos, sin):
    xr = x[..., :ROT_DIM].astype(jnp.float32)
    x1, x2 = xr[..., :ROT_DIM // 2], xr[..., ROT_DIM // 2:]
    rot = jnp.concatenate([x1 * cos - x2 * sin, x2 * cos + x1 * sin], axis=-1)
    return jnp.concatenate([rot.astype(x.dtype), x[..., ROT_DIM:]], axis=-1)

def dsa_attention(q, k, v, qi, ki, wi):
    bsz, seq = q.shape[0], q.shape[1]
    nb = seq // Q_BLOCK
    topk = min(TOPK_MAX, seq // 4)
    qi = qi * (IDX_DIM ** -0.5)
    wi = wi * (IDX_HEADS ** -0.5)
    gather = jax.vmap(lambda a, i: a[i])
    key_pos = jnp.arange(seq)

    def block(args):
        bi, qb, qib, wib = args
        t = bi * Q_BLOCK + jnp.arange(Q_BLOCK)
        causal = key_pos[None, :] <= t[:, None]
        rel = jax.nn.relu(jnp.einsum('bqhd,bsd->bqhs', qib, ki).astype(jnp.float32))
        score = jnp.einsum('bqh,bqhs->bqs', wib.astype(jnp.float32), rel)
        score = jnp.where(causal[None], score, -jnp.inf)
        _, sel = lax.top_k(score, topk)
        k_sel = gather(k, sel)
        v_sel = gather(v, sel)
        valid = sel <= t[None, :, None]
        logits = jnp.einsum('bqhd,bqkd->bqhk', qb, k_sel).astype(jnp.float32) * (HEAD_DIM ** -0.5)
        logits = jnp.where(valid[:, :, None, :], logits, -jnp.inf)
        p = jax.nn.softmax(logits, axis=-1).astype(v.dtype)
        return jnp.einsum('bqhk,bqkd->bqhd', p, v_sel)

    to_blocks = lambda a: a.reshape(bsz, nb, Q_BLOCK, *a.shape[2:]).swapaxes(0, 1)
    out = lax.map(block, (jnp.arange(nb), to_blocks(q), to_blocks(qi), to_blocks(wi)))
    return out.swapaxes(0, 1).reshape(bsz, seq, A_WIDTH)

def hybrid_layer(x, mem, cos, sin, norm_mix_g, w_in, w_out, conv_b_w, conv_b_b, ln_b_g, ln_b_b,
                 norm_cross_g, norm_mem_g, w_q_cross, w_k_cross, w_v_cross, w_o_cross,
                 norm_ffn_g, w_gate, w_up, ffn_conv_w, ffn_conv_b, w_down):
    bsz, seq, _ = x.shape
    h = rmsnorm(x, norm_mix_g)
    proj = h @ w_in
    cuts = [int(c) for c in np.cumsum(IN_SPLITS)[:-1]]
    q, k, v, qi, ki, wi, glu = jnp.split(proj, cuts, axis=-1)
    q = partial_rope(q.reshape(bsz, seq, A_HEADS, HEAD_DIM), cos, sin)
    k = partial_rope(k[:, :, None, :], cos, sin)[:, :, 0]
    qi = partial_rope(qi.reshape(bsz, seq, IDX_HEADS, IDX_DIM), cos, sin)
    ki = partial_rope(ki[:, :, None, :], cos, sin)[:, :, 0]
    a_out = dsa_attention(q, k, v, qi, ki, wi)
    ga, gg = jnp.split(glu, 2, axis=-1)
    u = ga * jax.nn.sigmoid(gg)
    u = causal_dwconv(u, conv_b_w, conv_b_b)
    b_out = jax.nn.silu(layernorm(u, ln_b_g, ln_b_b))
    x = x + jnp.concatenate([a_out, b_out], axis=-1) @ w_out
    hq = rmsnorm(x, norm_cross_g)
    m = rmsnorm(mem, norm_mem_g)
    qc = (hq @ w_q_cross).reshape(bsz, seq, CROSS_HEADS, CROSS_HEAD_DIM)
    kc = (m @ w_k_cross).reshape(bsz, -1, CROSS_HEADS, CROSS_HEAD_DIM)
    vc = (m @ w_v_cross).reshape(bsz, -1, CROSS_HEADS, CROSS_HEAD_DIM)
    logits = jnp.einsum('bshd,bnhd->bhsn', qc, kc).astype(jnp.float32) * (CROSS_HEAD_DIM ** -0.5)
    p = jax.nn.softmax(logits, axis=-1).astype(vc.dtype)
    oc = jnp.einsum('bhsn,bnhd->bshd', p, vc).reshape(bsz, seq, D_MODEL)
    x = x + oc @ w_o_cross
    hf = rmsnorm(x, norm_ffn_g)
    g = causal_dwconv(hf @ w_gate, ffn_conv_w, ffn_conv_b)
    x = x + (jax.nn.silu(g) * (hf @ w_up)) @ w_down
    return x

def first_inputs(seed: int = 0) -> dict:
    key = jax.random.key(seed)
    ks = jax.random.split(key, 24)
    f32 = jnp.float32
    nrm = lambda k, shape, scale: jax.random.normal(k, shape, f32) * scale
    gain = lambda k, shape: 1.0 + 0.02 * jax.random.normal(k, shape, f32)
    L = DEPTH
    offsets = jax.random.randint(ks[2], (BATCH, 1), 0, 2048, dtype=jnp.int32)
    positions = offsets + jnp.arange(SEQ, dtype=jnp.int32)[None, :]
    return {
        'x': nrm(ks[0], (BATCH, SEQ, D_MODEL), 1.0),
        'mem': nrm(ks[1], (BATCH, N_MEM, D_MODEL), 1.0),
        'positions': positions,
        'norm_mix_g': gain(ks[3], (L, D_MODEL)),
        'w_in': nrm(ks[4], (L, D_MODEL, IN_COLS), D_MODEL ** -0.5),
        'w_out': nrm(ks[5], (L, MIX_WIDTH, D_MODEL), MIX_WIDTH ** -0.5),
        'conv_b_w': nrm(ks[6], (L, CONV_B_WIDTH, B_WIDTH), CONV_B_WIDTH ** -0.5),
        'conv_b_b': nrm(ks[7], (L, B_WIDTH), 0.02),
        'ln_b_g': gain(ks[8], (L, B_WIDTH)),
        'ln_b_b': nrm(ks[9], (L, B_WIDTH), 0.02),
        'norm_cross_g': gain(ks[10], (L, D_MODEL)),
        'norm_mem_g': gain(ks[11], (L, D_MODEL)),
        'w_q_cross': nrm(ks[12], (L, D_MODEL, D_MODEL), D_MODEL ** -0.5),
        'w_k_cross': nrm(ks[13], (L, D_MODEL, D_MODEL), D_MODEL ** -0.5),
        'w_v_cross': nrm(ks[14], (L, D_MODEL, D_MODEL), D_MODEL ** -0.5),
        'w_o_cross': nrm(ks[15], (L, D_MODEL, D_MODEL), D_MODEL ** -0.5),
        'norm_ffn_g': gain(ks[16], (L, D_MODEL)),
        'w_gate': nrm(ks[17], (L, D_MODEL, D_FF), D_MODEL ** -0.5),
        'w_up': nrm(ks[18], (L, D_MODEL, D_FF), D_MODEL ** -0.5),
        'ffn_conv_w': nrm(ks[19], (L, FFN_CONV_WIDTH, D_FF), FFN_CONV_WIDTH ** -0.5),
        'ffn_conv_b': nrm(ks[20], (L, D_FF), 0.02),
        'w_down': nrm(ks[21], (L, D_FF, D_MODEL), D_FF ** -0.5),
        'norm_final_g': gain(ks[22], (D_MODEL,)),
    }

def first_block(x, mem, positions, norm_mix_g, w_in, w_out, conv_b_w, conv_b_b, ln_b_g, ln_b_b,
              norm_cross_g, norm_mem_g, w_q_cross, w_k_cross, w_v_cross, w_o_cross,
              norm_ffn_g, w_gate, w_up, ffn_conv_w, ffn_conv_b, w_down, norm_final_g):
    cos, sin = rope_tables(positions)
    for l in range(DEPTH):
        x = hybrid_layer(x, mem, cos, sin, norm_mix_g[l], w_in[l], w_out[l], conv_b_w[l], conv_b_b[l],
                         ln_b_g[l], ln_b_b[l], norm_cross_g[l], norm_mem_g[l], w_q_cross[l], w_k_cross[l],
                         w_v_cross[l], w_o_cross[l], norm_ffn_g[l], w_gate[l], w_up[l], ffn_conv_w[l],
                         ffn_conv_b[l], w_down[l])
    return rmsnorm(x, norm_final_g)


CHUNK = 64
MIX_WIDTH_2 = D_MODEL
LRU_WIDTH = MIX_WIDTH_2 // 2
ATT_WIDTH = MIX_WIDTH_2 - LRU_WIDTH
LRU_BLOCKS = 8
LRU_BLOCK_W = LRU_WIDTH // LRU_BLOCKS
CONV_W = 4
LRU_C = 8.0
ATT_HEADS = 8
ATT_HEAD_DIM = ATT_WIDTH // ATT_HEADS
D_FF_2 = -(-8 * D_MODEL // (3 * 256)) * 256
IN_COLS_2 = 2 * LRU_WIDTH + 3 * ATT_WIDTH


def rms_norm(x, g):
    xf = x.astype(jnp.float32)
    xf = xf * lax.rsqrt(jnp.mean(xf * xf, axis=-1, keepdims=True) + EPS)
    return xf.astype(x.dtype) * g

def causal_depthwise_conv(x, w, b):
    s = x.shape[1]
    xp = jnp.pad(x, ((0, 0), (CONV_W - 1, 0), (0, 0)))
    y = b
    for i in range(CONV_W):
        y = y + xp[:, i:i + s, :] * w[i]
    return y

def block_diag_linear(x, w, b):
    bsz, s, _ = x.shape
    xb = x.reshape(bsz, s, LRU_BLOCKS, LRU_BLOCK_W)
    y = jnp.einsum('bsnc,ncd->bsnd', xb, w) + b
    return y.reshape(bsz, s, LRU_WIDTH)

def rg_lru(x, w_rg, b_rg, w_ig, b_ig, lam):
    r = jax.nn.sigmoid(block_diag_linear(x, w_rg, b_rg).astype(jnp.float32))
    i = jax.nn.sigmoid(block_diag_linear(x, w_ig, b_ig).astype(jnp.float32))
    log_a = -LRU_C * r * jax.nn.softplus(-lam.astype(jnp.float32))
    a = jnp.exp(log_a)
    mult = jnp.sqrt(-jnp.expm1(2.0 * log_a))
    bterm = mult * (i * x.astype(jnp.float32))

    def combine(e1, e2):
        a1, b1 = e1
        a2, b2 = e2
        return a1 * a2, a2 * b1 + b2

    _, h = lax.associative_scan(combine, (a, bterm), axis=1)
    return h.astype(x.dtype)

def stick_breaking_attention(q, k, v):
    bsz, s, h, dh = q.shape
    nb = s // Q_BLOCK
    scale = 1.0 / math.sqrt(dh)
    qb = q.reshape(bsz, nb, Q_BLOCK, h, dh).transpose(1, 0, 2, 3, 4)
    key_pos = jnp.arange(s)

    def one_block(args):
        q_blk, blk = args
        z = jnp.einsum('bqhd,bkhd->bhqk', q_blk, k).astype(jnp.float32) * scale
        t = blk * Q_BLOCK + jnp.arange(Q_BLOCK)
        mask = key_pos[None, :] < t[:, None]
        log_beta = jax.nn.log_sigmoid(z)
        log_1mb = jnp.where(mask, jax.nn.log_sigmoid(-z), 0.0)
        suffix = lax.cumsum(log_1mb, axis=3, reverse=True) - log_1mb
        att = jnp.where(mask, jnp.exp(log_beta + suffix), 0.0)
        return jnp.einsum('bhqk,bkhd->bqhd', att.astype(v.dtype), v)

    out = lax.map(one_block, (qb, jnp.arange(nb)))
    return out.transpose(1, 0, 2, 3, 4).reshape(bsz, s, h, dh)

def second_inputs(seed: int = 0) -> dict:
    key = jax.random.key(seed)
    ks = jax.random.split(key, 20)
    f32 = jnp.float32
    nrm = lambda k, shp, sc: jax.random.normal(k, shp, f32) * sc
    gain = lambda k, shp: 1.0 + 0.05 * jax.random.normal(k, shp, f32)
    x = jax.random.normal(ks[0], (BATCH, SEQ, D_MODEL), f32)
    u = jax.random.uniform(ks[9], (DEPTH, LRU_WIDTH), f32, 0.9, 0.999)
    a0 = u ** (1.0 / LRU_C)
    lru_lambda = jnp.log(a0) - jnp.log1p(-a0)
    return {
        "x": x,
        "norm_mix": gain(ks[1], (DEPTH, D_MODEL)),
        "w_in": nrm(ks[2], (DEPTH, D_MODEL, IN_COLS_2), D_MODEL ** -0.5),
        "conv_w": nrm(ks[3], (DEPTH, CONV_W, LRU_WIDTH), CONV_W ** -0.5),
        "conv_b": nrm(ks[4], (DEPTH, LRU_WIDTH), 0.01),
        "w_rg": nrm(ks[5], (DEPTH, LRU_BLOCKS, LRU_BLOCK_W, LRU_BLOCK_W), LRU_BLOCK_W ** -0.5),
        "b_rg": nrm(ks[6], (DEPTH, LRU_BLOCKS, LRU_BLOCK_W), 0.01),
        "w_ig": nrm(ks[7], (DEPTH, LRU_BLOCKS, LRU_BLOCK_W, LRU_BLOCK_W), LRU_BLOCK_W ** -0.5),
        "b_ig": nrm(ks[8], (DEPTH, LRU_BLOCKS, LRU_BLOCK_W), 0.01),
        "lru_lambda": lru_lambda,
        "norm_lru_out": gain(ks[10], (DEPTH, LRU_WIDTH)),
        "norm_att_out": gain(ks[11], (DEPTH, ATT_WIDTH)),
        "w_out": nrm(ks[12], (DEPTH, MIX_WIDTH_2, D_MODEL), MIX_WIDTH_2 ** -0.5),
        "norm_ffn": gain(ks[13], (DEPTH, D_MODEL)),
        "w_ffn_in": nrm(ks[14], (DEPTH, D_MODEL, 2 * D_FF_2), D_MODEL ** -0.5),
        "w_ffn_out": nrm(ks[15], (DEPTH, D_FF_2, D_MODEL), D_FF_2 ** -0.5),
        "norm_final": gain(ks[16], (D_MODEL,)),
    }

def second_block(x, norm_mix, w_in, conv_w, conv_b, w_rg, b_rg, w_ig, b_ig, lru_lambda,
              norm_lru_out, norm_att_out, w_out, norm_ffn, w_ffn_in, w_ffn_out, norm_final):
    bsz, s, _ = x.shape
    for l in range(DEPTH):
        h = rms_norm(x, norm_mix[l])
        u = jnp.einsum('bsd,de->bse', h, w_in[l])
        o = 0
        lru_x = u[..., o:o + LRU_WIDTH]; o += LRU_WIDTH
        lru_g = u[..., o:o + LRU_WIDTH]; o += LRU_WIDTH
        q = u[..., o:o + ATT_WIDTH].reshape(bsz, s, ATT_HEADS, ATT_HEAD_DIM); o += ATT_WIDTH
        k = u[..., o:o + ATT_WIDTH].reshape(bsz, s, ATT_HEADS, ATT_HEAD_DIM); o += ATT_WIDTH
        v = u[..., o:o + ATT_WIDTH].reshape(bsz, s, ATT_HEADS, ATT_HEAD_DIM)

        xc = causal_depthwise_conv(lru_x, conv_w[l], conv_b[l])
        hl = rg_lru(xc, w_rg[l], b_rg[l], w_ig[l], b_ig[l], lru_lambda[l])
        y_lru = jax.nn.gelu(lru_g) * hl

        y_att = stick_breaking_attention(q, k, v).reshape(bsz, s, ATT_WIDTH)

        y = jnp.concatenate([rms_norm(y_lru, norm_lru_out[l]),
                             rms_norm(y_att, norm_att_out[l])], axis=-1)
        x = x + jnp.einsum('bse,ed->bsd', y, w_out[l])

        h2 = rms_norm(x, norm_ffn[l])
        gu = jnp.einsum('bsd,df->bsf', h2, w_ffn_in[l])
        x = x + jnp.einsum('bsf,fd->bsd', jax.nn.silu(gu[..., :D_FF_2]) * gu[..., D_FF_2:], w_ffn_out[l])
    return rms_norm(x, norm_final)


def setup_inputs(seed=0):
    out = dict(first_inputs(seed))
    for name, value in second_inputs(seed + 1).items():
        if name != "x":
            out[name + "_2"] = value
    return out


def reference(
    x, mem, positions, norm_mix_g, w_in, w_out, conv_b_w, conv_b_b, ln_b_g, ln_b_b,
    norm_cross_g, norm_mem_g, w_q_cross, w_k_cross, w_v_cross, w_o_cross, norm_ffn_g, w_gate,
    w_up, ffn_conv_w, ffn_conv_b, w_down, norm_final_g, norm_mix_2, w_in_2, conv_w_2, conv_b_2,
    w_rg_2, b_rg_2, w_ig_2, b_ig_2, lru_lambda_2, norm_lru_out_2, norm_att_out_2, w_out_2,
    norm_ffn_2, w_ffn_in_2, w_ffn_out_2, norm_final_2,
):
    x = first_block(
        x, mem, positions, norm_mix_g, w_in, w_out, conv_b_w, conv_b_b, ln_b_g, ln_b_b,
        norm_cross_g, norm_mem_g, w_q_cross, w_k_cross, w_v_cross, w_o_cross, norm_ffn_g,
        w_gate, w_up, ffn_conv_w, ffn_conv_b, w_down, norm_final_g,
    )
    return second_block(
        x, norm_mix_2, w_in_2, conv_w_2, conv_b_2, w_rg_2, b_rg_2, w_ig_2, b_ig_2, lru_lambda_2,
        norm_lru_out_2, norm_att_out_2, w_out_2, norm_ffn_2, w_ffn_in_2, w_ffn_out_2,
        norm_final_2,
    )


_drawn_inputs = setup_inputs


def setup_inputs(seed=0):
    import zlib

    import numpy as np

    out = dict(_drawn_inputs(seed))
    spreads = {}
    factors = {'norm_mix_g': 2.844,
     'ln_b_g': 3.506,
     'ln_b_b': 3.075,
     'norm_cross_g': 8.0,
     'norm_mem_g': 8.0,
     'norm_ffn_g': 3.397,
     'ffn_conv_b': 4.715,
     'b_rg_2': 50.956,
     'b_ig_2': 27.656}
    for name, (base, spread) in spreads.items():
        noise = np.random.default_rng([zlib.crc32(name.encode()), seed]).standard_normal(out[name].shape)
        drawn = base * np.exp(spread * noise) if base else spread * noise
        out[name] = __import__('jax').numpy.asarray(drawn.astype(out[name].dtype))
    for name, factor in factors.items():
        out[name] = (out[name] * factor).astype(out[name].dtype)
    return out
```

```python
import numpy as np
import concourse.bass as bass
from concourse import mybir
from contextlib import ExitStack

F32 = mybir.dt.float32
F32R = mybir.dt.float32r
I32 = mybir.dt.int32
ALU = mybir.AluOpType
ACT = mybir.ActivationFunctionType

P = 128
T = 512
QB = T // P
D = 1024
KB = D // P
F = 2816
FB = F // P
FH = FB // 2
HALF = 64
A_HEADS = 8
IDX_HEADS = 4
TOPK = 128
MB = 256 // P
X_HEADS = 4
X_KB = 256 // P
TAPS = 31
TAPS_FFN = 3
TAPS_LRU = 4
EPS = 1e-6
NEG = -1e30
CHOSEN = -3e38
ROUND = 1.5 * 2.0 ** 23
TWO_PI = (6.28125, 0.0019350051879882812, 3.0199159819567e-07)

GEMMS = (("in", 16), ("kc", 8), ("vc", 8), ("out", 8), ("qc", 8), ("oc", 8), ("ffn", 2 * FB),
         ("down", 16), ("in2", 20), ("out2", 8), ("ffn2", 2 * FB), ("down2", 16))
CHUNK, TILE = {}, {}
_c = _t = 0
for _name, _n in GEMMS:
    CHUNK[_name], TILE[_name] = _c, _t
    _c += _n
    _t += _n // 2 if _name.startswith("down") else _n
CHUNKS, TILES = _c, _t
WIDE = (("down", 0), ("down2", 16))

PARAMS = (("g_mix", KB), ("g_cross", KB), ("g_mem", KB), ("g_ffn", KB), ("g_final", KB),
          ("g_mix2", KB), ("g_ffn2", KB), ("g_final2", KB), ("ln_g", 4), ("ln_b", 4),
          ("g_lru", 4), ("g_att", 4), ("conv_w", 4 * TAPS), ("conv_b", 4), ("fconv_w", FB * TAPS_FFN),
          ("fconv_b", FB), ("lconv_w", 4 * TAPS_LRU), ("lconv_b", 4), ("b_rg", 4), ("b_ig", 4),
          ("lam", 4), ("freq", 1))
PCOL = {}
_p = 0
for _name, _n in PARAMS:
    PCOL[_name] = _p
    _p += _n
PCOLS = _p


class Steps:

    def __init__(self, eng, sem):
        self.eng, self.sem, self.at = eng, sem, 0

    def step(self, ins):
        ins.then_inc(self.sem, 1)
        self.at = self.at + 1

    def settle(self, lag=0):
        self.eng.wait_ge(self.sem, self.at - lag)

    def then(self, ins):
        self.step(ins)
        self.settle()

    def run(self, first, end, each, body):
        start, self.passes = self.at, 0
        with self.eng.Fori(first, end) as i:
            self.at = start + (i - first) * each
            body(i)
        self.at = start + (end - first) * each


def build(nc, w8, w11, x, mem, positions, params, blockdiag, out):
    ctx = ExitStack()
    with ctx:
        def sb(name, shape, dt=F32, where=ctx):
            return where.enter_context(nc.sbuf_tensor(name, shape, dt))

        def sem(name):
            return ctx.enter_context(nc.semaphore(name))

        weights_raw = sb("weights_raw", [P, 2, FH * P])
        weights_high = sb("weights_high", [P, 2, FH * P], F32R)
        weights_low = sb("weights_low", [P, 2, FH * P], F32R)
        residual = sb("residual", [P, KB, T])
        a_high = sb("a_high", [P, KB, T], F32R)
        a_low = sb("a_low", [P, KB, T], F32R)
        par = sb("par", [P, PCOLS])
        small = sb("small", [P, 64])
        ident = sb("ident", [P, P])
        ones = sb("ones", [P, P])
        rotate = sb("rotate", [P, P])
        twice = sb("twice", [P, P])
        causal = sb("causal", [P, P])
        before = sb("before", [P, P])
        notbefore = sb("notbefore", [P, P])
        row_factor = sb("row_factor", [P, T])
        root = sb("root", [P, T])
        square = sb("square", [P, T])
        square_sum = sb("square_sum", [P, T])

        def col(name, n=0, width=1):
            c = PCOL[name]
            return par[:, c + n:c + n + width]

        def dcol(name, n):
            return par[:, bass.ds(PCOL[name] + n, 1)]

        eps = small[:, 0:1]
        tok_sum = small[:, 1:7]
        tok_root = small[:, 7:13]
        tok_factor = small[:, 13:19]
        best = small[:, 19:27]
        least = small[:, 27:29]
        total = small[:, 29:31]
        inverse = small[:, 31:33]
        decay = small[:, 33:37]
        both_gains = small[:, 37:45]
        half_pi = small[:, 45:46]
        sp = small[:, 46:62]

        s12 = ExitStack()
        kcT = sb("kcT", [P, KB, MB * P], where=s12)
        vc = sb("vc", [P, MB, D], where=s12)
        s1 = ExitStack()
        m_high = sb("m_high", [P, KB, MB * P], F32R, s1)
        m_low = sb("m_low", [P, KB, MB * P], F32R, s1)
        qT = sb("qT", [P, 4, T], where=s1)
        qiT = sb("qiT", [P, 2, T], where=s1)
        kv = sb("kv", [P, T], where=s1)
        kiwi = sb("kiwi", [P, T], where=s1)
        kT = sb("kT", [P, T], where=s1)
        kiT = sb("kiT", [P, T], where=s1)
        v_pad = sb("v_pad", [P, QB, 2, P], where=s1)
        wi = sb("wi", [P, QB, IDX_HEADS], where=s1)
        cosine = sb("cosine", [P, T], where=s1)
        sine = sb("sine", [P, T], where=s1)
        s1a = ExitStack()
        x_tok = sb("x_tok", [P, 6, D], where=s1a)
        xn_tok = sb("xn_tok", [P, 6, D], where=s1a)
        s1a.close()
        s1b = ExitStack()
        glu = sb("glu", [P, 4, TAPS - 1 + T], where=s1b)
        gate = sb("gate", [P, 4, T], where=s1b)
        conv = sb("conv", [P, 4, T], where=s1b)
        score = sb("score", [P, 3, T], where=s1b)
        rel = sb("rel", [P, 2, T], where=s1b)
        masked = sb("masked", [P, 2, T], where=s1b)
        prob = sb("prob", [P, 2, T], where=s1b)
        probT = sb("probT", [P, 2, T], where=s1b)
        vcT = sb("vcT", [P, 2, MB * P], where=s1b)
        s1b.close()
        s1.close()
        s2 = ExitStack()
        b_high = sb("b_high", [P, KB, T], F32R, s2)
        b_low = sb("b_low", [P, KB, T], F32R, s2)
        qcT = sb("qcT", [P, KB, T], where=s2)
        zeros = sb("zeros", [P, MB * P], where=s2)
        xmasked = sb("xmasked", [P, 2, MB * P], where=s2)
        xprob = sb("xprob", [P, 2, MB * P], where=s2)
        xprobT = sb("xprobT", [P, 2, MB, T], where=s2)
        s2.close()
        s12.close()

        s3 = ExitStack()
        h_high = sb("h_high", [P, FB, T], F32R, s3)
        h_low = sb("h_low", [P, FB, T], F32R, s3)
        gated = sb("gated", [P, TAPS_FFN - 1 + T], where=s3)
        work = sb("work", [P, 2, T], where=s3)
        y_tok = sb("y_tok", [P, QB, D], where=s3)
        s3.close()

        s4 = ExitStack()
        y_high = sb("y_high", [P, KB, T], F32R, s4)
        y_low = sb("y_low", [P, KB, T], F32R, s4)
        lru_weights = sb("lru_weights", [P, 2, 4, P], where=s4)
        lru_in = sb("lru_in", [P, 4, TAPS_LRU - 1 + T], where=s4)
        lru_gate = sb("lru_gate", [P, 4, T], where=s4)
        q2 = sb("q2", [P, 4, T], where=s4)
        k2 = sb("k2", [P, 4, T], where=s4)
        vT2 = sb("vT2", [P, 2, T], where=s4)
        v2 = sb("v2", [P, QB, A_HEADS, P], where=s4)
        s4a = ExitStack()
        xc = sb("xc", [P, T], where=s4a)
        gates = sb("gates", [P, 2, T], where=s4a)
        half_tanh = sb("half_tanh", [P, T], where=s4a)
        gate_root = sb("gate_root", [P, T], where=s4a)
        inverse_sum = sb("inverse_sum", [P, T], where=s4a)
        s4a.close()
        s4b = ExitStack()
        stay = sb("stay", [P, 2, T], where=s4b)
        take = sb("take", [P, 2, T], where=s4b)
        left = sb("left", [P, T], where=s4b)
        takeT = sb("takeT", [P, 2, T], where=s4b)
        no_add = sb("no_add", [P, T], where=s4b)
        s4b.close()
        s4.close()

        acc = ctx.enter_context(nc.psum_tensor("acc", [P, 2, T], F32))
        aux = [ctx.enter_context(nc.psum_tensor(f"aux{i}", [P, T], F32)) for i in range(6)]
        chunk_landed = [sem("chunk_landed0"), sem("chunk_landed1")]
        weight_high = sem("weight_high")
        weight_low = sem("weight_low")
        chunk_done = sem("chunk_done")
        tile_out = [sem("tile_out0"), sem("tile_out1")]
        operand_high = sem("operand_high")
        operand_low = sem("operand_low")
        squared = sem("squared")
        summed = sem("summed")
        sums_ready = sem("sums_ready")
        root_ready = sem("root_ready")
        act_steps = sem("act_steps")
        dve_steps = sem("dve_steps")
        consts_ready = sem("consts_ready")
        params_in = sem("params_in")
        positions_in = sem("positions_in")
        blockdiag_in = sem("blockdiag_in")
        x_in = [sem(f"x_in{i}") for i in range(6)]
        angle_ready = sem("angle_ready")
        tables_ready = sem("tables_ready")
        softplus_exp = sem("softplus_exp")
        token_root = sem("token_root")
        token_scaled = sem("token_scaled")
        xnT_done = sem("xnT_done")
        xT_done = sem("xT_done")
        residual_in = sem("residual_in")
        mT_done = sem("mT_done")
        rotated = sem("rotated")
        roped = sem("roped")
        doubled = sem("doubled")
        doubled_out = sem("doubled_out")
        vwi_done = sem("vwi_done")
        v_out = sem("v_out")
        cleared = sem("cleared")
        index_logits = sem("index_logits")
        rel_ready = sem("rel_ready")
        rel_used = sem("rel_used")
        vcT_done = sem("vcT_done")
        vc_out = sem("vc_out")
        conv_ready = sem("conv_ready")
        mean_ready = sem("mean_ready")
        centred = sem("centred")
        centred_squared = sem("centred_squared")
        variance_ready = sem("variance_ready")
        ln_root = sem("ln_root")
        ln_scaled = sem("ln_scaled")
        logits = sem("logits")
        logits_masked = sem("logits_masked")
        prob_raw = sem("prob_raw")
        prob_ready = sem("prob_ready")
        probT_done = sem("probT_done")
        probT_ready = sem("probT_ready")
        heads_done = sem("heads_done")
        x_logits = sem("x_logits")
        x_masked = sem("x_masked")
        x_prob_raw = sem("x_prob_raw")
        x_prob_ready = sem("x_prob_ready")
        x_probT_done = sem("x_probT_done")
        x_probT_ready = sem("x_probT_ready")
        x_heads_done = sem("x_heads_done")
        gate_ready = sem("gate_ready")
        silu_ready = sem("silu_ready")
        hidden_ready = sem("hidden_ready")
        rescaled = sem("rescaled")
        lconv_ready = sem("lconv_ready")
        lgates_done = sem("lgates_done")
        lgates_ready = sem("lgates_ready")
        tanh_ready = sem("tanh_ready")
        lroot_ready = sem("lroot_ready")
        lru_done = sem("lru_done")
        gelu_ready = sem("gelu_ready")
        y_scaled = sem("y_scaled")
        vT2_done = sem("vT2_done")
        v2_out = sem("v2_out")
        v2_clear = sem("v2_clear")
        sticks = sem("sticks")
        breaks = sem("breaks")
        taken = sem("taken")
        takenT = sem("takenT")
        takenT_ready = sem("takenT_ready")
        stick_heads = sem("stick_heads")
        att_out = sem("att_out")
        out_scaled = sem("out_scaled")
        outT_done = sem("outT_done")
        outT_out = sem("outT_out")
        out_sums = sem("out_sums")
        out_ready = sem("out_ready")
        stored = sem("stored")

        OP = {"x": 0, "mem": 8, "b": 16, "a": 20, "out": 36, "oc": 44, "wo": 52, "h": 60,
              "down": 82, "ylru": 90, "yatt": 94, "out2": 98, "h2": 106}
        SQ = {"out": 0, "wo": 8, "down": 16, "ylru": 32, "yatt": 36, "out2": 40, "down2": 48}
        RT = {"out": 0, "wo": 1, "down": 2, "ylru": 4, "yatt": 5, "out2": 6, "down2": 7}
        TT = range(6)
        DSA = [(qb, h) for qb in range(QB) for h in range(A_HEADS)]
        CROSS = [(h, qb) for h in range(X_HEADS) for qb in range(QB)]
        STICK = [(p, qb, sub) for p in range(4) for qb in range(QB) for sub in range(2)]
        INDEX = [(qb, h) for qb in range(1, QB) for h in range(IDX_HEADS)]

        def w8_chunk(c):
            return w8[bass.ds(c, 1)].rearrange("a p n -> (a p) n")

        block = ctx.enter_context(nc.Block())

        @block.sync
        def _(sp):
            def load(m, s, src, cols):
                sp.wait_ge(weight_low, 2 * m + s - 1)
                sp.dma_start(weights_raw[:, s, 0:cols], src).then_inc(chunk_landed[s], 16)

            for tt in range(QB):
                sp.dma_start(x_tok[:, tt], x[tt * P:(tt + 1) * P, :]).then_inc(x_in[tt], 16)
            for s in range(2):
                sp.dma_start(weights_raw[:, s, 0:KB * P], w8[s]).then_inc(chunk_landed[s], 16)
            for tt in range(2):
                sp.dma_start(x_tok[:, QB + tt], mem[tt * P:(tt + 1) * P, :]).then_inc(x_in[QB + tt], 16)
            with sp.Fori(1, CHUNK["down"] // 2) as m:
                for s in range(2):
                    load(m, s, w8_chunk(2 * m + s), KB * P)
            with sp.Fori(0, 8) as m:
                for s in range(2):
                    load(m + CHUNK["down"] // 2, s,
                         w11[bass.ds(2 * m + s, 1)].rearrange("a p n -> (a p) n"), FH * P)
            with sp.Fori(CHUNK["in2"] // 2, CHUNK["down2"] // 2) as m:
                for s in range(2):
                    load(m, s, w8_chunk(2 * m + s - 16), KB * P)
            with sp.Fori(0, 8) as m:
                for s in range(2):
                    load(m + CHUNK["down2"] // 2, s,
                         w11[bass.ds(2 * m + s + 16, 1)].rearrange("a p n -> (a p) n"), FH * P)
            for tt in range(QB):
                sp.wait_ge(out_ready, tt + 1)
                sp.dma_start(out[tt * P:(tt + 1) * P, :], y_tok[:, tt]).then_inc(stored, 16)
            sp.wait_ge(stored, 16 * QB)

        @block.gpsimd
        def _(pool):
            made = [0]

            def then(ins):
                made[0] += 1
                ins.then_inc(consts_ready, 1)
                pool.wait_ge(consts_ready, made[0])

            g = nc.gpsimd
            for t in (ident, rotate, twice, causal):
                then(g.memset(t[:], 0.0))
            for t in (ones, before):
                then(g.memset(t[:], 1.0))
            then(g.memset(notbefore[:], 0.0))
            then(g.memset(eps, EPS))
            then(g.memset(half_pi, float(np.pi / 2)))
            then(g.affine_select(out=ident[:], in_=ident[:], compare_op=ALU.not_equal, fill=1.0, base=0,
                                 pattern=[[-1, P]], channel_multiplier=1))
            heads = rotate[:].rearrange("p (a b) -> p a b", b=HALF)
            then(g.affine_select(out=heads[:, :, 0:8], in_=heads[:, :, 0:8], compare_op=ALU.not_equal,
                                 fill=-1.0, base=-8, pattern=[[-HALF, 2], [-1, 8]], channel_multiplier=1))
            then(g.affine_select(out=heads[:, :, 8:16], in_=heads[:, :, 8:16], compare_op=ALU.not_equal,
                                 fill=1.0, base=0, pattern=[[-HALF, 2], [-1, 8]], channel_multiplier=1))
            copies = twice[:].rearrange("p (a b) -> p a b", b=HALF)
            then(g.affine_select(out=copies, in_=copies, compare_op=ALU.not_equal, fill=1.0, base=0,
                                 pattern=[[0, 2], [-1, HALF]], channel_multiplier=1))
            then(g.affine_select(out=causal[:], in_=causal[:], compare_op=ALU.is_ge, fill=NEG, base=0,
                                 pattern=[[-1, P]], channel_multiplier=1))
            then(g.affine_select(out=before[:], in_=before[:], compare_op=ALU.is_gt, fill=0.0, base=0,
                                 pattern=[[-1, P]], channel_multiplier=1))
            then(g.affine_select(out=notbefore[:], in_=notbefore[:], compare_op=ALU.is_gt, fill=1.0,
                                 base=0, pattern=[[-1, P]], channel_multiplier=1))

            def low(m, s, cols):
                pool.wait_ge(weight_high, 2 * m + s + 1)
                g.tensor_tensor(weights_low[:, s, 0:cols], weights_raw[:, s, 0:cols],
                                weights_high[:, s, 0:cols].bitcast(F32), ALU.subtract
                                ).then_inc(weight_low, 1)

            for first, end, cols in ((0, CHUNK["down"], KB * P), (CHUNK["down"], CHUNK["in2"], FH * P),
                                     (CHUNK["in2"], CHUNK["down2"], KB * P),
                                     (CHUNK["down2"], CHUNKS, FH * P)):
                with pool.Fori(first // 2, end // 2) as m:
                    for s in range(2):
                        low(m, s, cols)
        NCONST = 16

        @block.scalar
        def _(act):
            a = nc.scalar
            own = Steps(act, act_steps)

            act.dma_start(par[:], params).then_inc(params_in, 16)
            act.dma_start(sine[:].bitcast(I32), positions.partition_broadcast(P)).then_inc(positions_in, 16)

            def high(m, s, cols=KB * P):
                act.wait_ge(chunk_landed[s], 16 * (m + 1))
                act.wait_ge(chunk_done, 2 * m + s - 1)
                a.copy(weights_high[:, s, 0:cols], weights_raw[:, s, 0:cols]).then_inc(weight_high, 1)

            def high_next(m, s, cols=KB * P):
                high(m + 1, s, cols)

            def tile_done(m, s):
                act.wait_ge(chunk_done, 2 * m + s + 1)

            act.wait_ge(consts_ready, NCONST)

            def row_roots(tt):
                act.wait_ge(x_in[tt], 16)
                own.then(a.activation(xn_tok[:, tt], x_tok[:, tt], ACT.Square,
                                      accum_out=tok_sum[:, tt:tt + 1]))
                a.activation(tok_root[:, tt:tt + 1], tok_sum[:, tt:tt + 1], ACT.Sqrt, scale=1.0 / D,
                             bias=eps).then_inc(token_root, 1)

            for tt in range(QB):
                row_roots(tt)
            for s in range(2):
                act.wait_ge(chunk_landed[s], 16)
                a.copy(weights_high[:, s, 0:KB * P], weights_raw[:, s, 0:KB * P]).then_inc(weight_high, 1)
            act.wait_ge(params_in, 16)
            for k in range(KB):
                act.wait_ge(xnT_done, k + 1)
                a.activation(a_high[:, k], aux[k % 2][:], ACT.Copy, scale=col("g_mix", k)
                             ).then_inc(operand_high, 1)
            act.wait_ge(angle_ready, 2)
            own.step(a.activation(sine[:], sine[:], ACT.Sin))
            a.activation(cosine[:], cosine[:], ACT.Sin, bias=half_pi, scale=-1.0).then_inc(tables_ready, 1)
            act.wait_ge(angle_ready, 3)
            a.activation(sp[:, 0:4], sp[:, 0:4], ACT.Exp, scale=-1.0).then_inc(softplus_exp, 1)
            for tt in (4, 5):
                row_roots(tt)
            for n, dst in enumerate((kv[:], kiwi[:], qiT[:, 0], qiT[:, 1])):
                m, s = n // 2, n % 2
                high_next(m, s)
                tile_done(m, s)
                a.copy(dst, acc[:, s]).then_inc(tile_out[s], 1)
            for n, dst in enumerate((kT, kiT)):
                act.wait_ge(doubled, n + 1)
                a.copy(dst[:], aux[4 + n][:]).then_inc(doubled_out, 1)
            for k in range(KB):
                act.wait_ge(xT_done, k + 1)
                a.copy(residual[:, k], aux[k % 2][:]).then_inc(residual_in, 1)
            for k in range(KB):
                act.wait_ge(mT_done, k + 1)
                a.activation(m_high[:, k], aux[k % 2][:, 0:MB * P], ACT.Copy, scale=col("g_mem", k)
                             ).then_inc(operand_high, 1)
            act.wait_ge(vwi_done, 1)
            act.wait_ge(cleared, 1)
            v_tok = aux[4][:].rearrange("p (b f) -> p b f", f=P)[:, :, HALF:P]
            a.copy(v_pad[:, :, 0, 0:HALF], v_tok).then_inc(v_out, 1)
            a.copy(v_pad[:, :, 1, HALF:P], v_tok).then_inc(v_out, 1)
            act.wait_ge(vwi_done, 2)
            a.mul(wi[:], aux[5][:].rearrange("p (b f) -> p b f", f=P)[:, :, HALF:HALF + IDX_HEADS],
                  IDX_HEADS ** -0.5).then_inc(v_out, 1)
            for n, (qb, h) in enumerate(INDEX):
                act.wait_ge(index_logits, n + 1)
                if n >= 2:
                    act.wait_ge(rel_used, n - 1)
                bank = aux[2 + h % 2 + 2 * (n // 2 % 2)]
                a.activation(rel[:, n % 2, 0:(qb + 1) * P], bank[:, 0:(qb + 1) * P], ACT.Relu,
                             scale=HALF ** -0.5).then_inc(rel_ready, 1)
            for n in range(4):
                m, s = 2 + n // 2, n % 2
                high_next(m, s)
                tile_done(m, s)
                a.copy(qT[:, n], acc[:, s]).then_inc(tile_out[s], 1)
            for n in range(4):
                m = 4 + n
                high_next(m, 0)
                tile_done(m, 0)
                a.copy(glu[:, n, TAPS - 1:TAPS - 1 + T], acc[:, 0]).then_inc(tile_out[0], 1)
                high_next(m, 1)
                tile_done(m, 1)
                a.activation(gate[:, n], acc[:, 1], ACT.Sigmoid).then_inc(tile_out[1], 1)
            with act.Fori(CHUNK["kc"] // 2, CHUNK["vc"] // 2) as m:
                for s in range(2):
                    high_next(m, s)
                    tile_done(m, s)
                    a.copy(kcT[:, bass.ds(2 * m + s - CHUNK["kc"], 1)].rearrange("p a n -> p (a n)"),
                           acc[:, s, 0:MB * P]).then_inc(tile_out[s], 1)

            def vc_back(n):
                act.wait_ge(vcT_done, n + 1)
                a.copy(vc[:, :, n * P:(n + 1) * P],
                       aux[4 + n % 2][:, 0:MB * P].rearrange("p (b f) -> p b f", f=P)).then_inc(vc_out, 1)

            for n in range(KB):
                m, s = CHUNK["vc"] // 2 + n // 2, n % 2
                high_next(m, s)
                tile_done(m, s)
                if n >= 2:
                    act.wait_ge(vcT_done, n - 1)
                a.copy(vcT[:, s], acc[:, s, 0:MB * P]).then_inc(tile_out[s], 1)
                if n:
                    vc_back(n - 1)
            vc_back(KB - 1)
            for n in range(4):
                act.wait_ge(centred, n + 1)
                a.activation(gate[:, n], conv[:, n], ACT.Square).then_inc(centred_squared, 1)
            act.wait_ge(variance_ready, 1)
            a.activation(root[:], aux[1][:], ACT.Sqrt, scale=1.0 / (4 * P), bias=eps).then_inc(ln_root, 1)
            for n in range(4):
                act.wait_ge(ln_scaled, n + 1)
                own.then(a.activation(conv[:, n], conv[:, n], ACT.Silu, scale=col("ln_g", n),
                                      bias=col("ln_b", n)))
                a.copy(a_high[:, 4 + n], conv[:, n]).then_inc(operand_high, 1)
            for step in range(len(DSA) + 3):
                if step < len(DSA):
                    qb, h = DSA[step]
                    w = (qb + 1) * P
                    act.wait_ge(logits_masked, step + 1)
                    if step >= 2:
                        act.wait_ge(probT_done, step - 1)
                    a.activation(prob[:, step % 2, 0:w], masked[:, step % 2, 0:w], ACT.Exp, scale=-1.0,
                                 bias=least[:, step % 2:step % 2 + 1],
                                 accum_out=total[:, step % 2:step % 2 + 1]).then_inc(prob_raw, 1)
                j = step - 1
                if 0 <= j < len(DSA):
                    w = (DSA[j][0] + 1) * P
                    act.wait_ge(probT_done, j + 1)
                    if j >= 2:
                        act.wait_ge(heads_done, j - 1)
                    a.copy(probT[:, j % 2, 0:w], aux[2 + j % 2][:, 0:w]).then_inc(probT_ready, 1)
                j = step - 3
                if j >= 0 and j % 2:
                    qb, h = DSA[j]
                    act.wait_ge(heads_done, j + 1)
                    a.copy(a_high[:, h // 2, qb * P:(qb + 1) * P], aux[4 + j // 2 % 2][:, 0:P]
                           ).then_inc(operand_high, 1)

            def take_root(rt, bank, width):
                act.wait_ge(sums_ready, rt + 1)
                a.activation(root[:], bank[:], ACT.Sqrt, scale=1.0 / width, bias=eps
                             ).then_inc(root_ready, 1)

            def residual_tile(m, s, n, sq, op, gain, dst):
                act.wait_ge(tile_out[s], m + 1)
                if sq is not None:
                    act.wait_ge(summed, sq + n)
                    a.activation(square[:], residual[:, bass.ds(n, 1)], ACT.Square
                                 ).then_inc(squared, 1)
                a.activation(dst[:, bass.ds(n, 1)], residual[:, bass.ds(n, 1)], ACT.Copy,
                             scale=dcol(gain, n)).then_inc(operand_high, 1)

            def residual_gemm(name, sq, op, gain, dst):
                first = CHUNK[name] // 2
                tile = TILE[name] // 2
                with act.Fori(0, KB // 2) as i:
                    for s in range(2):
                        high_next(first + i, s)
                        residual_tile(tile + i, s, 2 * i + s, sq, op, gain, dst)

            residual_gemm("out", SQ["out"], OP["out"], "g_cross", b_high)
            for n in range(KB):
                m, s = CHUNK["qc"] // 2 + n // 2, n % 2
                high_next(m, s)
                if n == 0:
                    take_root(RT["out"], aux[0], D)
            for step in range(len(CROSS) + 3):
                if step < len(CROSS):
                    act.wait_ge(x_masked, step + 1)
                    if step >= 2:
                        act.wait_ge(x_probT_done, step - 1)
                    a.activation(xprob[:, step % 2], xmasked[:, step % 2], ACT.Exp, scale=-1.0,
                                 bias=least[:, step % 2:step % 2 + 1],
                                 accum_out=total[:, step % 2:step % 2 + 1]).then_inc(x_prob_raw, 1)
                j = step - 1
                if 0 <= j < len(CROSS):
                    h, qb = CROSS[j]
                    act.wait_ge(x_probT_done, j + 1)
                    if h >= 2:
                        act.wait_ge(x_heads_done, 2 * (h - 1))
                    a.copy(xprobT[:, h % 2, :, qb * P:(qb + 1) * P],
                           aux[2 + j % 2][:, 0:MB * P].rearrange("p (b f) -> p b f", f=P)
                           ).then_inc(x_probT_ready, 1)
                j = step - 3
                if j >= 0 and j % QB == QB - 1:
                    h = CROSS[j][0]
                    for d in range(2):
                        act.wait_ge(x_heads_done, 2 * h + d + 1)
                        a.copy(b_high[:, 2 * h + d], aux[4 + d][:]).then_inc(operand_high, 1)
            residual_gemm("oc", SQ["wo"], OP["wo"], "g_ffn", a_high)

            def ffn(name, dst, last_cols, rt, base_):
                def pair(m, n, first=False, cols=KB * P):
                    high_next(m, 0, cols)
                    if first:
                        take_root(rt, aux[0], D)
                    if name == "ffn":
                        act.wait_ge(gate_ready, n + 1)
                    else:
                        act.wait_ge(tile_out[0], TILE[name] // 2 + n + 1)
                    a.activation(work[:, 0], work[:, 0], ACT.Silu).then_inc(silu_ready, 1)
                    high_next(m, 1, cols)
                    act.wait_ge(hidden_ready, base_ + n + 1)
                    a.copy(dst[:, bass.ds(n, 1)], work[:, bass.ds(1, 1)]).then_inc(operand_high, 1)

                base = CHUNK[name] // 2
                pair(base, 0, first=True)
                with act.Fori(1, FB - 1) as i:
                    pair(base + i, i)
                pair(base + FB - 1, FB - 1, cols=last_cols)

            ffn("ffn", h_high, FH * P, RT["wo"], 0)
            def down_tile(m, t, s, n, next_cols):
                high(m + 1, 0, next_cols)
                high(m + 1, 1, next_cols)
                act.wait_ge(tile_out[s], t + 1)
                act.wait_ge(summed, SQ["down"] + 2 * n)
                a.activation(square[:], residual[:, bass.ds(n, 1)], ACT.Square).then_inc(squared, 1)
                a.activation(work[:, bass.ds(0, 1)], residual[:, bass.ds(n, 1)], ACT.Square,
                             scale=dcol("g_final", n)).then_inc(squared, 1)
                a.activation(a_high[:, bass.ds(n, 1)], residual[:, bass.ds(n, 1)], ACT.Copy,
                             scale=both_gains[:, bass.ds(n, 1)]).then_inc(operand_high, 1)

            with act.Fori(0, 3) as i:
                for s in range(2):
                    down_tile(CHUNK["down"] // 2 + 2 * i + s, TILE["down"] // 2 + i, s, 2 * i + s, FH * P)
            for s in range(2):
                down_tile(CHUNK["down"] // 2 + 6 + s, TILE["down"] // 2 + 3, s, 6 + s,
                          FH * P if s == 0 else KB * P)

            c0, t0 = CHUNK["in2"] // 2, TILE["in2"] // 2
            act.dma_start(lru_weights[:], blockdiag).then_inc(blockdiag_in, 16)
            high_next(c0, 0)
            take_root(RT["down"], aux[0], D)
            act.wait_ge(rescaled, 1)
            a.activation(root[:], square[:], ACT.Sqrt, scale=1.0 / D, bias=eps).then_inc(root_ready, 1)
            high_next(c0, 1)
            with act.Fori(1, 4) as i:
                for s in range(2):
                    high_next(c0 + i, s)
            for n in range(4):
                act.wait_ge(tile_out[n % 2], t0 + 2 + n // 2 + 1)
                a.activation(lru_gate[:, n], lru_gate[:, n], ACT.Gelu_apprx_tanh).then_inc(gelu_ready, 1)
            for j in range(4):
                chunks = [8 + 3 * j + r for r in range(3)]
                high_next(c0 + chunks[0] // 2, chunks[0] % 2)
                for r, name in enumerate(("b_rg", "b_ig")):
                    act.wait_ge(lgates_done, 2 * j + r + 1)
                    ins = a.activation(gates[:, r], aux[1 + r][:], ACT.Sigmoid, bias=col(name, j))
                    ins.then_inc(lgates_ready, 1)
                act.wait_ge(lgates_ready, 2 * j + 1)
                a.activation(half_tanh[:], gates[:, 0], ACT.Tanh, scale=decay[:, j:j + 1]
                             ).then_inc(tanh_ready, 1)
                high_next(c0 + chunks[1] // 2, chunks[1] % 2)
                act.wait_ge(tanh_ready, j + 1)
                a.activation(gate_root[:], half_tanh[:], ACT.Sqrt).then_inc(lroot_ready, 1)
                act.wait_ge(vT2_done, j + 1)
                act.wait_ge(v2_clear, 1)
                blocks = aux[3][:].rearrange("p (b f) -> p b f", f=P)
                for sub in range(2):
                    a.copy(v2[:, :, 2 * j + sub, sub * HALF:(sub + 1) * HALF],
                           blocks[:, :, sub * HALF:(sub + 1) * HALF]).then_inc(v2_out, 1)
                high_next(c0 + chunks[2] // 2, chunks[2] % 2)

            def y_norm(src, sq, rt, done, done_base, op, block0, bank):
                for n in range(4):
                    act.wait_ge(done, done_base + n + 1)
                    act.wait_ge(summed, sq + n)
                    a.activation(square[:], src[:, n], ACT.Square).then_inc(squared, 1)
                take_root(rt, bank, 4 * P)
                for n in range(4):
                    act.wait_ge(y_scaled, block0 + n + 1)
                    a.copy(y_high[:, block0 + n], src[:, n]).then_inc(operand_high, 1)

            y_norm(lru_gate, SQ["ylru"], RT["ylru"], lru_done, 0, OP["ylru"], 0, aux[0])
            for step in range(len(STICK) + 1):
                if step < len(STICK):
                    p, qb, sub = STICK[step]
                    w = (qb + 1) * P
                    act.wait_ge(sticks, step + 1)
                    if step >= 2:
                        act.wait_ge(takenT, step - 1)
                    a.activation(take[:, step % 2, 0:w], aux[sub][:, 0:w], ACT.Sigmoid,
                                 scale=HALF ** -0.5).then_inc(breaks, 1)
                    a.activation(stay[:, step % 2, 0:w], aux[sub][:, 0:w], ACT.Sigmoid,
                                 scale=-HALF ** -0.5).then_inc(breaks, 1)
                j = step - 1
                if j >= 0:
                    w = (STICK[j][1] + 1) * P
                    act.wait_ge(takenT, j + 1)
                    if j >= 2:
                        act.wait_ge(stick_heads, j - 1)
                    a.copy(takeT[:, j % 2, 0:w], aux[2 + j % 2][:, 0:w]).then_inc(takenT_ready, 1)
            y_norm(q2, SQ["yatt"], RT["yatt"], att_out, 0, OP["yatt"], 4, aux[0])
            residual_gemm("out2", SQ["out2"], OP["out2"], "g_ffn2", a_high)
            ffn("ffn2", h_high, FH * P, RT["out2"], FB)

            def last_tile(m, t, s, n, more=True):
                if more:
                    high(m + 1, 0, FH * P)
                    high(m + 1, 1, FH * P)
                act.wait_ge(tile_out[s], t + 1)
                act.wait_ge(summed, SQ["down2"] + n)
                a.activation(square[:], residual[:, bass.ds(n, 1)], ACT.Square).then_inc(squared, 1)
                if n >= 2:
                    act.wait_ge(outT_done, n - 1)
                a.activation(work[:, s], residual[:, bass.ds(n, 1)], ACT.Copy,
                             scale=dcol("g_final2", n)).then_inc(out_scaled, 1)
                act.wait_ge(outT_done, n + 1)
                a.copy(y_tok[:, :, bass.ds(n * P, P)], aux[2 + s][:].rearrange("p (b f) -> p b f", f=P)
                       ).then_inc(outT_out, 1)

            for n in range(KB):
                last_tile(CHUNK["down2"] // 2 + n, TILE["down2"] // 2 + n // 2, n % 2, n, n < KB - 1)
            act.wait_ge(out_sums, 1)
            a.activation(tok_root[:, 0:QB], aux[0][:, 0:QB], ACT.Sqrt, scale=1.0 / D, bias=eps
                         ).then_inc(root_ready, 1)

        @block.vector
        def _(dve):
            v = nc.vector
            own = Steps(dve, dve_steps)

            dve.wait_ge(params_in, 16)
            dve.wait_ge(positions_in, 16)
            own.then(v.tensor_copy(cosine[:], sine[:].bitcast(I32)))
            own.then(v.tensor_scalar(sine[:], cosine[:], col("freq"), None, ALU.mult))
            own.then(v.tensor_scalar(cosine[:], sine[:], float(1 / (2 * np.pi)), ROUND, ALU.mult, ALU.add))
            own.then(v.tensor_scalar(cosine[:], cosine[:], -ROUND, None, ALU.add))
            for piece in TWO_PI:
                own.then(v.scalar_tensor_tensor(sine[:], cosine[:], -piece, sine[:], ALU.mult, ALU.add))
            v.tensor_scalar(sine[:], sine[:], 3.1415925, -3.1415925, ALU.min, ALU.max
                            ).then_inc(angle_ready, 1)
            dve.wait_ge(angle_ready, 1)
            v.scalar_tensor_tensor(cosine[:], sine[:], -1.0, sine[:], ALU.mult, ALU.max).then_inc(angle_ready, 1)
            v.scalar_tensor_tensor(sp[:, 0:4], col("lam", 0, 4), -1.0, col("lam", 0, 4), ALU.mult, ALU.max
                                   ).then_inc(angle_ready, 1)
            own.step(v.tensor_tensor(both_gains, col("g_final", 0, KB), col("g_mix2", 0, KB), ALU.mult))
            v.memset(v_pad[:], 0.0).then_inc(cleared, 1)

            def scale_rows(tt):
                dve.wait_ge(token_root, tt + 1)
                own.then(v.reciprocal(tok_factor[:, tt:tt + 1], tok_root[:, tt:tt + 1]))
                v.tensor_scalar(xn_tok[:, tt], x_tok[:, tt], tok_factor[:, tt:tt + 1], None, ALU.mult
                                ).then_inc(token_scaled, 1)

            for tt in range(QB):
                scale_rows(tt)
            for k in range(KB):
                dve.wait_ge(operand_high, OP["x"] + k + 1)
                v.scalar_tensor_tensor(a_low[:, k], aux[k % 2][:], col("g_mix", k),
                                       a_high[:, k].bitcast(F32), ALU.mult, ALU.subtract
                                       ).then_inc(operand_low, 1)
            dve.wait_ge(softplus_exp, 1)
            e, s1_, s2_, po = sp[:, 0:4], sp[:, 4:8], sp[:, 8:12], sp[:, 12:16]
            own.then(v.tensor_scalar(s1_, e, 2.0, None, ALU.add))
            own.then(v.reciprocal(s1_, s1_))
            own.then(v.tensor_tensor(s1_, s1_, e, ALU.mult))
            own.then(v.tensor_tensor(s2_, s1_, s1_, ALU.mult))
            own.then(v.tensor_scalar(po, s2_, 1.0 / 15, 1.0 / 13, ALU.mult, ALU.add))
            for n in (11, 9, 7, 5, 3, 1):
                own.then(v.tensor_tensor(po, po, s2_, ALU.mult))
                own.then(v.tensor_scalar(po, po, 1.0 / n, None, ALU.add))
            own.then(v.tensor_tensor(po, po, s1_, ALU.mult))
            own.then(v.tensor_scalar(s2_, col("lam", 0, 4), -4.0, 0.0, ALU.mult, ALU.max))
            own.then(v.scalar_tensor_tensor(decay, po, 8.0, s2_, ALU.mult, ALU.add))
            for tt in (4, 5):
                scale_rows(tt)
            dve.wait_ge(tables_ready, 1)

            def rope(n, t, rows, bank):
                dve.wait_ge(rotated, n + 1)
                own.step(v.tensor_tensor(t, t, cosine[0:rows], ALU.mult))
                own.then(v.tensor_tensor(root[0:rows], bank[0:rows], sine[0:rows], ALU.mult))
                v.tensor_tensor(t, t, root[0:rows], ALU.add).then_inc(roped, 1)
                dve.wait_ge(roped, n + 1)

            rope(0, kv[0:HALF], HALF, aux[2])
            rope(1, kiwi[0:HALF], HALF, aux[3])
            rope(2, qiT[:, 0], P, aux[2])
            rope(3, qiT[:, 1], P, aux[3])
            for k in range(KB):
                dve.wait_ge(operand_high, OP["mem"] + k + 1)
                v.scalar_tensor_tensor(m_low[:, k], aux[k % 2][:, 0:MB * P], col("g_mem", k),
                                       m_high[:, k].bitcast(F32), ALU.mult, ALU.subtract
                                       ).then_inc(operand_low, 1)
            dve.wait_ge(v_out, 3)
            for n, (qb, h) in enumerate(INDEX):
                dve.wait_ge(rel_ready, n + 1)
                w = (qb + 1) * P
                dst, src, weight = score[:, qb - 1, 0:w], rel[:, n % 2, 0:w], wi[:, qb, h:h + 1]
                if h == 0:
                    v.tensor_scalar(dst, src, weight, None, ALU.mult).then_inc(rel_used, 1)
                else:
                    v.scalar_tensor_tensor(dst, src, weight, dst, ALU.mult, ALU.add
                                           ).then_inc(rel_used, 1)
                dve.wait_ge(rel_used, n + 1)
            for qb in range(1, QB):
                w = (qb + 1) * P
                row = score[:, qb - 1, 0:w]
                diag = score[:, qb - 1, qb * P:w]
                own.then(v.tensor_tensor(diag, diag, causal[:], ALU.add))
                for _ in range(TOPK // 8):
                    own.then(v.max(best, row))
                    own.then(v.match_replace(out=row, in_to_replace=best, in_values=row,
                                             imm_value=CHOSEN))
                own.then(v.tensor_scalar(row, row, CHOSEN, NEG, ALU.not_equal, ALU.mult))
            for n in range(4):
                rope(4 + n, qT[:, n], P, aux[n])
            own.then(v.memset(glu[:, :, 0:TAPS - 1], 0.0))
            for n in range(4):
                dve.wait_ge(tile_out[1], TILE["in"] // 2 + 4 + n + 1)
                dve.wait_ge(tile_out[0], TILE["in"] // 2 + 4 + n + 1)
                body = glu[:, n, TAPS - 1:TAPS - 1 + T]
                own.step(v.tensor_tensor(body, body, gate[:, n], ALU.mult))
            own.settle()
            for pair in range(2):
                for k in range(TAPS):
                    for n in (2 * pair, 2 * pair + 1):
                        src, weight = glu[:, n, k:k + T], col("conv_w", n * TAPS + k)
                        if k == 0:
                            own.step(v.tensor_scalar(conv[:, n], src, weight, col("conv_b", n),
                                                     ALU.mult, ALU.add))
                            continue
                        own.settle(0 if k == TAPS - 1 and n % 2 else 1)
                        ins = v.scalar_tensor_tensor(conv[:, n], src, weight, conv[:, n], ALU.mult, ALU.add)
                        if k < TAPS - 1:
                            own.step(ins)
                        else:
                            ins.then_inc(conv_ready, 1)
            dve.wait_ge(mean_ready, 1)
            for n in range(4):
                v.scalar_tensor_tensor(conv[:, n], aux[0][:], -1.0 / (4 * P), conv[:, n], ALU.mult, ALU.add
                                       ).then_inc(centred, 1)
            dve.wait_ge(ln_root, 1)
            own.then(v.reciprocal(root[:], root[:]))
            dve.wait_ge(centred, 4)
            for n in range(4):
                v.tensor_tensor(conv[:, n], conv[:, n], root[:], ALU.mult).then_inc(ln_scaled, 1)
            for n in range(4):
                dve.wait_ge(operand_high, OP["b"] + n + 1)
                v.tensor_tensor(a_low[:, 4 + n], conv[:, n], a_high[:, 4 + n].bitcast(F32), ALU.subtract
                                ).then_inc(operand_low, 1)
            for step in range(len(DSA) + 3):
                if step < len(DSA):
                    qb, h = DSA[step]
                    w = (qb + 1) * P
                    dve.wait_ge(logits, step + 1)
                    if step >= 2:
                        dve.wait_ge(prob_raw, step - 1)
                    mask = causal[:] if qb == 0 else score[:, qb - 1, 0:w]
                    v.tensor_tensor_reduce(out=masked[:, step % 2, 0:w], in0=aux[h % 2][:, 0:w], in1=mask,
                                           scale=-HALF ** -0.5, scalar=3e38, op0=ALU.add, op1=ALU.min,
                                           accum_out=least[:, step % 2:step % 2 + 1]
                                           ).then_inc(logits_masked, 1)
                j = step - 1
                if 0 <= j < len(DSA):
                    w = (DSA[j][0] + 1) * P
                    dve.wait_ge(prob_raw, j + 1)
                    own.then(v.reciprocal(inverse[:, j % 2:j % 2 + 1], total[:, j % 2:j % 2 + 1]))
                    v.tensor_scalar(prob[:, j % 2, 0:w], prob[:, j % 2, 0:w], inverse[:, j % 2:j % 2 + 1],
                                    None, ALU.mult).then_inc(prob_ready, 1)
                j = step - 3
                if j >= 0 and j % 2:
                    qb, h = DSA[j]
                    dve.wait_ge(operand_high, OP["a"] + j // 2 + 1)
                    span = slice(qb * P, (qb + 1) * P)
                    v.tensor_tensor(a_low[:, h // 2, span], aux[4 + j // 2 % 2][:, 0:P],
                                    a_high[:, h // 2, span].bitcast(F32), ALU.subtract
                                    ).then_inc(operand_low, 1)

            def new_factor(rt):
                dve.wait_ge(root_ready, rt + 1)
                own.then(v.reciprocal(row_factor[:], root[:]))

            def residual_tile(c, t, s, n):
                dve.wait_ge(chunk_done, c)
                v.tensor_tensor(residual[:, bass.ds(n, 1)].rearrange("p a n -> p (a n)"), acc[:, s],
                                residual[:, bass.ds(n, 1)].rearrange("p a n -> p (a n)"), ALU.add
                                ).then_inc(tile_out[s], 1)
                dve.wait_ge(tile_out[s], t + 1)

            def at(x, n):
                return x[:, bass.ds(n, 1)].rearrange("p a n -> p (a n)")

            def add_squares(count, total_, squares):
                dve.wait_ge(squared, count)
                v.tensor_tensor(total_, total_, squares, ALU.add).then_inc(summed, 1)

            def low_part(dst, src_high, n, gain, count):
                dve.wait_ge(operand_high, count)
                v.scalar_tensor_tensor(at(dst, n), at(residual, n), gain, at(src_high, n).bitcast(F32),
                                       ALU.mult, ALU.subtract).then_inc(operand_low, 1)

            def residual_gemm(name, sq, op, gain, dst_high, dst_low):
                own.then(v.memset(square_sum[:], 0.0))

                def body(i):
                    for s in range(2):
                        n = 2 * i + s
                        residual_tile(CHUNK[name] + n + 1, TILE[name] // 2 + i, s, n)
                        add_squares(sq + n + 1, square_sum[:], square[:])
                        low_part(dst_low, dst_high, n, dcol(gain, n), op + n + 1)
                        dve.wait_ge(summed, sq + n + 1)
                own.run(0, KB // 2, 0, body)

            residual_gemm("out", SQ["out"], OP["out"], "g_cross", b_high, b_low)
            own.then(v.memset(zeros[:], 0.0))
            new_factor(RT["out"])

            def queries(i):
                for s in range(2):
                    dve.wait_ge(chunk_done, CHUNK["qc"] + 2 * i + s + 1)
                    v.tensor_tensor(at(qcT, 2 * i + s), acc[:, s], row_factor[:], ALU.mult
                                    ).then_inc(tile_out[s], 1)
            own.run(0, KB // 2, 0, queries)
            for step in range(len(CROSS) + 3):
                if step < len(CROSS):
                    dve.wait_ge(x_logits, step + 1)
                    if step >= 2:
                        dve.wait_ge(x_prob_raw, step - 1)
                    v.tensor_tensor_reduce(out=xmasked[:, step % 2], in0=aux[step % 2][:, 0:MB * P],
                                           in1=zeros[:], scale=-(X_KB * P) ** -0.5, scalar=3e38,
                                           op0=ALU.add, op1=ALU.min,
                                           accum_out=least[:, step % 2:step % 2 + 1]).then_inc(x_masked, 1)
                j = step - 1
                if 0 <= j < len(CROSS):
                    dve.wait_ge(x_prob_raw, j + 1)
                    own.then(v.reciprocal(inverse[:, j % 2:j % 2 + 1], total[:, j % 2:j % 2 + 1]))
                    v.tensor_scalar(xprob[:, j % 2], xprob[:, j % 2], inverse[:, j % 2:j % 2 + 1], None,
                                    ALU.mult).then_inc(x_prob_ready, 1)
                j = step - 3
                if j >= 0 and j % QB == QB - 1:
                    for d in range(2):
                        n = 2 * CROSS[j][0] + d
                        dve.wait_ge(operand_high, OP["oc"] + n + 1)
                        v.tensor_tensor(b_low[:, n], aux[4 + d][:], b_high[:, n].bitcast(F32),
                                        ALU.subtract).then_inc(operand_low, 1)
            residual_gemm("oc", SQ["wo"], OP["wo"], "g_ffn", a_high, a_low)

            def ffn(name, dst_high, dst_low, op, base, taps):
                def pair(i):
                    t = TILE[name] // 2 + i
                    dve.wait_ge(chunk_done, CHUNK[name] + 2 * i + 1)
                    dst = gated[:, TAPS_FFN - 1:TAPS_FFN - 1 + T] if taps else work[:, 0]
                    ins = v.tensor_tensor(dst, acc[:, 0], row_factor[:], ALU.mult)
                    ins.then_inc(tile_out[0], 1)
                    if taps:
                        dve.wait_ge(tile_out[0], t + 1)
                        c = i * TAPS_FFN
                        own.then(v.tensor_scalar(work[:, 0], gated[:, 2:2 + T], dcol("fconv_w", c + 2),
                                                 dcol("fconv_b", i), ALU.mult, ALU.add))
                        own.then(v.scalar_tensor_tensor(work[:, 0], gated[:, 1:1 + T], dcol("fconv_w", c + 1),
                                                        work[:, 0], ALU.mult, ALU.add))
                        v.scalar_tensor_tensor(work[:, 0], gated[:, 0:T], dcol("fconv_w", c), work[:, 0],
                                               ALU.mult, ALU.add).then_inc(gate_ready, 1)
                    dve.wait_ge(chunk_done, CHUNK[name] + 2 * i + 2)
                    v.tensor_tensor(work[:, 1], acc[:, 1], row_factor[:], ALU.mult).then_inc(tile_out[1], 1)
                    dve.wait_ge(tile_out[1], t + 1)
                    dve.wait_ge(silu_ready, base + i + 1)
                    v.tensor_tensor(work[:, 1], work[:, 1], work[:, 0], ALU.mult).then_inc(hidden_ready, 1)
                    dve.wait_ge(hidden_ready, base + i + 1)
                    dve.wait_ge(operand_high, op + i + 1)
                    v.tensor_tensor(at(dst_low, i), work[:, 1], at(dst_high, i).bitcast(F32), ALU.subtract
                                    ).then_inc(operand_low, 1)
                    dve.wait_ge(operand_low, op + i + 1)
                own.run(0, FB, 2 if taps else 0, pair)

            own.then(v.memset(gated[:, 0:TAPS_FFN - 1], 0.0))
            new_factor(RT["wo"])
            ffn("ffn", h_high, h_low, OP["h"], 0, True)

            own.step(v.memset(square_sum[:], 0.0))
            own.then(v.memset(work[:, 1], 0.0))

            def down(i):
                for s in range(2):
                    n = 2 * i + s
                    residual_tile(CHUNK["down"] + 2 * n + 2, TILE["down"] // 2 + i, s, n)
                    add_squares(SQ["down"] + 2 * n + 1, square_sum[:], square[:])
                    add_squares(SQ["down"] + 2 * n + 2, work[:, 1], work[:, 0])
                    low_part(a_low, a_high, n, both_gains[:, bass.ds(n, 1)], OP["down"] + n + 1)
                    dve.wait_ge(summed, SQ["down"] + 2 * n + 2)
            own.run(0, KB // 2, 0, down)

            new_factor(RT["down"])
            dve.wait_ge(sums_ready, RT["down"] + 2)
            own.then(v.tensor_tensor(square[:], aux[1][:], row_factor[:], ALU.mult))
            v.tensor_tensor(square[:], square[:], row_factor[:], ALU.mult).then_inc(rescaled, 1)
            own.then(v.tensor_copy(square_sum[:], row_factor[:]))
            dve.wait_ge(root_ready, RT["down"] + 2)
            own.then(v.reciprocal(row_factor[:], root[:]))
            own.then(v.tensor_tensor(row_factor[:], row_factor[:], square_sum[:], ALU.mult))

            own.step(v.memset(lru_in[:, :, 0:TAPS_LRU - 1], 0.0))

            def out_of(n, dst):
                dve.wait_ge(chunk_done, CHUNK["in2"] + n + 1)
                v.tensor_tensor(dst, acc[:, n % 2], row_factor[:], ALU.mult).then_inc(tile_out[n % 2], 1)
                dve.wait_ge(tile_out[n % 2], TILE["in2"] // 2 + n // 2 + 1)

            for n in range(4):
                out_of(n, lru_in[:, n, TAPS_LRU - 1:TAPS_LRU - 1 + T])
                for k in (2 * n, 2 * n + 1):
                    own.step(v.scalar_tensor_tensor(residual[:, k], residual[:, k], col("g_final", k),
                                                    square_sum[:], ALU.mult, ALU.mult))
            for n in range(4):
                out_of(4 + n, lru_gate[:, n])
            v.memset(v2[:], 0.0).then_inc(v2_clear, 1)
            own.then(v.memset(square_sum[:], 0.0))
            dve.wait_ge(blockdiag_in, 16)
            for j in range(4):
                if j:
                    dve.wait_ge(lgates_done, 2 * j)
                for k in range(TAPS_LRU - 1, -1, -1):
                    src, weight = lru_in[:, j, k:k + T], col("lconv_w", j * TAPS_LRU + k)
                    if k == TAPS_LRU - 1:
                        own.then(v.tensor_scalar(xc[:], src, weight, col("lconv_b", j), ALU.mult, ALU.add))
                    elif k:
                        own.then(v.scalar_tensor_tensor(xc[:], src, weight, xc[:], ALU.mult, ALU.add))
                    else:
                        v.scalar_tensor_tensor(xc[:], src, weight, xc[:], ALU.mult, ALU.add
                                               ).then_inc(lconv_ready, 1)
                out_of(8 + 3 * j, vT2[:, j % 2])
                dve.wait_ge(tanh_ready, j + 1)
                own.then(v.tensor_scalar(inverse_sum[:], half_tanh[:], 1.0, None, ALU.add))
                own.then(v.reciprocal(inverse_sum[:], inverse_sum[:]))
                dve.wait_ge(lgates_ready, 2 * j + 2)
                own.then(v.tensor_tensor(gates[:, 1], gates[:, 1], xc[:], ALU.mult))
                out_of(9 + 3 * j, q2[:, j])
                dve.wait_ge(lroot_ready, j + 1)
                own.then(v.scalar_tensor_tensor(gate_root[:], gate_root[:], 2.0, inverse_sum[:], ALU.mult,
                                                ALU.mult))
                own.step(v.tensor_tensor(gate_root[:], gate_root[:], gates[:, 1], ALU.mult))
                own.then(v.tensor_scalar(inverse_sum[:], inverse_sum[:], 2.0, -1.0, ALU.mult, ALU.add))
                own.then(v.tensor_tensor_scan(half_tanh[:], inverse_sum[:], gate_root[:], 0.0, ALU.mult,
                                              ALU.add))
                dve.wait_ge(gelu_ready, j + 1)
                v.tensor_tensor(lru_gate[:, j], lru_gate[:, j], half_tanh[:], ALU.mult
                                ).then_inc(lru_done, 1)
                out_of(10 + 3 * j, k2[:, j])

            def y_norm(src, sq, rt, base, gain, op, block0):
                for n in range(4):
                    add_squares(sq + n + 1, square_sum[:], square[:])
                    dve.wait_ge(summed, sq + n + 1)
                dve.wait_ge(root_ready, rt + 1)
                own.then(v.reciprocal(root[:], root[:]))
                for n in range(4):
                    v.scalar_tensor_tensor(src[:, n], src[:, n], col(gain, n), root[:], ALU.mult, ALU.mult
                                           ).then_inc(y_scaled, 1)
                for n in range(4):
                    dve.wait_ge(operand_high, op + n + 1)
                    v.tensor_tensor(y_low[:, block0 + n], src[:, n], y_high[:, block0 + n].bitcast(F32),
                                    ALU.subtract).then_inc(operand_low, 1)

            dve.wait_ge(lru_done, 4)
            y_norm(lru_gate, SQ["ylru"], RT["ylru"], 0, "g_lru", OP["ylru"], 0)
            own.step(v.memset(square_sum[:], 0.0))
            own.then(v.memset(no_add[:], 0.0))
            for step, (p, qb, sub) in enumerate(STICK):
                w = (qb + 1) * P
                i = step % 2
                dve.wait_ge(breaks, 2 * step + 2)
                own.step(v.tensor_tensor(stay[:, i, w - P:w], stay[:, i, w - P:w], notbefore[:], ALU.max))
                own.then(v.tensor_tensor(take[:, i, w - P:w], take[:, i, w - P:w], before[:], ALU.mult))
                own.then(v.tensor_tensor_scan(left[:, w - 1::-1] if w == T else left[:, 0:w][:, ::-1],
                                              stay[:, i, 0:w][:, ::-1], no_add[:, 0:w], 1.0, ALU.mult,
                                              ALU.add))
                v.tensor_tensor(take[:, i, 0:w - 1], take[:, i, 0:w - 1], left[:, 1:w], ALU.mult
                                ).then_inc(taken, 1)
                dve.wait_ge(taken, step + 1)
                if step % 8 == 1 and p:
                    dve.wait_ge(stick_heads, 8 * p)
                    v.tensor_copy(q2[:, p - 1], aux[4 + (p - 1) % 2][:]).then_inc(att_out, 1)
            dve.wait_ge(stick_heads, len(STICK))
            v.tensor_copy(q2[:, 3], aux[5][:]).then_inc(att_out, 1)
            dve.wait_ge(att_out, 4)
            y_norm(q2, SQ["yatt"], RT["yatt"], 4, "g_att", OP["yatt"], 4)
            residual_gemm("out2", SQ["out2"], OP["out2"], "g_ffn2", a_high, a_low)
            new_factor(RT["out2"])
            ffn("ffn2", h_high, h_low, OP["h2"], FB, False)

            own.then(v.memset(square_sum[:], 0.0))
            for n in range(KB):
                residual_tile(CHUNK["down2"] + 2 * n + 2, TILE["down2"] // 2 + n // 2, n % 2, n)
                add_squares(SQ["down2"] + n + 1, square_sum[:], square[:])
                dve.wait_ge(summed, SQ["down2"] + n + 1)
            dve.wait_ge(root_ready, RT["down2"] + 1)
            own.then(v.reciprocal(tok_factor[:, 0:QB], tok_root[:, 0:QB]))
            dve.wait_ge(outT_out, KB)
            for tt in range(QB):
                v.tensor_scalar(y_tok[:, tt], y_tok[:, tt], tok_factor[:, tt:tt + 1], None, ALU.mult
                                ).then_inc(out_ready, 1)

        @block.tensor
        def _(pe):
            t_ = nc.tensor
            A = (a_high, a_low)
            B = (b_high, b_low)
            M = (m_high, m_low)
            Y = (y_high, y_low)
            H = (h_high, h_low)

            def chunk(m, s, blocks, bank, operand, k0=0, start=True, stop=True, ready=None, cols=T):
                pe.wait_ge(weight_low, 2 * m + s + 1)
                high, low = operand
                for k in range(blocks):
                    if ready is not None:
                        pe.wait_ge(operand_low, ready + k + 1)
                    wide = slice(k * P, (k + 1) * P)
                    passes = ((weights_high, high), (weights_high, low), (weights_low, high))
                    for n, (w, x_) in enumerate(passes):
                        last = t_.matmul(acc[:, bank, 0:cols], w[:, s, wide], x_[:, k0 + k, 0:cols],
                                         start=start and k == 0 and n == 0,
                                         stop=stop and k == blocks - 1 and n == 2)
                last.then_inc(chunk_done, 1)

            def free(bank, t):
                pe.wait_ge(tile_out[bank], t)

            def gemm_pair(name, i, operand, ready=None, cols=T, between=None):
                m, t = CHUNK[name] // 2 + i, TILE[name] // 2 + i
                free(0, t)
                chunk(m, 0, KB, 0, operand, ready=ready, cols=cols)
                if between:
                    between()
                free(1, t)
                chunk(m, 1, KB, 1, operand, cols=cols)

            def gemm(name, pairs, operand, ready, between=None, cols=T):
                gemm_pair(name, 0, operand, ready=ready, between=between, cols=cols)
                with pe.Fori(1, pairs) as i:
                    gemm_pair(name, i, operand, cols=cols)

            def sum_features(count, src, bank):
                pe.wait_ge(summed, count)
                t_.matmul(bank[:], ones[:], src, start=True, stop=True).then_inc(sums_ready, 1)

            pe.wait_ge(consts_ready, NCONST)
            pe.wait_ge(token_scaled, QB)
            for k in range(KB):
                if k >= 2:
                    pe.wait_ge(operand_low, k - 1)
                for tt in range(QB):
                    last = t_.transpose(aux[k % 2][:, tt * P:(tt + 1) * P],
                                        xn_tok[:, tt, k * P:(k + 1) * P], ident[:])
                last.then_inc(xnT_done, 1)

            def in_tile(n):
                m, s = n // 2, n % 2
                if m:
                    free(s, m)
                chunk(m, s, KB, s, A, ready=0 if n == 0 else None)

            def rotation(src, rows, bank):
                t_.matmul(bank[0:rows], rotate[0:rows, 0:rows], src, start=True, stop=True
                          ).then_inc(rotated, 1)

            in_tile(0)
            in_tile(1)
            pe.wait_ge(tile_out[0], 1)
            rotation(kv[0:HALF], HALF, aux[2])
            in_tile(2)
            pe.wait_ge(tile_out[1], 1)
            rotation(kiwi[0:HALF], HALF, aux[3])
            pe.wait_ge(roped, 1)
            t_.matmul(aux[4][:], twice[0:HALF], kv[0:HALF], start=True, stop=True).then_inc(doubled, 1)
            in_tile(3)
            pe.wait_ge(tile_out[0], 2)
            rotation(qiT[:, 0], P, aux[2])
            pe.wait_ge(roped, 2)
            t_.matmul(aux[5][:], twice[0:HALF], kiwi[0:HALF], start=True, stop=True).then_inc(doubled, 1)
            pe.wait_ge(tile_out[1], 2)
            rotation(qiT[:, 1], P, aux[3])
            for k in range(KB):
                pe.wait_ge(operand_low, KB) if k < 2 else pe.wait_ge(residual_in, k - 1)
                for tt in range(QB):
                    last = t_.transpose(aux[k % 2][:, tt * P:(tt + 1) * P],
                                        x_tok[:, tt, k * P:(k + 1) * P], ident[:])
                last.then_inc(xT_done, 1)
            pe.wait_ge(token_scaled, 6)
            for k in range(KB):
                if k < 2:
                    pe.wait_ge(residual_in, KB - 1 + k)
                else:
                    pe.wait_ge(operand_low, OP["mem"] + k - 1)
                for tt in range(MB):
                    last = t_.transpose(aux[k % 2][:, tt * P:(tt + 1) * P],
                                        xn_tok[:, QB + tt, k * P:(k + 1) * P], ident[:])
                last.then_inc(mT_done, 1)
            for n, src in enumerate((kv, kiwi)):
                pe.wait_ge(doubled_out, n + 1)
                for b in range(QB):
                    last = t_.transpose(aux[4 + n][:, b * P:(b + 1) * P], src[:, b * P:(b + 1) * P],
                                        ident[:])
                last.then_inc(vwi_done, 1)
            pe.wait_ge(roped, 4)
            pe.wait_ge(v_out, 3)
            for n, (qb, h) in enumerate(INDEX):
                if n >= 4:
                    pe.wait_ge(rel_ready, n - 3)
                w, rows = (qb + 1) * P, slice(h % 2 * HALF, h % 2 * HALF + HALF)
                t_.matmul(aux[2 + h % 2 + 2 * (n // 2 % 2)][:, 0:w],
                          qiT[rows, h // 2, qb * P:(qb + 1) * P], kiT[rows, 0:w], start=True, stop=True
                          ).then_inc(index_logits, 1)
            in_tile(4)
            for n in range(4):
                in_tile(5 + n)
                pe.wait_ge(tile_out[n % 2], 3 + n // 2)
                if n == 0:
                    pe.wait_ge(operand_low, OP["mem"] + KB)
                if n == 2:
                    pe.wait_ge(rel_ready, len(INDEX))
                rotation(qT[:, n], P, aux[n])
            for n in range(9, 16):
                in_tile(n)
            with pe.Fori(0, KB // 2) as i:
                gemm_pair("kc", i, M, cols=MB * P)

            def turn_values(n):
                pe.wait_ge(tile_out[n % 2], TILE["vc"] // 2 + n // 2 + 1)
                if n >= 2:
                    pe.wait_ge(vc_out, n - 1)
                for b in range(MB):
                    last = t_.transpose(aux[4 + n % 2][:, b * P:(b + 1) * P], vcT[:, n % 2, b * P:(b + 1) * P],
                                        ident[:])
                last.then_inc(vcT_done, 1)

            for n in range(KB):
                m, s = CHUNK["vc"] // 2 + n // 2, n % 2
                free(s, TILE["vc"] // 2 + n // 2)
                chunk(m, s, KB, s, M, cols=MB * P)
                if n:
                    turn_values(n - 1)
            turn_values(KB - 1)
            pe.wait_ge(roped, 8)
            for n in range(4):
                pe.wait_ge(conv_ready, n + 1)
                last = t_.matmul(aux[0][:], ones[:], conv[:, n], start=n == 0, stop=n == 3)
            last.then_inc(mean_ready, 1)
            for n in range(4):
                pe.wait_ge(centred_squared, n + 1)
                last = t_.matmul(aux[1][:], ones[:], gate[:, n], start=n == 0, stop=n == 3)
            last.then_inc(variance_ready, 1)
            pe.wait_ge(ln_root, 1)
            pe.wait_ge(vc_out, KB)
            for step in range(len(DSA) + 2):
                if step < len(DSA):
                    qb, h = DSA[step]
                    if step >= 2:
                        pe.wait_ge(logits_masked, step - 1)
                    w, rows = (qb + 1) * P, slice(h % 2 * HALF, h % 2 * HALF + HALF)
                    t_.matmul(aux[h % 2][:, 0:w], qT[rows, h // 2, qb * P:(qb + 1) * P], kT[rows, 0:w],
                              start=True, stop=True).then_inc(logits, 1)
                j = step - 1
                if 0 <= j < len(DSA):
                    pe.wait_ge(prob_ready, j + 1)
                    if j >= 2:
                        pe.wait_ge(probT_ready, j - 1)
                    for b in range(DSA[j][0] + 1):
                        last = t_.transpose(aux[2 + j % 2][:, b * P:(b + 1) * P],
                                            prob[:, j % 2, b * P:(b + 1) * P], ident[:])
                    last.then_inc(probT_done, 1)
                j = step - 2
                if j >= 0:
                    qb, h = DSA[j]
                    g = j // 2
                    pe.wait_ge(probT_ready, j + 1)
                    if g >= 2 and h % 2 == 0:
                        pe.wait_ge(operand_low, OP["a"] + g - 1)
                    for b in range(qb + 1):
                        last = t_.matmul(aux[4 + g % 2][:, 0:P], v_pad[:, b, h % 2],
                                         probT[:, j % 2, b * P:(b + 1) * P],
                                         start=h % 2 == 0 and b == 0, stop=h % 2 == 1 and b == qb)
                    last.then_inc(heads_done, 1)

            pe.wait_ge(operand_low, OP["out"])
            gemm("out", KB // 2, A, None)
            gemm("qc", KB // 2, B, OP["out"],
                 between=lambda: sum_features(SQ["out"] + KB, square_sum[:], aux[0]))
            pe.wait_ge(tile_out[0], TILE["qc"] // 2 + KB // 2)
            pe.wait_ge(tile_out[1], TILE["qc"] // 2 + KB // 2)
            for step in range(len(CROSS) + 2):
                if step < len(CROSS):
                    h, qb = CROSS[step]
                    if step >= 2:
                        pe.wait_ge(x_masked, step - 1)
                    for c in range(X_KB):
                        last = t_.matmul(aux[step % 2][:, 0:MB * P],
                                         qcT[:, X_KB * h + c, qb * P:(qb + 1) * P], kcT[:, X_KB * h + c],
                                         start=c == 0, stop=c == X_KB - 1)
                    last.then_inc(x_logits, 1)
                j = step - 1
                if 0 <= j < len(CROSS):
                    pe.wait_ge(x_prob_ready, j + 1)
                    if j >= 2:
                        pe.wait_ge(x_probT_ready, j - 1)
                    for b in range(MB):
                        last = t_.transpose(aux[2 + j % 2][:, b * P:(b + 1) * P],
                                            xprob[:, j % 2, b * P:(b + 1) * P], ident[:])
                    last.then_inc(x_probT_done, 1)
                j = step - 2
                if j >= 0 and j % QB == QB - 1:
                    h = CROSS[j][0]
                    pe.wait_ge(x_probT_ready, j + 1)
                    for d in range(2):
                        if h:
                            pe.wait_ge(operand_low, OP["oc"] + 2 * (h - 1) + d + 1)
                        col0 = h * X_KB * P + d * P
                        for b in range(MB):
                            last = t_.matmul(aux[4 + d][:], vc[:, b, col0:col0 + P], xprobT[:, h % 2, b],
                                             start=b == 0, stop=b == MB - 1)
                        last.then_inc(x_heads_done, 1)
            gemm("oc", KB // 2, B, OP["oc"])
            gemm("ffn", FB, A, OP["wo"],
                 between=lambda: sum_features(SQ["wo"] + KB, square_sum[:], aux[0]))

            def down(name, n, t, s, ready=None):
                m = CHUNK[name] // 2 + n
                free(s, t)
                for half in range(2):
                    chunk(m, half, FH, s, H, k0=half * FH, start=half == 0, stop=half == 1,
                          ready=None if ready is None else ready + half * FH)

            def down_gemm(name, ready, after=None):
                for s in range(2):
                    down(name, s, TILE[name] // 2, s, ready=ready if s == 0 else None)
                with pe.Fori(1, KB // 2) as i:
                    for s in range(2):
                        down(name, 2 * i + s, TILE[name] // 2 + i, s)

            down_gemm("down", OP["h"])

            def two_sums():
                sum_features(SQ["down"] + 2 * KB, square_sum[:], aux[0])
                sum_features(SQ["down"] + 2 * KB, work[:, 1], aux[1])

            gemm("in2", 4, A, OP["down"], between=two_sums)

            def in2_tile(n):
                m, s = CHUNK["in2"] // 2 + n // 2, n % 2
                free(s, TILE["in2"] // 2 + n // 2)
                chunk(m, s, KB, s, A)

            pe.wait_ge(blockdiag_in, 16)
            for j in range(4):
                in2_tile(8 + 3 * j)
                pe.wait_ge(lconv_ready, j + 1)
                for r in range(2):
                    if j:
                        pe.wait_ge(lgates_ready, 2 * j - 1 + r)
                    t_.matmul(aux[1 + r][:], lru_weights[:, r, j], xc[:], start=True, stop=True
                              ).then_inc(lgates_done, 1)
                in2_tile(9 + 3 * j)
                pe.wait_ge(tile_out[j % 2], TILE["in2"] // 2 + (8 + 3 * j) // 2 + 1)
                if j:
                    pe.wait_ge(v2_out, 2 * j)
                for b in range(QB):
                    last = t_.transpose(aux[3][:, b * P:(b + 1) * P], vT2[:, j % 2, b * P:(b + 1) * P],
                                        ident[:])
                last.then_inc(vT2_done, 1)
                in2_tile(10 + 3 * j)
            sum_features(SQ["ylru"] + 4, square_sum[:], aux[0])
            pe.wait_ge(root_ready, RT["ylru"] + 1)
            pe.wait_ge(v2_out, 8)
            pe.wait_ge(tile_out[0], TILE["out2"] // 2)
            pe.wait_ge(tile_out[1], TILE["out2"] // 2)
            for step in range(len(STICK) + 2):
                if step < len(STICK):
                    p, qb, sub = STICK[step]
                    if step >= 2:
                        pe.wait_ge(breaks, 2 * (step - 1))
                    w, rows = (qb + 1) * P, slice(sub * HALF, (sub + 1) * HALF)
                    t_.matmul(aux[sub][:, 0:w], q2[rows, p, qb * P:(qb + 1) * P], k2[rows, p, 0:w],
                              start=True, stop=True).then_inc(sticks, 1)
                j = step - 1
                if 0 <= j < len(STICK):
                    pe.wait_ge(taken, j + 1)
                    if j >= 2:
                        pe.wait_ge(takenT_ready, j - 1)
                    for b in range(STICK[j][1] + 1):
                        last = t_.transpose(aux[2 + j % 2][:, b * P:(b + 1) * P],
                                            take[:, j % 2, b * P:(b + 1) * P], ident[:])
                    last.then_inc(takenT, 1)
                j = step - 2
                if j >= 0:
                    p, qb, sub = STICK[j]
                    pe.wait_ge(takenT_ready, j + 1)
                    if p >= 2 and qb == 0 and sub == 0:
                        pe.wait_ge(att_out, p - 1)
                    for b in range(qb + 1):
                        last = t_.matmul(aux[4 + p % 2][:, qb * P:(qb + 1) * P], v2[:, b, 2 * p + sub],
                                         takeT[:, j % 2, b * P:(b + 1) * P],
                                         start=sub == 0 and b == 0, stop=sub == 1 and b == qb)
                    last.then_inc(stick_heads, 1)
            sum_features(SQ["yatt"] + 4, square_sum[:], aux[0])
            gemm("out2", KB // 2, Y, OP["ylru"])
            gemm("ffn2", FB, A, OP["out2"],
                 between=lambda: sum_features(SQ["out2"] + KB, square_sum[:], aux[0]))

            def turn_out(n):
                pe.wait_ge(out_scaled, n + 1)
                if n >= 2:
                    pe.wait_ge(outT_out, n - 1)
                for b in range(QB):
                    last = t_.transpose(aux[2 + n % 2][:, b * P:(b + 1) * P],
                                        work[:, n % 2, b * P:(b + 1) * P], ident[:])
                last.then_inc(outT_done, 1)

            for n in range(KB):
                down("down2", n, TILE["down2"] // 2 + n // 2, n % 2, ready=OP["h2"] if n == 0 else None)
                if n:
                    turn_out(n - 1)
            turn_out(KB - 1)
            pe.wait_ge(summed, SQ["down2"] + KB)
            for tt in range(QB):
                last = t_.matmul(aux[0][:, tt:tt + 1], square_sum[:, tt * P:(tt + 1) * P], ones[:, 0:1],
                                 start=True, stop=True)
            last.then_inc(out_sums, 1)


def _column_blocks(w, starts, width=P):
    rows = w.shape[0] // P
    cut = np.stack([w[:, s:s + width] for s in starts])
    return cut.reshape(len(starts), rows, P, width).transpose(0, 2, 1, 3).reshape(len(starts), P, -1)


def _columns(v):
    v = v.reshape(-1, v.shape[-1] // P, P)
    return v.transpose(2, 1, 0).reshape(P, -1)


def kernel(**a):
    from concourse import bacc
    from concourse.bass_utils import run_bass_kernel_spmd
    a = {k: np.asarray(v) for k, v in a.items()}
    every = [n * P for n in range(FB)]
    d = every[:KB]
    w_in, w_in2, ffn_in2 = a["w_in"][0], a["w_in_2"][0], a["w_ffn_in_2"][0]
    glu0 = 964
    starts = [512, 896, 640, 768] + every[:4]
    for n in range(4):
        starts += [glu0 + n * P, glu0 + 512 + n * P]
    starts2 = every[:8]
    for n in range(4):
        starts2 += [2048 + n * P, 1024 + n * P, 1536 + n * P]
    pairs = []
    for gate, up in ((a["w_gate"][0], a["w_up"][0]), (ffn_in2[:, :F], ffn_in2[:, F:])):
        both = np.stack([_column_blocks(gate, every), _column_blocks(up, every)], 1)
        pairs.append(both.reshape(2 * FB, P, -1))
    w8 = np.concatenate([
        _column_blocks(w_in, starts), _column_blocks(a["w_k_cross"][0], d),
        _column_blocks(a["w_v_cross"][0], d), _column_blocks(a["w_out"][0], d),
        _column_blocks(a["w_q_cross"][0], d), _column_blocks(a["w_o_cross"][0], d), pairs[0],
        _column_blocks(w_in2, starts2), _column_blocks(a["w_out_2"][0], d), pairs[1]])
    halves = []
    for w in (a["w_down"][0], a["w_ffn_out_2"][0]):
        halves.append(_column_blocks(w, d).reshape(KB, P, 2, FH * P).transpose(0, 2, 1, 3)
                      .reshape(2 * KB, P, FH * P))
    w11 = np.concatenate(halves)
    freq = np.float32(500000.0) ** (-np.arange(0, 16, 2, dtype=np.float32) / np.float32(16))
    head = np.concatenate([freq, freq, np.zeros(48, np.float32)]).astype(np.float32)
    given = {"g_mix": a["norm_mix_g"], "g_cross": a["norm_cross_g"], "g_mem": a["norm_mem_g"],
             "g_ffn": a["norm_ffn_g"], "g_final": a["norm_final_g"], "g_mix2": a["norm_mix_2"],
             "g_ffn2": a["norm_ffn_2"], "g_final2": a["norm_final_2"], "ln_g": a["ln_b_g"],
             "ln_b": a["ln_b_b"], "g_lru": a["norm_lru_out_2"], "g_att": a["norm_att_out_2"],
             "conv_w": a["conv_b_w"][0], "conv_b": a["conv_b_b"], "fconv_w": a["ffn_conv_w"][0],
             "fconv_b": a["ffn_conv_b"], "lconv_w": a["conv_w_2"][0], "lconv_b": a["conv_b_2"],
             "b_rg": a["b_rg_2"].reshape(-1), "b_ig": a["b_ig_2"].reshape(-1),
             "lam": a["lru_lambda_2"], "freq": np.concatenate([head, head])}
    params = np.ascontiguousarray(np.concatenate([_columns(given[k]) for k, _ in PARAMS], 1))
    blockdiag = np.zeros((P, 2, 4, P), np.float32)
    for r, name in enumerate(("w_rg_2", "w_ig_2")):
        for n in range(8):
            at = slice(n % 2 * HALF, n % 2 * HALF + HALF)
            blockdiag[at, r, n // 2, at] = a[name][0, n]
    arrays = {"w8": w8, "w11": w11, "x": a["x"][0], "mem": a["mem"][0],
              "positions": a["positions"][0].astype(np.int32), "params": params,
              "blockdiag": blockdiag}
    arrays = {k: np.ascontiguousarray(v) for k, v in arrays.items()}
    nc = bacc.Bacc("TRN2", target_bir_lowering=False, num_devices=1)
    aps = [nc.dram_tensor(k, v.shape, mybir.dt.from_np(v.dtype), kind="ExternalInput").ap()
           for k, v in arrays.items()]
    out = nc.dram_tensor("out", (T, D), F32, kind="ExternalOutput").ap()
    build(nc, *aps, out)
    r = run_bass_kernel_spmd(nc, [arrays], core_ids=[0])
    return r.results[0]["out"].reshape(1, T, D)
```

```python
import numpy as np
import concourse.bass as bass
from concourse import mybir
from contextlib import ExitStack

F32 = mybir.dt.float32
F32R = mybir.dt.float32r
I32 = mybir.dt.int32
ALU = mybir.AluOpType
ACT = mybir.ActivationFunctionType

P = 128
T = 512
QB = T // P
D = 1024
KB = D // P
F = 2816
FB = F // P
FH = FB // 2
HALF = 64
A_HEADS = 8
IDX_HEADS = 4
TOPK = 128
MB = 256 // P
X_HEADS = 4
X_KB = 256 // P
TAPS = 31
TAPS_FFN = 3
TAPS_LRU = 4
EPS = 1e-6
NEG = -1e30
CHOSEN = -3e38
ROUND = 1.5 * 2.0 ** 23
TWO_PI = (6.28125, 0.0019350051879882812, 3.0199159819567e-07)

GEMMS = (("in", 16), ("kc", 8), ("vc", 8), ("out", 8), ("qc", 8), ("oc", 8), ("ffn", 2 * FB),
         ("down", 16), ("in2", 20), ("out2", 8), ("ffn2", 2 * FB), ("down2", 16))
CHUNK, TILE = {}, {}
_c = _t = 0
for _name, _n in GEMMS:
    CHUNK[_name], TILE[_name] = _c, _t
    _c += _n
    _t += _n // 2 if _name.startswith("down") else _n
CHUNKS, TILES = _c, _t
WIDE = (("down", 0), ("down2", 16))

PARAMS = (("g_mix", KB), ("g_cross", KB), ("g_mem", KB), ("g_ffn", KB), ("g_final", KB),
          ("g_mix2", KB), ("g_ffn2", KB), ("g_final2", KB), ("ln_g", 4), ("ln_b", 4),
          ("g_lru", 4), ("g_att", 4), ("conv_w", 4 * TAPS), ("conv_b", 4), ("fconv_w", FB * TAPS_FFN),
          ("fconv_b", FB), ("lconv_w", 4 * TAPS_LRU), ("lconv_b", 4), ("b_rg", 4), ("b_ig", 4),
          ("lam", 4), ("freq", 1))
PCOL = {}
_p = 0
for _name, _n in PARAMS:
    PCOL[_name] = _p
    _p += _n
PCOLS = _p


class Steps:

    def __init__(self, eng, sem):
        self.eng, self.sem, self.at = eng, sem, 0

    def step(self, ins):
        ins.then_inc(self.sem, 1)
        self.at = self.at + 1

    def settle(self, lag=0):
        self.eng.wait_ge(self.sem, self.at - lag)

    def then(self, ins):
        self.step(ins)
        self.settle()

    def run(self, first, end, each, body):
        start, self.passes = self.at, 0
        with self.eng.Fori(first, end) as i:
            self.at = start + (i - first) * each
            body(i)
        self.at = start + (end - first) * each


def build(nc, w8, w11, x, mem, positions, params, blockdiag, out):
    ctx = ExitStack()
    with ctx:
        def sb(name, shape, dt=F32, where=ctx):
            return where.enter_context(nc.sbuf_tensor(name, shape, dt))

        def sem(name):
            return ctx.enter_context(nc.semaphore(name))

        weights_raw = sb("weights_raw", [P, 2, FH * P])
        weights_high = sb("weights_high", [P, 2, FH * P], F32R)
        weights_low = sb("weights_low", [P, 2, FH * P], F32R)
        residual = sb("residual", [P, KB, T])
        a_high = sb("a_high", [P, KB, T], F32R)
        a_low = sb("a_low", [P, KB, T], F32R)
        par = sb("par", [P, PCOLS])
        small = sb("small", [P, 72])
        ident = sb("ident", [P, P])
        ones = sb("ones", [P, P])
        rotate = sb("rotate", [P, P])
        twice = sb("twice", [P, P])
        causal = sb("causal", [P, P])
        before = sb("before", [P, P])
        notbefore = sb("notbefore", [P, P])
        row_factor = sb("row_factor", [P, T])
        square = sb("square", [P, T])
        square_sum = sb("square_sum", [P, T])

        def col(name, n=0, width=1):
            c = PCOL[name]
            return par[:, c + n:c + n + width]

        def dcol(name, n):
            return par[:, bass.ds(PCOL[name] + n, 1)]

        eps = small[:, 0:1]
        tok_sum = small[:, 1:7]
        tok_root = small[:, 7:13]
        tok_factor = small[:, 13:19]
        best = small[:, 19:27]
        least = small[:, 27:29]
        total = small[:, 29:31]
        inverse = small[:, 31:33]
        decay = small[:, 33:37]
        both_gains = small[:, 37:45]
        first_factor = small[:, 62:66]
        scaled_sum = small[:, 66:70]
        half_pi = small[:, 45:46]
        sp = small[:, 46:62]

        s12 = ExitStack()
        kcT = sb("kcT", [P, KB, MB * P], where=s12)
        vc = sb("vc", [P, MB, D], where=s12)
        s1 = ExitStack()
        m_high = sb("m_high", [P, KB, MB * P], F32R, s1)
        m_low = sb("m_low", [P, KB, MB * P], F32R, s1)
        qT = sb("qT", [P, 4, T], where=s1)
        qiT = sb("qiT", [P, 2, T], where=s1)
        kv = sb("kv", [P, T], where=s1)
        kiwi = sb("kiwi", [P, T], where=s1)
        kT = sb("kT", [P, T], where=s1)
        kiT = sb("kiT", [P, T], where=s1)
        v_pad = sb("v_pad", [P, QB, 2, P], where=s1)
        wi = sb("wi", [P, QB, IDX_HEADS], where=s1)
        cosine = sb("cosine", [P, T], where=s1)
        turned = sb("turned", [P, T], where=s1)
        sine = sb("sine", [P, T], where=s1)
        s1a = ExitStack()
        x_tok = sb("x_tok", [P, 6, D], where=s1a)
        xn_tok = sb("xn_tok", [P, 6, D], where=s1a)
        s1a.close()
        s1b = ExitStack()
        glu = sb("glu", [P, 4, TAPS - 1 + T], where=s1b)
        gate = sb("gate", [P, 4, T], where=s1b)
        conv = sb("conv", [P, 4, T], where=s1b)
        score = sb("score", [P, 3, T], where=s1b)
        rel = sb("rel", [P, 2, T], where=s1b)
        masked = sb("masked", [P, 2, T], where=s1b)
        prob = sb("prob", [P, 3, T], where=s1b)
        probT = sb("probT", [P, 2, T], where=s1b)
        vcT = sb("vcT", [P, 2, MB * P], where=s1b)
        s1b.close()
        s1.close()
        s2 = ExitStack()
        b_high = sb("b_high", [P, KB, T], F32R, s2)
        b_low = sb("b_low", [P, KB, T], F32R, s2)
        qcT = sb("qcT", [P, KB, T], where=s2)
        zeros = sb("zeros", [P, MB * P], where=s2)
        o_high = sb("o_high", [P, KB, T], F32R, s2)
        o_low = sb("o_low", [P, KB, T], F32R, s2)
        xmasked = sb("xmasked", [P, 2, MB * P], where=s2)
        xprob = sb("xprob", [P, 3, MB * P], where=s2)
        xprobT = sb("xprobT", [P, 2, MB, T], where=s2)
        s2.close()
        s12.close()

        s3 = ExitStack()
        h_high = sb("h_high", [P, FB, T], F32R, s3)
        h_low = sb("h_low", [P, FB, T], F32R, s3)
        gated = sb("gated", [P, TAPS_FFN - 1 + T], where=s3)
        work = sb("work", [P, 2, T], where=s3)
        y_tok = sb("y_tok", [P, QB, D], where=s3)
        s3.close()

        s4 = ExitStack()
        y_high = sb("y_high", [P, KB, T], F32R, s4)
        y_low = sb("y_low", [P, KB, T], F32R, s4)
        lru_weights = sb("lru_weights", [P, 2, 4, P], where=s4)
        lru_in = sb("lru_in", [P, 4, TAPS_LRU - 1 + T], where=s4)
        lru_gate = sb("lru_gate", [P, 4, T], where=s4)
        q2 = sb("q2", [P, 4, T], where=s4)
        k2 = sb("k2", [P, 4, T], where=s4)
        vT2 = sb("vT2", [P, T], where=s4)
        v2 = sb("v2", [P, QB, A_HEADS, P], where=s4)
        xc = sb("xc", [P, T], where=s4)
        gates = sb("gates", [P, 2, T], where=s4)
        half_tanh = sb("half_tanh", [P, T], where=s4)
        gate_root = sb("gate_root", [P, T], where=s4)
        inverse_sum = sb("inverse_sum", [P, T], where=s4)
        stay = sb("stay", [P, 2, T], where=s4)
        take = sb("take", [P, 3, T], where=s4)
        left = sb("left", [P, T], where=s4)
        takeT = sb("takeT", [P, 2, T], where=s4)
        s4.close()

        acc = ctx.enter_context(nc.psum_tensor("acc", [P, 2, T], F32))
        aux = [ctx.enter_context(nc.psum_tensor(f"aux{i}", [P, T], F32)) for i in range(6)]
        chunk_landed = [sem("chunk_landed0"), sem("chunk_landed1")]
        weight_high = sem("weight_high")
        weight_low = sem("weight_low")
        chunk_done = sem("chunk_done")
        tile_out = [sem("tile_out0"), sem("tile_out1")]
        operand_high = sem("operand_high")
        operand_low = sem("operand_low")
        squared = sem("squared")
        summed = sem("summed")
        sums_ready = sem("sums_ready")
        root_ready = sem("root_ready")
        factor_ready = sem("factor_ready")
        factor_spread = sem("factor_spread")
        act_steps = sem("act_steps")
        dve_steps = sem("dve_steps")
        consts_ready = sem("consts_ready")
        params_in = sem("params_in")
        positions_in = sem("positions_in")
        blockdiag_in = sem("blockdiag_in")
        x_in = [sem(f"x_in{i}") for i in range(6)]
        angle_ready = sem("angle_ready")
        tables_ready = sem("tables_ready")
        softplus_exp = sem("softplus_exp")
        token_root = sem("token_root")
        token_scaled = sem("token_scaled")
        xnT_done = sem("xnT_done")
        xT_done = sem("xT_done")
        residual_in = sem("residual_in")
        mT_done = sem("mT_done")
        rotated = sem("rotated")
        roped = sem("roped")
        doubled = sem("doubled")
        doubled_out = sem("doubled_out")
        vwi_done = sem("vwi_done")
        v_out = sem("v_out")
        cleared = sem("cleared")
        index_logits = sem("index_logits")
        rel_ready = sem("rel_ready")
        rel_used = sem("rel_used")
        vcT_done = sem("vcT_done")
        vc_out = sem("vc_out")
        conv_steps = sem("conv_steps")
        b_high_ready = sem("b_high_ready")
        b_low_ready = sem("b_low_ready")
        mean_ready = sem("mean_ready")
        centred = sem("centred")
        centred_squared = sem("centred_squared")
        variance_ready = sem("variance_ready")
        ln_root = sem("ln_root")
        ln_factor = sem("ln_factor")
        ln_spread = sem("ln_spread")
        ln_scaled = sem("ln_scaled")
        logits = sem("logits")
        logits_masked = sem("logits_masked")
        prob_raw = sem("prob_raw")
        prob_inverse = sem("prob_inverse")
        prob_ready = sem("prob_ready")
        probT_done = sem("probT_done")
        probT_ready = sem("probT_ready")
        heads_done = sem("heads_done")
        x_logits = sem("x_logits")
        x_masked = sem("x_masked")
        x_prob_raw = sem("x_prob_raw")
        x_prob_ready = sem("x_prob_ready")
        x_probT_done = sem("x_probT_done")
        x_probT_ready = sem("x_probT_ready")
        x_heads_done = sem("x_heads_done")
        gate_ready = sem("gate_ready")
        silu_ready = sem("silu_ready")
        hidden_ready = sem("hidden_ready")
        rescaled = sem("rescaled")
        lconv_ready = sem("lconv_ready")
        lgates_done = sem("lgates_done")
        lgates_ready = sem("lgates_ready")
        tanh_ready = sem("tanh_ready")
        lroot_ready = sem("lroot_ready")
        lru_done = sem("lru_done")
        gelu_ready = sem("gelu_ready")
        y_scaled = sem("y_scaled")
        vT2_done = sem("vT2_done")
        v2_out = sem("v2_out")
        v2_clear = sem("v2_clear")
        sticks = sem("sticks")
        breaks = sem("breaks")
        taken = sem("taken")
        takenT = sem("takenT")
        takenT_ready = sem("takenT_ready")
        stick_heads = sem("stick_heads")
        att_out = sem("att_out")
        out_scaled = sem("out_scaled")
        outT_done = sem("outT_done")
        outT_out = sem("outT_out")
        out_sums = sem("out_sums")
        out_ready = sem("out_ready")
        stored = sem("stored")

        OP = {"x": 0, "mem": 8, "a": 16, "out": 32, "oc": 40, "wo": 48, "h": 56,
              "down": 78, "ylru": 86, "yatt": 90, "out2": 94, "h2": 102}
        SQ = {"out": 0, "wo": 8, "down": 16, "ylru": 32, "yatt": 36, "out2": 40, "down2": 48}
        RT = {"out": 0, "wo": 1, "down": 2, "ylru": 4, "yatt": 5, "out2": 6, "down2": 7}
        TT = range(6)
        DSA = [(qb, h) for qb in range(QB) for h in range(A_HEADS)]
        CROSS = [(h, qb) for h in range(X_HEADS) for qb in range(QB)]
        STICK = [(p, qb, sub) for p in range(4) for qb in range(QB) for sub in range(2)]
        CONV = [(n, k) for pair in range(2) for k in range(TAPS) for n in (2 * pair, 2 * pair + 1)]
        CONV_STEPS = 22
        LN_MEAN, LN_VAR, LN_OUT, LN_LOW = 22, 24, 25, 26
        DSA_STEPS = len(DSA) + 4
        EARLY_TAPS = 36
        CROSS_PLAN = [("query", 0, 0, 8), ("query", 1, 0, 4), ("factor", 0), ("query", 1, 4, 8)]
        for n in range(2, KB):
            for half in range(2):
                step = 2 * (n - 2) + half
                CROSS_PLAN += [("query", n, 4 * half, 4 * half + 3), ("step", step),
                               ("query", n, 4 * half + 3, 4 * half + 4)]
        for step, piece in enumerate(((0, 0, 2), (0, 2, 4), (1, 0, 2), (1, 2, 4), (0, 4, 5), (0, 5, 6),
                                      (1, 4, 5), (1, 5, 6), ()), 12):
            if step < 20:
                CROSS_PLAN += [("step", step)]
            if piece:
                CROSS_PLAN += [("first", *piece)]
        CROSS_PLAN += [("first", 0, 6, 8), ("first", 1, 6, 8)]
        REC_PLAN = []

        def piece(n, k):
            return [("tile", n, 2 * k, 2 * k + 2)]

        for j in range(4):
            steps = [[("step", 8 * (j - 1) + i)] if j else [] for i in range(8)]
            V, Q, K = ([piece(8 + 3 * j + i, k) for k in range(4)] for i in range(3))
            for part in (V[0], [("conv", j)], V[1], steps[0], V[2], [("gate", j, 0)], V[3], steps[1],
                         Q[0], [("gate", j, 1)], steps[2], Q[1], [("turn", j)], steps[3], Q[2],
                         [("late", j)], Q[3], steps[4], K[0], steps[5], K[1], [("square", j)], steps[6],
                         K[2], steps[7], K[3]):
                REC_PLAN += part
        REC_PLAN += [("lru_sum",), ("step", 24), ("lru_spread",), ("step", 25), ("lru_scale",), ("step", 26),
                     ("lru_low",), ("step", 27), ("first", 0, 0, 2),
                     ("step", 28), ("att_square", 0), ("step", 29), ("first", 0, 2, 4),
                     ("att_square", 1), ("step", 30), ("att_square", 2), ("first", 1, 0, 2), ("step", 31),
                     ("step", 32), ("first", 1, 2, 4), ("step", 33),
                     ("step", 34), ("step", 35), ("att_square", 3), ("att_sum",), ("att_spread",),
                     ("att_scale",), ("first", 0, 4, 8), ("first", 1, 4, 8)]
        SPREAD = 4
        INDEX = [(qb, h) for qb in range(1, QB) for h in range(IDX_HEADS)]

        def w8_chunk(c):
            return w8[bass.ds(c, 1)].rearrange("a p n -> (a p) n")

        def w_of(step):
            return (DSA[step][0] + 1) * P

        block = ctx.enter_context(nc.Block())

        @block.sync
        def _(sp):
            def load(m, s, src, cols):
                sp.wait_ge(weight_low, 2 * m + s - 1)
                sp.dma_start(weights_raw[:, s, 0:cols], src).then_inc(chunk_landed[s], 16)

            for tt in range(QB):
                sp.dma_start(x_tok[:, tt], x[tt * P:(tt + 1) * P, :]).then_inc(x_in[tt], 16)
            for s in range(2):
                sp.dma_start(weights_raw[:, s, 0:KB * P], w8[s]).then_inc(chunk_landed[s], 16)
            for tt in range(2):
                sp.dma_start(x_tok[:, QB + tt], mem[tt * P:(tt + 1) * P, :]).then_inc(x_in[QB + tt], 16)
            with sp.Fori(1, CHUNK["down"] // 2) as m:
                for s in range(2):
                    load(m, s, w8_chunk(2 * m + s), KB * P)
            with sp.Fori(0, 8) as m:
                for s in range(2):
                    load(m + CHUNK["down"] // 2, s,
                         w11[bass.ds(2 * m + s, 1)].rearrange("a p n -> (a p) n"), FH * P)
            with sp.Fori(CHUNK["in2"] // 2, CHUNK["down2"] // 2) as m:
                for s in range(2):
                    load(m, s, w8_chunk(2 * m + s - 16), KB * P)
            with sp.Fori(0, 8) as m:
                for s in range(2):
                    load(m + CHUNK["down2"] // 2, s,
                         w11[bass.ds(2 * m + s + 16, 1)].rearrange("a p n -> (a p) n"), FH * P)
            for tt in range(QB):
                sp.wait_ge(out_ready, tt + 1)
                sp.dma_start(out[tt * P:(tt + 1) * P, :], y_tok[:, tt]).then_inc(stored, 16)
            sp.wait_ge(stored, 16 * QB)

        @block.gpsimd
        def _(pool):
            made = [0]

            def then(ins):
                made[0] += 1
                ins.then_inc(consts_ready, 1)
                pool.wait_ge(consts_ready, made[0])

            g = nc.gpsimd
            for t in (ident, rotate, twice, causal):
                then(g.memset(t[:], 0.0))
            for t in (ones, before):
                then(g.memset(t[:], 1.0))
            then(g.memset(notbefore[:], 0.0))
            then(g.memset(eps, EPS))
            then(g.memset(half_pi, float(np.pi / 2)))
            then(g.affine_select(out=ident[:], in_=ident[:], compare_op=ALU.not_equal, fill=1.0, base=0,
                                 pattern=[[-1, P]], channel_multiplier=1))
            heads = rotate[:].rearrange("p (a b) -> p a b", b=HALF)
            then(g.affine_select(out=heads[:, :, 0:8], in_=heads[:, :, 0:8], compare_op=ALU.not_equal,
                                 fill=-1.0, base=-8, pattern=[[-HALF, 2], [-1, 8]], channel_multiplier=1))
            then(g.affine_select(out=heads[:, :, 8:16], in_=heads[:, :, 8:16], compare_op=ALU.not_equal,
                                 fill=1.0, base=0, pattern=[[-HALF, 2], [-1, 8]], channel_multiplier=1))
            copies = twice[:].rearrange("p (a b) -> p a b", b=HALF)
            then(g.affine_select(out=copies, in_=copies, compare_op=ALU.not_equal, fill=1.0, base=0,
                                 pattern=[[0, 2], [-1, HALF]], channel_multiplier=1))
            then(g.affine_select(out=causal[:], in_=causal[:], compare_op=ALU.is_ge, fill=NEG, base=0,
                                 pattern=[[-1, P]], channel_multiplier=1))
            then(g.affine_select(out=before[:], in_=before[:], compare_op=ALU.is_gt, fill=0.0, base=0,
                                 pattern=[[-1, P]], channel_multiplier=1))
            then(g.affine_select(out=notbefore[:], in_=notbefore[:], compare_op=ALU.is_gt, fill=1.0,
                                 base=0, pattern=[[-1, P]], channel_multiplier=1))

            def low(m, s, cols):
                pool.wait_ge(weight_high, 2 * m + s + 1)
                g.tensor_tensor(weights_low[:, s, 0:cols], weights_raw[:, s, 0:cols],
                                weights_high[:, s, 0:cols].bitcast(F32), ALU.subtract
                                ).then_inc(weight_low, 1)

            for first, end, cols in ((0, CHUNK["down"], KB * P), (CHUNK["down"], CHUNK["in2"], FH * P),
                                     (CHUNK["in2"], CHUNK["down2"], KB * P),
                                     (CHUNK["down2"], CHUNKS, FH * P)):
                with pool.Fori(first // 2, end // 2) as m:
                    for s in range(2):
                        low(m, s, cols)
        NCONST = 16

        @block.scalar
        def _(act):
            a = nc.scalar
            own = Steps(act, act_steps)

            act.dma_start(par[:], params).then_inc(params_in, 16)
            act.dma_start(sine[:].bitcast(I32), positions.partition_broadcast(P)).then_inc(positions_in, 16)

            def high(m, s, cols=KB * P):
                act.wait_ge(chunk_landed[s], 16 * (m + 1))
                act.wait_ge(chunk_done, 2 * m + s - 1)
                a.copy(weights_high[:, s, 0:cols], weights_raw[:, s, 0:cols]).then_inc(weight_high, 1)

            def high_next(m, s, cols=KB * P):
                high(m + 1, s, cols)

            def tile_done(m, s):
                act.wait_ge(chunk_done, 2 * m + s + 1)

            act.wait_ge(consts_ready, NCONST)

            def row_roots(tt):
                act.wait_ge(x_in[tt], 16)
                own.then(a.activation(xn_tok[:, tt], x_tok[:, tt], ACT.Square,
                                      accum_out=tok_sum[:, tt:tt + 1]))
                a.activation(tok_root[:, tt:tt + 1], tok_sum[:, tt:tt + 1], ACT.Sqrt, scale=1.0 / D,
                             bias=eps).then_inc(token_root, 1)

            for tt in range(QB):
                row_roots(tt)
            for s in range(2):
                act.wait_ge(chunk_landed[s], 16)
                a.copy(weights_high[:, s, 0:KB * P], weights_raw[:, s, 0:KB * P]).then_inc(weight_high, 1)
            act.wait_ge(params_in, 16)
            for k in range(KB):
                act.wait_ge(xnT_done, k + 1)
                a.activation(a_high[:, k], aux[k % 6][:], ACT.Copy, scale=col("g_mix", k)
                             ).then_inc(operand_high, 1)
            act.wait_ge(angle_ready, 2)
            own.step(a.activation(sine[:], sine[:], ACT.Sin))
            a.activation(cosine[:], cosine[:], ACT.Sin, bias=half_pi, scale=-1.0).then_inc(tables_ready, 1)
            act.wait_ge(angle_ready, 3)
            a.activation(sp[:, 0:4], sp[:, 0:4], ACT.Exp, scale=-1.0).then_inc(softplus_exp, 1)
            for tt in (4, 5):
                row_roots(tt)
            for n, dst in enumerate((kv[:], kiwi[:], qiT[:, 0], qiT[:, 1])):
                m, s = n // 2, n % 2
                high_next(m, s)
                tile_done(m, s)
                a.copy(dst, acc[:, s]).then_inc(tile_out[s], 1)
            for n, dst in enumerate((kT, kiT)):
                act.wait_ge(doubled, n + 1)
                a.copy(dst[:], aux[4 + n][:]).then_inc(doubled_out, 1)
            for k in range(KB):
                act.wait_ge(xT_done, k + 1)
                a.copy(residual[:, k], aux[k % 2][:]).then_inc(residual_in, 1)
            for k in range(KB):
                act.wait_ge(mT_done, k + 1)
                a.activation(m_high[:, k], aux[k % 2][:, 0:MB * P], ACT.Copy, scale=col("g_mem", k)
                             ).then_inc(operand_high, 1)
            act.wait_ge(vwi_done, 1)
            act.wait_ge(cleared, 1)
            v_tok = aux[4][:].rearrange("p (b f) -> p b f", f=P)[:, :, HALF:P]
            a.copy(v_pad[:, :, 0, 0:HALF], v_tok).then_inc(v_out, 1)
            a.copy(v_pad[:, :, 1, HALF:P], v_tok).then_inc(v_out, 1)
            act.wait_ge(vwi_done, 2)
            a.mul(wi[:], aux[5][:].rearrange("p (b f) -> p b f", f=P)[:, :, HALF:HALF + IDX_HEADS],
                  IDX_HEADS ** -0.5).then_inc(v_out, 1)
            for n, (qb, h) in enumerate(INDEX):
                act.wait_ge(index_logits, n + 1)
                if n >= 2:
                    act.wait_ge(rel_used, n - 1)
                bank = aux[2 + h % 2 + 2 * (n // 2 % 2)]
                a.activation(rel[:, n % 2, 0:(qb + 1) * P], bank[:, 0:(qb + 1) * P], ACT.Relu,
                             scale=HALF ** -0.5).then_inc(rel_ready, 1)
            for n in range(4):
                m, s = 2 + n // 2, n % 2
                high_next(m, s)
                tile_done(m, s)
                a.copy(qT[:, n], acc[:, s]).then_inc(tile_out[s], 1)
            for n in range(4):
                m = 4 + n
                high_next(m, 0)
                tile_done(m, 0)
                a.copy(glu[:, n, TAPS - 1:TAPS - 1 + T], acc[:, 0]).then_inc(tile_out[0], 1)
                high_next(m, 1)
                tile_done(m, 1)
                a.activation(gate[:, n], acc[:, 1], ACT.Sigmoid).then_inc(tile_out[1], 1)
            with act.Fori(CHUNK["kc"] // 2, CHUNK["vc"] // 2) as m:
                for s in range(2):
                    high_next(m, s)
                    tile_done(m, s)
                    a.copy(kcT[:, bass.ds(2 * m + s - CHUNK["kc"], 1)].rearrange("p a n -> p (a n)"),
                           acc[:, s, 0:MB * P]).then_inc(tile_out[s], 1)

            def vc_back(n):
                act.wait_ge(vcT_done, n + 1)
                a.copy(vc[:, :, n * P:(n + 1) * P],
                       acc[:, n % 2, MB * P:2 * MB * P].rearrange("p (b f) -> p b f", f=P)
                       ).then_inc(vc_out, 1)

            def vc_tile(n):
                m, s = CHUNK["vc"] // 2 + n // 2, n % 2
                high_next(m, s)
                if n >= 2:
                    act.wait_ge(vcT_done, n - 1)
                a.copy(vcT[:, s], acc[:, s, 0:MB * P]).then_inc(tile_out[s], 1)

            for step in range(DSA_STEPS):
                if step < len(DSA):
                    w = w_of(step)
                    act.wait_ge(logits_masked, step + 1)
                    if step >= 3:
                        act.wait_ge(probT_done, step - 2)
                    a.activation(prob[:, step % 3, 0:w], masked[:, step % 2, 0:w], ACT.Exp, scale=-1.0,
                                 bias=least[:, step % 2:step % 2 + 1],
                                 accum_out=total[:, step % 2:step % 2 + 1]).then_inc(prob_raw, 1)
                j = step - 1
                if 0 <= j < len(DSA):
                    w = w_of(j)
                    act.wait_ge(prob_inverse, j + 1)
                    a.activation(prob[:, j % 3, 0:w], prob[:, j % 3, 0:w], ACT.Copy,
                                 scale=inverse[:, j % 2:j % 2 + 1]).then_inc(prob_ready, 1)
                if step < KB:
                    vc_tile(step)
                if 1 <= step <= KB:
                    vc_back(step - 1)
                j = step - 2
                if 0 <= j < len(DSA):
                    w = w_of(j)
                    act.wait_ge(probT_done, j + 1)
                    if j >= 2:
                        act.wait_ge(heads_done, j - 1)
                    a.copy(probT[:, j % 2, 0:w], aux[2 + j % 2][:, 0:w]).then_inc(probT_ready, 1)
                j = step - 4
                if j >= 0 and j % 2:
                    qb, h = DSA[j]
                    act.wait_ge(heads_done, j + 1)
                    a.copy(a_high[:, h // 2, qb * P:(qb + 1) * P], aux[4 + j // 2 % 2][:, 0:P]
                           ).then_inc(operand_high, 1)
                if step == LN_MEAN:
                    for n in range(4):
                        act.wait_ge(centred, n + 1)
                        a.activation(gate[:, n], conv[:, n], ACT.Square).then_inc(centred_squared, 1)
                if step == LN_VAR:
                    act.wait_ge(variance_ready, 1)
                    a.activation(tok_root[:, 0:QB], acc[:, 1, 0:QB], ACT.Sqrt, scale=1.0 / (4 * P), bias=eps
                                 ).then_inc(ln_root, 1)
                if step == LN_OUT:
                    for n in range(4):
                        act.wait_ge(ln_scaled, n + 1)
                        own.then(a.activation(conv[:, n], conv[:, n], ACT.Silu, scale=col("ln_g", n),
                                              bias=col("ln_b", n)))
                        a.copy(a_high[:, 4 + n], conv[:, n]).then_inc(b_high_ready, 1)

            def take_root(rt, bank, width):
                act.wait_ge(sums_ready, rt + 1)
                a.activation(tok_root[:, 0:QB], bank[:, 0:QB], ACT.Sqrt, scale=1.0 / width, bias=eps
                             ).then_inc(root_ready, 1)

            def residual_tile(m, s, n, sq, op, gain, dst):
                act.wait_ge(tile_out[s], m + 1)
                if sq is not None:
                    act.wait_ge(summed, sq + n)
                    a.activation(square[:], residual[:, bass.ds(n, 1)], ACT.Square
                                 ).then_inc(squared, 1)
                a.activation(dst[:, bass.ds(n, 1)], residual[:, bass.ds(n, 1)], ACT.Copy,
                             scale=dcol(gain, n)).then_inc(operand_high, 1)

            def residual_gemm(name, sq, op, gain, dst):
                first = CHUNK[name] // 2
                tile = TILE[name] // 2
                with act.Fori(0, KB // 2) as i:
                    for s in range(2):
                        high_next(first + i, s)
                        residual_tile(tile + i, s, 2 * i + s, sq, op, gain, dst)

            residual_gemm("out", SQ["out"], OP["out"], "g_cross", b_high)
            def cross_step(step):
                if step < len(CROSS):
                    act.wait_ge(x_masked, step + 1)
                    if step >= 3:
                        act.wait_ge(x_probT_done, step - 2)
                    a.activation(xprob[:, step % 3], xmasked[:, step % 2], ACT.Exp, scale=-1.0,
                                 bias=least[:, step % 2:step % 2 + 1],
                                 accum_out=total[:, step % 2:step % 2 + 1]).then_inc(x_prob_raw, 1)
                j = step - 2
                if 0 <= j < len(CROSS):
                    h, qb = CROSS[j]
                    act.wait_ge(x_probT_done, j + 1)
                    if h >= 2:
                        act.wait_ge(x_heads_done, 2 * (h - 1))
                    a.copy(xprobT[:, h % 2, :, qb * P:(qb + 1) * P],
                           aux[2 + j % 2][:, 0:MB * P].rearrange("p (b f) -> p b f", f=P)
                           ).then_inc(x_probT_ready, 1)
                j = step - 4
                if j >= 0 and j % QB == QB - 1:
                    h = CROSS[j][0]
                    for d in range(2):
                        act.wait_ge(x_heads_done, 2 * h + d + 1)
                        a.copy(o_high[:, 2 * h + d], aux[4 + d][:]).then_inc(operand_high, 1)

            for what, n, *span in CROSS_PLAN:
                if what == "query" and span[1] == KB:
                    high_next(CHUNK["qc"] // 2 + n // 2, n % 2)
                    if n == 0:
                        take_root(RT["out"], aux[0], D)
                elif what == "step":
                    cross_step(n)
            residual_gemm("oc", SQ["wo"], OP["wo"], "g_ffn", a_high)

            def ffn(name, dst, last_cols, rt, base_):
                def pair(m, n, first=False, cols=KB * P):
                    high_next(m, 0, cols)
                    if first:
                        take_root(rt, aux[0], D)
                    if name == "ffn":
                        act.wait_ge(gate_ready, n + 1)
                    else:
                        act.wait_ge(tile_out[0], TILE[name] // 2 + n + 1)
                    a.activation(work[:, 0], work[:, 0], ACT.Silu).then_inc(silu_ready, 1)
                    high_next(m, 1, cols)
                    act.wait_ge(hidden_ready, base_ + n + 1)
                    a.copy(dst[:, bass.ds(n, 1)], work[:, bass.ds(1, 1)]).then_inc(operand_high, 1)

                base = CHUNK[name] // 2
                pair(base, 0, first=True)
                with act.Fori(1, FB - 1) as i:
                    pair(base + i, i)
                pair(base + FB - 1, FB - 1, cols=last_cols)

            ffn("ffn", h_high, FH * P, RT["wo"], 0)
            def down_tile(m, t, s, n, next_cols):
                high(m + 1, 0, next_cols)
                high(m + 1, 1, next_cols)
                act.wait_ge(tile_out[s], t + 1)
                act.wait_ge(summed, SQ["down"] + 2 * n)
                a.activation(square[:], residual[:, bass.ds(n, 1)], ACT.Square).then_inc(squared, 1)
                a.activation(work[:, bass.ds(0, 1)], residual[:, bass.ds(n, 1)], ACT.Square,
                             scale=dcol("g_final", n)).then_inc(squared, 1)
                a.activation(a_high[:, bass.ds(n, 1)], residual[:, bass.ds(n, 1)], ACT.Copy,
                             scale=both_gains[:, bass.ds(n, 1)]).then_inc(operand_high, 1)

            with act.Fori(0, 3) as i:
                for s in range(2):
                    down_tile(CHUNK["down"] // 2 + 2 * i + s, TILE["down"] // 2 + i, s, 2 * i + s, FH * P)
            for s in range(2):
                down_tile(CHUNK["down"] // 2 + 6 + s, TILE["down"] // 2 + 3, s, 6 + s,
                          FH * P if s == 0 else KB * P)

            c0, t0 = CHUNK["in2"] // 2, TILE["in2"] // 2
            act.dma_start(lru_weights[:], blockdiag).then_inc(blockdiag_in, 16)
            high_next(c0, 0)
            take_root(RT["down"], aux[0], D)
            act.wait_ge(rescaled, 1)
            a.activation(tok_root[:, 0:QB], scaled_sum, ACT.Sqrt, scale=1.0 / D, bias=eps
                         ).then_inc(root_ready, 1)
            high_next(c0, 1)
            with act.Fori(1, 4) as i:
                for s in range(2):
                    high_next(c0 + i, s)
            for n in range(4):
                act.wait_ge(tile_out[n % 2], t0 + 2 + n // 2 + 1)
                a.activation(lru_gate[:, n], lru_gate[:, n], ACT.Gelu_apprx_tanh).then_inc(gelu_ready, 1)
            def squares(src, n, sq, count, sem_):
                act.wait_ge(sem_, count)
                act.wait_ge(summed, sq + n)
                a.activation(square[:], src[:, n], ACT.Square).then_inc(squared, 1)

            def high_parts(src, block0):
                for n in range(4):
                    act.wait_ge(y_scaled, block0 + n + 1)
                    a.copy(y_high[:, block0 + n], src[:, n]).then_inc(operand_high, 1)

            def stick_step(step):
                if step < len(STICK):
                    p, qb, sub = STICK[step]
                    w = (qb + 1) * P
                    act.wait_ge(sticks, step + 1)
                    if step >= 3:
                        act.wait_ge(takenT, step - 2)
                    a.activation(take[:, step % 3, 0:w], aux[sub][:, 0:w], ACT.Sigmoid,
                                 scale=HALF ** -0.5).then_inc(breaks, 1)
                    if step >= 2:
                        act.wait_ge(taken, step - 1)
                    a.activation(stay[:, step % 2, 0:w], aux[sub][:, 0:w], ACT.Sigmoid,
                                 scale=-HALF ** -0.5).then_inc(breaks, 1)
                j = step - 2
                if 0 <= j < len(STICK):
                    w = (STICK[j][1] + 1) * P
                    act.wait_ge(takenT, j + 1)
                    if j >= 2:
                        act.wait_ge(stick_heads, j - 1)
                    a.copy(takeT[:, j % 2, 0:w], aux[2 + j % 2][:, 0:w]).then_inc(takenT_ready, 1)

            for what, *n in REC_PLAN:
                j = n[0] if n else 0
                if what == "tile":
                    if n[2] == KB:
                        high_next(c0 + j // 2, j % 2)
                elif what == "gate":
                    r = n[1]
                    act.wait_ge(lgates_done, 2 * j + r + 1)
                    if r and j:
                        act.wait_ge(lru_done, j)
                    a.activation(gates[:, r], aux[5][:], ACT.Sigmoid, bias=col(("b_rg", "b_ig")[r], j)
                                 ).then_inc(lgates_ready, 1)
                    if r == 0:
                        act.wait_ge(lgates_ready, 2 * j + 1)
                        if j:
                            act.wait_ge(lru_done, j)
                        a.activation(half_tanh[:], gates[:, 0], ACT.Tanh, scale=decay[:, j:j + 1]
                                     ).then_inc(tanh_ready, 1)
                elif what == "turn":
                    act.wait_ge(vT2_done, j + 1)
                    act.wait_ge(v2_clear, 1)
                    blocks = aux[5][:].rearrange("p (b f) -> p b f", f=P)
                    for sub in range(2):
                        a.copy(v2[:, :, 2 * j + sub, sub * HALF:(sub + 1) * HALF],
                               blocks[:, :, sub * HALF:(sub + 1) * HALF]).then_inc(v2_out, 1)
                elif what == "late":
                    act.wait_ge(tanh_ready, j + 1)
                    a.activation(gate_root[:], half_tanh[:], ACT.Sqrt).then_inc(lroot_ready, 1)
                elif what == "square":
                    squares(lru_gate, j, SQ["ylru"], j + 1, lru_done)
                elif what == "step":
                    stick_step(j)
                elif what == "lru_sum":
                    take_root(RT["ylru"], aux[5], 4 * P)
                elif what == "lru_low":
                    high_parts(lru_gate, 0)
                elif what == "att_square":
                    squares(q2, j, SQ["yatt"], j + 1, att_out)
                elif what == "att_sum":
                    take_root(RT["yatt"], aux[5], 4 * P)
                elif what == "att_scale":
                    high_parts(q2, 4)
            residual_gemm("out2", SQ["out2"], OP["out2"], "g_ffn2", a_high)
            ffn("ffn2", h_high, FH * P, RT["out2"], FB)

            def back(n):
                act.wait_ge(outT_done, n + 1)
                a.copy(y_tok[:, :, n * P:(n + 1) * P],
                       aux[2 + n % 2][:].rearrange("p (b f) -> p b f", f=P)).then_inc(outT_out, 1)

            def last_tile(m, t, s, n, more=True):
                if more:
                    high(m + 1, 0, FH * P)
                if n:
                    back(n - 1)
                if more:
                    high(m + 1, 1, FH * P)
                act.wait_ge(tile_out[s], t + 1)
                act.wait_ge(summed, SQ["down2"] + n)
                a.activation(square[:], residual[:, bass.ds(n, 1)], ACT.Square).then_inc(squared, 1)
                if n >= 2:
                    act.wait_ge(outT_done, n - 1)
                a.activation(work[:, s], residual[:, bass.ds(n, 1)], ACT.Copy,
                             scale=dcol("g_final2", n)).then_inc(out_scaled, 1)

            for n in range(KB):
                last_tile(CHUNK["down2"] // 2 + n, TILE["down2"] // 2 + n // 2, n % 2, n, n < KB - 1)
            back(KB - 1)
            act.wait_ge(out_sums, 1)
            a.activation(tok_root[:, 0:QB], aux[0][:, 0:QB], ACT.Sqrt, scale=1.0 / D, bias=eps
                         ).then_inc(root_ready, 1)

        @block.vector
        def _(dve):
            v = nc.vector
            own = Steps(dve, dve_steps)

            dve.wait_ge(params_in, 16)
            dve.wait_ge(positions_in, 16)
            own.then(v.tensor_copy(cosine[:], sine[:].bitcast(I32)))
            own.then(v.tensor_scalar(sine[:], cosine[:], col("freq"), None, ALU.mult))
            own.then(v.tensor_scalar(cosine[:], sine[:], float(1 / (2 * np.pi)), ROUND, ALU.mult, ALU.add))
            own.then(v.tensor_scalar(cosine[:], cosine[:], -ROUND, None, ALU.add))
            for piece in TWO_PI:
                own.then(v.scalar_tensor_tensor(sine[:], cosine[:], -piece, sine[:], ALU.mult, ALU.add))
            v.tensor_scalar(sine[:], sine[:], 3.1415925, -3.1415925, ALU.min, ALU.max
                            ).then_inc(angle_ready, 1)
            dve.wait_ge(angle_ready, 1)
            v.scalar_tensor_tensor(cosine[:], sine[:], -1.0, sine[:], ALU.mult, ALU.max).then_inc(angle_ready, 1)
            v.scalar_tensor_tensor(sp[:, 0:4], col("lam", 0, 4), -1.0, col("lam", 0, 4), ALU.mult, ALU.max
                                   ).then_inc(angle_ready, 1)
            own.step(v.tensor_tensor(both_gains, col("g_final", 0, KB), col("g_mix2", 0, KB), ALU.mult))
            v.memset(v_pad[:], 0.0).then_inc(cleared, 1)

            def scale_rows(tt):
                dve.wait_ge(token_root, tt + 1)
                own.then(v.reciprocal(tok_factor[:, tt:tt + 1], tok_root[:, tt:tt + 1]))
                v.tensor_scalar(xn_tok[:, tt], x_tok[:, tt], tok_factor[:, tt:tt + 1], None, ALU.mult
                                ).then_inc(token_scaled, 1)

            for tt in range(QB):
                scale_rows(tt)
            for k in range(KB):
                dve.wait_ge(operand_high, OP["x"] + k + 1)
                v.scalar_tensor_tensor(a_low[:, k], aux[k % 6][:], col("g_mix", k),
                                       a_high[:, k].bitcast(F32), ALU.mult, ALU.subtract
                                       ).then_inc(operand_low, 1)
            dve.wait_ge(softplus_exp, 1)
            e, s1_, s2_, po = sp[:, 0:4], sp[:, 4:8], sp[:, 8:12], sp[:, 12:16]
            own.then(v.tensor_scalar(s1_, e, 2.0, None, ALU.add))
            own.then(v.reciprocal(s1_, s1_))
            own.then(v.tensor_tensor(s1_, s1_, e, ALU.mult))
            own.then(v.tensor_tensor(s2_, s1_, s1_, ALU.mult))
            own.then(v.tensor_scalar(po, s2_, 1.0 / 15, 1.0 / 13, ALU.mult, ALU.add))
            for n in (11, 9, 7, 5, 3, 1):
                own.then(v.tensor_tensor(po, po, s2_, ALU.mult))
                own.then(v.tensor_scalar(po, po, 1.0 / n, None, ALU.add))
            own.then(v.tensor_tensor(po, po, s1_, ALU.mult))
            own.then(v.tensor_scalar(s2_, col("lam", 0, 4), -4.0, 0.0, ALU.mult, ALU.max))
            own.then(v.scalar_tensor_tensor(decay, po, 8.0, s2_, ALU.mult, ALU.add))
            for tt in (4, 5):
                scale_rows(tt)
            dve.wait_ge(tables_ready, 1)

            def rope(n, t, rows, bank):
                dve.wait_ge(rotated, n + 1)
                own.step(v.tensor_tensor(t, t, cosine[0:rows], ALU.mult))
                own.then(v.tensor_tensor(turned[0:rows], bank[0:rows], sine[0:rows], ALU.mult))
                v.tensor_tensor(t, t, turned[0:rows], ALU.add).then_inc(roped, 1)
                dve.wait_ge(roped, n + 1)

            rope(0, kv[0:HALF], HALF, aux[2])
            rope(1, kiwi[0:HALF], HALF, aux[3])
            rope(2, qiT[:, 0], P, aux[2])
            rope(3, qiT[:, 1], P, aux[3])
            for k in range(KB):
                dve.wait_ge(operand_high, OP["mem"] + k + 1)
                v.scalar_tensor_tensor(m_low[:, k], aux[k % 2][:, 0:MB * P], col("g_mem", k),
                                       m_high[:, k].bitcast(F32), ALU.mult, ALU.subtract
                                       ).then_inc(operand_low, 1)
            dve.wait_ge(v_out, 3)
            for n, (qb, h) in enumerate(INDEX):
                dve.wait_ge(rel_ready, n + 1)
                w = (qb + 1) * P
                dst, src, weight = score[:, qb - 1, 0:w], rel[:, n % 2, 0:w], wi[:, qb, h:h + 1]
                if h == 0:
                    v.tensor_scalar(dst, src, weight, None, ALU.mult).then_inc(rel_used, 1)
                else:
                    v.scalar_tensor_tensor(dst, src, weight, dst, ALU.mult, ALU.add
                                           ).then_inc(rel_used, 1)
                dve.wait_ge(rel_used, n + 1)
            for qb in range(1, QB):
                w = (qb + 1) * P
                row = score[:, qb - 1, 0:w]
                diag = score[:, qb - 1, qb * P:w]
                own.then(v.tensor_tensor(diag, diag, causal[:], ALU.add))
                for _ in range(TOPK // 8):
                    own.then(v.max(best, row))
                    own.then(v.match_replace(out=row, in_to_replace=best, in_values=row,
                                             imm_value=CHOSEN))
                own.then(v.tensor_scalar(row, row, CHOSEN, NEG, ALU.not_equal, ALU.mult))
            for n in range(4):
                rope(4 + n, qT[:, n], P, aux[n])
            own.then(v.memset(glu[:, :, 0:TAPS - 1], 0.0))
            for n in range(4):
                dve.wait_ge(tile_out[1], TILE["in"] // 2 + 4 + n + 1)
                dve.wait_ge(tile_out[0], TILE["in"] // 2 + 4 + n + 1)
                body = glu[:, n, TAPS - 1:TAPS - 1 + T]
                own.step(v.tensor_tensor(body, body, gate[:, n], ALU.mult))
            own.settle()

            def conv_tap(i):
                n, k = CONV[i]
                src, weight = glu[:, n, k:k + T], col("conv_w", n * TAPS + k)
                if k == 0:
                    ins = v.tensor_scalar(conv[:, n], src, weight, col("conv_b", n), ALU.mult, ALU.add)
                else:
                    dve.wait_ge(conv_steps, i - 1)
                    ins = v.scalar_tensor_tensor(conv[:, n], src, weight, conv[:, n], ALU.mult, ALU.add)
                ins.then_inc(conv_steps, 1)

            for i in range(EARLY_TAPS):
                conv_tap(i)

            for step in range(DSA_STEPS):
                if step < len(DSA):
                    qb, h = DSA[step]
                    w = (qb + 1) * P
                    dve.wait_ge(logits, step + 1)
                    if step >= 2:
                        dve.wait_ge(prob_raw, step - 1)
                    mask = causal[:] if qb == 0 else score[:, qb - 1, 0:w]
                    v.tensor_tensor_reduce(out=masked[:, step % 2, 0:w], in0=aux[h % 2][:, 0:w], in1=mask,
                                           scale=-HALF ** -0.5, scalar=3e38, op0=ALU.add, op1=ALU.min,
                                           accum_out=least[:, step % 2:step % 2 + 1]
                                           ).then_inc(logits_masked, 1)
                taps = [min(EARLY_TAPS + i * (len(CONV) - EARLY_TAPS) // CONV_STEPS, len(CONV))
                        for i in (step, step + 1)]
                taps = range(*taps)
                j = step - 1
                if 0 <= j < len(DSA):
                    dve.wait_ge(prob_raw, j + 1)
                    v.reciprocal(inverse[:, j % 2:j % 2 + 1], total[:, j % 2:j % 2 + 1]
                                 ).then_inc(prob_inverse, 1)
                for i in taps:
                    conv_tap(i)
                j = step - 4
                if j >= 0 and j % 2:
                    qb, h = DSA[j]
                    dve.wait_ge(operand_high, OP["a"] + j // 2 + 1)
                    span = slice(qb * P, (qb + 1) * P)
                    v.tensor_tensor(a_low[:, h // 2, span], aux[4 + j // 2 % 2][:, 0:P],
                                    a_high[:, h // 2, span].bitcast(F32), ALU.subtract
                                    ).then_inc(operand_low, 1)
                if step == LN_MEAN:
                    dve.wait_ge(mean_ready, 1)
                    for n in range(4):
                        v.scalar_tensor_tensor(conv[:, n], acc[:, 0], -1.0 / (4 * P), conv[:, n], ALU.mult,
                                               ALU.add).then_inc(centred, 1)
                if step == LN_VAR:
                    dve.wait_ge(ln_root, 1)
                    v.reciprocal(tok_factor[:, 0:QB], tok_root[:, 0:QB]).then_inc(ln_factor, 1)
                if step == LN_OUT:
                    dve.wait_ge(centred, 4)
                    dve.wait_ge(ln_spread, 1)
                    for n in range(4):
                        v.tensor_tensor(conv[:, n], conv[:, n], acc[:, 1], ALU.mult).then_inc(ln_scaled, 1)
                if step == LN_LOW:
                    for n in range(4):
                        dve.wait_ge(b_high_ready, n + 1)
                        v.tensor_tensor(a_low[:, 4 + n], conv[:, n], a_high[:, 4 + n].bitcast(F32),
                                        ALU.subtract).then_inc(b_low_ready, 1)

            def token_factor(rt):
                dve.wait_ge(root_ready, rt + 1)
                v.reciprocal(tok_factor[:, 0:QB], tok_root[:, 0:QB]).then_inc(factor_ready, 1)

            def new_factor(rt):
                token_factor(rt)
                dve.wait_ge(factor_spread, rt + 1)
                own.then(v.tensor_copy(row_factor[:], aux[0][:]))

            def residual_tile(c, t, s, n):
                dve.wait_ge(chunk_done, c)
                v.tensor_tensor(residual[:, bass.ds(n, 1)].rearrange("p a n -> p (a n)"), acc[:, s],
                                residual[:, bass.ds(n, 1)].rearrange("p a n -> p (a n)"), ALU.add
                                ).then_inc(tile_out[s], 1)
                dve.wait_ge(tile_out[s], t + 1)

            def at(x, n):
                return x[:, bass.ds(n, 1)].rearrange("p a n -> p (a n)")

            def add_squares(count, total_, squares):
                dve.wait_ge(squared, count)
                v.tensor_tensor(total_, total_, squares, ALU.add).then_inc(summed, 1)

            def low_part(dst, src_high, n, gain, count):
                dve.wait_ge(operand_high, count)
                v.scalar_tensor_tensor(at(dst, n), at(residual, n), gain, at(src_high, n).bitcast(F32),
                                       ALU.mult, ALU.subtract).then_inc(operand_low, 1)

            def residual_gemm(name, sq, op, gain, dst_high, dst_low):
                own.then(v.memset(square_sum[:], 0.0))

                def body(i):
                    for s in range(2):
                        n = 2 * i + s
                        residual_tile(CHUNK[name] + n + 1, TILE[name] // 2 + i, s, n)
                        add_squares(sq + n + 1, square_sum[:], square[:])
                        low_part(dst_low, dst_high, n, dcol(gain, n), op + n + 1)
                        dve.wait_ge(summed, sq + n + 1)
                own.run(0, KB // 2, 0, body)

            residual_gemm("out", SQ["out"], OP["out"], "g_cross", b_high, b_low)
            own.then(v.memset(zeros[:], 0.0))
            new_factor(RT["out"])

            def cross_step(step):
                if step < len(CROSS):
                    dve.wait_ge(x_logits, step + 1)
                    if step >= 2:
                        dve.wait_ge(x_prob_raw, step - 1)
                    v.tensor_tensor_reduce(out=xmasked[:, step % 2], in0=aux[step % 2][:, 0:MB * P],
                                           in1=zeros[:], scale=-(X_KB * P) ** -0.5, scalar=3e38,
                                           op0=ALU.add, op1=ALU.min,
                                           accum_out=least[:, step % 2:step % 2 + 1]).then_inc(x_masked, 1)
                j = step - 1
                if 0 <= j < len(CROSS):
                    dve.wait_ge(x_prob_raw, j + 1)
                    own.then(v.reciprocal(inverse[:, j % 2:j % 2 + 1], total[:, j % 2:j % 2 + 1]))
                    v.tensor_scalar(xprob[:, j % 3], xprob[:, j % 3], inverse[:, j % 2:j % 2 + 1], None,
                                    ALU.mult).then_inc(x_prob_ready, 1)
                j = step - 4
                if j >= 0 and j % QB == QB - 1:
                    for d in range(2):
                        n = 2 * CROSS[j][0] + d
                        dve.wait_ge(operand_high, OP["oc"] + n + 1)
                        v.tensor_tensor(o_low[:, n], aux[4 + d][:], o_high[:, n].bitcast(F32),
                                        ALU.subtract).then_inc(operand_low, 1)

            for what, n, *span in CROSS_PLAN:
                if what == "query" and span[1] == KB:
                    dve.wait_ge(chunk_done, CHUNK["qc"] + n + 1)
                    v.tensor_tensor(qcT[:, n], acc[:, n % 2], row_factor[:], ALU.mult
                                    ).then_inc(tile_out[n % 2], 1)
                elif what == "step":
                    cross_step(n)
            residual_gemm("oc", SQ["wo"], OP["wo"], "g_ffn", a_high, a_low)

            def ffn(name, dst_high, dst_low, op, base, taps):
                def pair(i):
                    t = TILE[name] // 2 + i
                    dve.wait_ge(chunk_done, CHUNK[name] + 2 * i + 1)
                    dst = gated[:, TAPS_FFN - 1:TAPS_FFN - 1 + T] if taps else work[:, 0]
                    ins = v.tensor_tensor(dst, acc[:, 0], row_factor[:], ALU.mult)
                    ins.then_inc(tile_out[0], 1)
                    if taps:
                        dve.wait_ge(tile_out[0], t + 1)
                        c = i * TAPS_FFN
                        own.then(v.tensor_scalar(work[:, 0], gated[:, 2:2 + T], dcol("fconv_w", c + 2),
                                                 dcol("fconv_b", i), ALU.mult, ALU.add))
                        own.then(v.scalar_tensor_tensor(work[:, 0], gated[:, 1:1 + T], dcol("fconv_w", c + 1),
                                                        work[:, 0], ALU.mult, ALU.add))
                        v.scalar_tensor_tensor(work[:, 0], gated[:, 0:T], dcol("fconv_w", c), work[:, 0],
                                               ALU.mult, ALU.add).then_inc(gate_ready, 1)
                    dve.wait_ge(chunk_done, CHUNK[name] + 2 * i + 2)
                    v.tensor_tensor(work[:, 1], acc[:, 1], row_factor[:], ALU.mult).then_inc(tile_out[1], 1)
                    dve.wait_ge(tile_out[1], t + 1)
                    dve.wait_ge(silu_ready, base + i + 1)
                    v.tensor_tensor(work[:, 1], work[:, 1], work[:, 0], ALU.mult).then_inc(hidden_ready, 1)
                    dve.wait_ge(hidden_ready, base + i + 1)
                    dve.wait_ge(operand_high, op + i + 1)
                    v.tensor_tensor(at(dst_low, i), work[:, 1], at(dst_high, i).bitcast(F32), ALU.subtract
                                    ).then_inc(operand_low, 1)
                    dve.wait_ge(operand_low, op + i + 1)
                own.run(0, FB, 2 if taps else 0, pair)

            own.then(v.memset(gated[:, 0:TAPS_FFN - 1], 0.0))
            new_factor(RT["wo"])
            ffn("ffn", h_high, h_low, OP["h"], 0, True)

            own.step(v.memset(square_sum[:], 0.0))
            own.then(v.memset(work[:, 1], 0.0))

            def down(i):
                for s in range(2):
                    n = 2 * i + s
                    residual_tile(CHUNK["down"] + 2 * n + 2, TILE["down"] // 2 + i, s, n)
                    add_squares(SQ["down"] + 2 * n + 1, square_sum[:], square[:])
                    add_squares(SQ["down"] + 2 * n + 2, work[:, 1], work[:, 0])
                    low_part(a_low, a_high, n, both_gains[:, bass.ds(n, 1)], OP["down"] + n + 1)
                    dve.wait_ge(summed, SQ["down"] + 2 * n + 2)
            own.run(0, KB // 2, 0, down)

            dve.wait_ge(root_ready, RT["down"] + 1)
            v.reciprocal(first_factor, tok_root[:, 0:QB]).then_inc(factor_ready, 1)
            dve.wait_ge(factor_ready, RT["down"] + 1)
            dve.wait_ge(sums_ready, RT["down"] + 2)
            own.then(v.tensor_tensor(scaled_sum, aux[1][:, 0:QB], first_factor, ALU.mult))
            v.tensor_tensor(scaled_sum, scaled_sum, first_factor, ALU.mult).then_inc(rescaled, 1)
            dve.wait_ge(root_ready, RT["down"] + 2)
            own.then(v.reciprocal(tok_factor[:, 0:QB], tok_root[:, 0:QB]))
            v.tensor_tensor(tok_factor[:, 0:QB], tok_factor[:, 0:QB], first_factor, ALU.mult
                            ).then_inc(factor_ready, 1)
            dve.wait_ge(factor_spread, RT["down"] + 2)
            own.step(v.tensor_copy(row_factor[:], aux[0][:]))
            own.then(v.tensor_copy(square_sum[:], aux[1][:]))

            own.step(v.memset(lru_in[:, :, 0:TAPS_LRU - 1], 0.0))

            def out_of(n, dst):
                dve.wait_ge(chunk_done, CHUNK["in2"] + n + 1)
                v.tensor_tensor(dst, acc[:, n % 2], row_factor[:], ALU.mult).then_inc(tile_out[n % 2], 1)
                dve.wait_ge(tile_out[n % 2], TILE["in2"] // 2 + n // 2 + 1)

            for n in range(4):
                out_of(n, lru_in[:, n, TAPS_LRU - 1:TAPS_LRU - 1 + T])
                for k in (2 * n, 2 * n + 1):
                    own.step(v.scalar_tensor_tensor(residual[:, k], residual[:, k], col("g_final", k),
                                                    square_sum[:], ALU.mult, ALU.mult))
            for n in range(4):
                out_of(4 + n, lru_gate[:, n])
            v.memset(v2[:], 0.0).then_inc(v2_clear, 1)
            own.then(v.memset(square_sum[:], 0.0))
            dve.wait_ge(blockdiag_in, 16)
            def scale_parts(rt, src, gain):
                dve.wait_ge(factor_spread, rt + 1)
                for n in range(4):
                    v.scalar_tensor_tensor(src[:, n], src[:, n], col(gain, n), aux[5][:], ALU.mult, ALU.mult
                                           ).then_inc(y_scaled, 1)

            def low_parts(src, op, block0):
                for n in range(4):
                    dve.wait_ge(operand_high, op + n + 1)
                    v.tensor_tensor(y_low[:, block0 + n], src[:, n], y_high[:, block0 + n].bitcast(F32),
                                    ALU.subtract).then_inc(operand_low, 1)

            def stick_step(step):
                if step % 8 == 3 and step > 3:
                    p = step // 8 - 1
                    dve.wait_ge(stick_heads, 8 * (p + 1))
                    v.tensor_copy(q2[:, p], aux[4][:]).then_inc(att_out, 1)
                if step >= len(STICK):
                    return
                p, qb, sub = STICK[step]
                w = (qb + 1) * P
                i, to = step % 2, step % 3
                dve.wait_ge(breaks, 2 * step + 2)
                own.step(v.tensor_tensor(stay[:, i, w - P:w], stay[:, i, w - P:w], notbefore[:], ALU.max))
                own.then(v.tensor_tensor(take[:, to, w - P:w], take[:, to, w - P:w], before[:], ALU.mult))
                back = stay[:, i, 0:w][:, ::-1]
                own.then(v.tensor_tensor_scan(left[:, 0:w][:, ::-1], back, back, 1.0, ALU.mult, ALU.min))
                v.tensor_tensor(take[:, to, 0:w - 1], take[:, to, 0:w - 1], left[:, 1:w], ALU.mult
                                ).then_inc(taken, 1)

            for what, *n in REC_PLAN:
                j = n[0] if n else 0
                if what == "conv":
                    if j:
                        dve.wait_ge(lgates_done, 2 * j)
                    for k in range(TAPS_LRU - 1, -1, -1):
                        src, weight = lru_in[:, j, k:k + T], col("lconv_w", j * TAPS_LRU + k)
                        if k == TAPS_LRU - 1:
                            own.then(v.tensor_scalar(xc[:], src, weight, col("lconv_b", j), ALU.mult,
                                                     ALU.add))
                        elif k:
                            own.then(v.scalar_tensor_tensor(xc[:], src, weight, xc[:], ALU.mult, ALU.add))
                        else:
                            v.scalar_tensor_tensor(xc[:], src, weight, xc[:], ALU.mult, ALU.add
                                                   ).then_inc(lconv_ready, 1)
                elif what == "tile" and n[2] == KB:
                    p, kind = (j - 8) // 3, (j - 8) % 3
                    if kind == 0 and p:
                        dve.wait_ge(vT2_done, p)
                    out_of(j, (vT2[:], q2[:, p], k2[:, p])[kind])
                elif what == "gate" and n[1] == 1:
                    dve.wait_ge(tanh_ready, j + 1)
                    own.then(v.tensor_scalar(inverse_sum[:], half_tanh[:], 1.0, None, ALU.add))
                    own.then(v.reciprocal(inverse_sum[:], inverse_sum[:]))
                    dve.wait_ge(lgates_ready, 2 * j + 2)
                    own.then(v.tensor_tensor(gates[:, 1], gates[:, 1], xc[:], ALU.mult))
                elif what == "late":
                    dve.wait_ge(lroot_ready, j + 1)
                    own.then(v.scalar_tensor_tensor(gate_root[:], gate_root[:], 2.0, inverse_sum[:],
                                                    ALU.mult, ALU.mult))
                    own.step(v.tensor_tensor(gate_root[:], gate_root[:], gates[:, 1], ALU.mult))
                    own.then(v.tensor_scalar(inverse_sum[:], inverse_sum[:], 2.0, -1.0, ALU.mult, ALU.add))
                    own.then(v.tensor_tensor_scan(half_tanh[:], inverse_sum[:], gate_root[:], 0.0,
                                                  ALU.mult, ALU.add))
                    dve.wait_ge(gelu_ready, j + 1)
                    v.tensor_tensor(lru_gate[:, j], lru_gate[:, j], half_tanh[:], ALU.mult
                                    ).then_inc(lru_done, 1)
                elif what == "square":
                    add_squares(SQ["ylru"] + j + 1, square_sum[:], square[:])
                    dve.wait_ge(summed, SQ["ylru"] + j + 1)
                elif what == "step":
                    stick_step(j)
                elif what == "lru_spread":
                    token_factor(RT["ylru"])
                elif what == "att_spread":
                    token_factor(RT["yatt"])
                elif what == "lru_scale":
                    scale_parts(RT["ylru"], lru_gate, "g_lru")
                    own.then(v.memset(square_sum[:], 0.0))
                elif what == "lru_low":
                    low_parts(lru_gate, OP["ylru"], 0)
                elif what == "att_square":
                    add_squares(SQ["yatt"] + j + 1, square_sum[:], square[:])
                    dve.wait_ge(summed, SQ["yatt"] + j + 1)
                elif what == "att_scale":
                    scale_parts(RT["yatt"], q2, "g_att")
                    low_parts(q2, OP["yatt"], 4)
            residual_gemm("out2", SQ["out2"], OP["out2"], "g_ffn2", a_high, a_low)
            new_factor(RT["out2"])
            ffn("ffn2", h_high, h_low, OP["h2"], FB, False)

            own.then(v.memset(square_sum[:], 0.0))
            for n in range(KB):
                residual_tile(CHUNK["down2"] + 2 * n + 2, TILE["down2"] // 2 + n // 2, n % 2, n)
                add_squares(SQ["down2"] + n + 1, square_sum[:], square[:])
                dve.wait_ge(summed, SQ["down2"] + n + 1)
            dve.wait_ge(root_ready, RT["down2"] + 1)
            own.then(v.reciprocal(tok_factor[:, 0:QB], tok_root[:, 0:QB]))
            dve.wait_ge(outT_out, KB)
            for tt in range(QB):
                v.tensor_scalar(y_tok[:, tt], y_tok[:, tt], tok_factor[:, tt:tt + 1], None, ALU.mult
                                ).then_inc(out_ready, 1)

        @block.tensor
        def _(pe):
            t_ = nc.tensor
            A = (a_high, a_low)
            B = (b_high, b_low)
            M = (m_high, m_low)
            O = (o_high, o_low)
            Y = (y_high, y_low)
            H = (h_high, h_low)

            def chunk(m, s, blocks, bank, operand, k0=0, start=True, stop=True, ready=None, cols=T,
                      before_block=None, first=0):
                pe.wait_ge(weight_low, 2 * m + s + 1)
                high, low = operand
                whole = FH if blocks == FH else KB
                for k in range(first, blocks):
                    if before_block:
                        before_block(k)
                    if ready is not None:
                        pe.wait_ge(operand_low, ready + k + 1)
                    wide = slice(k * P, (k + 1) * P)
                    passes = ((weights_high, high), (weights_high, low), (weights_low, high))
                    for n, (w, x_) in enumerate(passes):
                        last = t_.matmul(acc[:, bank, 0:cols], w[:, s, wide], x_[:, k0 + k, 0:cols],
                                         start=start and k == 0 and n == 0,
                                         stop=stop and k == whole - 1 and n == 2)
                if blocks == whole:
                    last.then_inc(chunk_done, 1)

            def free(bank, t):
                pe.wait_ge(tile_out[bank], t)

            def gemm_pair(name, i, operand, cols=T):
                m, t = CHUNK[name] // 2 + i, TILE[name] // 2 + i
                for s in range(2):
                    free(s, t)
                    chunk(m, s, KB, s, operand, cols=cols)

            def gemm(name, pairs, operand, ready=None, sums=None, spreads=None, cols=T):
                m, t = CHUNK[name] // 2, TILE[name] // 2
                free(0, t)
                chunk(m, 0, KB, 0, operand, ready=ready, cols=cols)
                if sums:
                    sums()
                free(1, t)
                chunk(m, 1, SPREAD, 1, operand, cols=cols)
                if spreads:
                    spreads()
                chunk(m, 1, KB, 1, operand, cols=cols, first=SPREAD)
                with pe.Fori(1, pairs) as i:
                    gemm_pair(name, i, operand, cols=cols)

            def gemm_rest(name, pairs, operand):
                with pe.Fori(1, pairs) as i:
                    gemm_pair(name, i, operand)

            def first_tile(name, n, operand, ready, k, end):
                if k == 0:
                    free(n, TILE[name] // 2)
                chunk(CHUNK[name] // 2, n, end, n, operand, ready=ready, first=k)

            def sum_features(count, src, bank):
                pe.wait_ge(summed, count)
                for tt in range(QB):
                    last = t_.matmul(bank[:, tt:tt + 1], src[:, tt * P:(tt + 1) * P],
                                     ones[:, 0:1], start=True, stop=True)
                last.then_inc(sums_ready, 1)

            def spread(factor, bank):
                for tt in range(QB):
                    last = t_.matmul(bank[:, tt * P:(tt + 1) * P],
                                     factor[:, tt:tt + 1].broadcast_to([P, P]), ident[:],
                                     start=True, stop=True)
                return last

            def spread_factor(rt, bank):
                pe.wait_ge(factor_ready, rt + 1)
                spread(tok_factor, bank).then_inc(factor_spread, 1)

            pe.wait_ge(consts_ready, NCONST)
            pe.wait_ge(token_scaled, QB)

            def turn_x(k):
                if k >= 6:
                    pe.wait_ge(operand_low, k - 5)
                for tt in range(QB):
                    last = t_.transpose(aux[k % 6][:, tt * P:(tt + 1) * P],
                                        xn_tok[:, tt, k * P:(k + 1) * P], ident[:])
                last.then_inc(xnT_done, 1)

            for k in range(3):
                turn_x(k)

            def in_tile(n):
                m, s = n // 2, n % 2
                if m:
                    free(s, m)
                chunk(m, s, KB, s, A, ready=0 if n == 0 else None,
                      before_block=(lambda k: turn_x(k + 3) if k + 3 < KB else None) if n == 0 else None)

            def rotation(src, rows, bank):
                t_.matmul(bank[0:rows], rotate[0:rows, 0:rows], src, start=True, stop=True
                          ).then_inc(rotated, 1)

            in_tile(0)
            in_tile(1)
            pe.wait_ge(tile_out[0], 1)
            rotation(kv[0:HALF], HALF, aux[2])
            in_tile(2)
            pe.wait_ge(tile_out[1], 1)
            rotation(kiwi[0:HALF], HALF, aux[3])
            pe.wait_ge(roped, 1)
            t_.matmul(aux[4][:], twice[0:HALF], kv[0:HALF], start=True, stop=True).then_inc(doubled, 1)
            in_tile(3)
            pe.wait_ge(tile_out[0], 2)
            rotation(qiT[:, 0], P, aux[2])
            pe.wait_ge(roped, 2)
            t_.matmul(aux[5][:], twice[0:HALF], kiwi[0:HALF], start=True, stop=True).then_inc(doubled, 1)
            pe.wait_ge(tile_out[1], 2)
            rotation(qiT[:, 1], P, aux[3])
            for k in range(KB):
                pe.wait_ge(operand_low, KB) if k < 2 else pe.wait_ge(residual_in, k - 1)
                for tt in range(QB):
                    last = t_.transpose(aux[k % 2][:, tt * P:(tt + 1) * P],
                                        x_tok[:, tt, k * P:(k + 1) * P], ident[:])
                last.then_inc(xT_done, 1)
            pe.wait_ge(token_scaled, 6)
            for k in range(KB):
                if k < 2:
                    pe.wait_ge(residual_in, KB - 1 + k)
                else:
                    pe.wait_ge(operand_low, OP["mem"] + k - 1)
                for tt in range(MB):
                    last = t_.transpose(aux[k % 2][:, tt * P:(tt + 1) * P],
                                        xn_tok[:, QB + tt, k * P:(k + 1) * P], ident[:])
                last.then_inc(mT_done, 1)
            for n, src in enumerate((kv, kiwi)):
                pe.wait_ge(doubled_out, n + 1)
                for b in range(QB):
                    last = t_.transpose(aux[4 + n][:, b * P:(b + 1) * P], src[:, b * P:(b + 1) * P],
                                        ident[:])
                last.then_inc(vwi_done, 1)
            pe.wait_ge(roped, 4)
            pe.wait_ge(v_out, 3)
            for n, (qb, h) in enumerate(INDEX):
                if n >= 4:
                    pe.wait_ge(rel_ready, n - 3)
                w, rows = (qb + 1) * P, slice(h % 2 * HALF, h % 2 * HALF + HALF)
                t_.matmul(aux[2 + h % 2 + 2 * (n // 2 % 2)][:, 0:w],
                          qiT[rows, h // 2, qb * P:(qb + 1) * P], kiT[rows, 0:w], start=True, stop=True
                          ).then_inc(index_logits, 1)
            in_tile(4)
            for n in range(4):
                in_tile(5 + n)
                pe.wait_ge(tile_out[n % 2], 3 + n // 2)
                if n == 0:
                    pe.wait_ge(operand_low, OP["mem"] + KB)
                if n == 2:
                    pe.wait_ge(rel_ready, len(INDEX))
                rotation(qT[:, n], P, aux[n])
            for n in range(9, 16):
                in_tile(n)
            with pe.Fori(0, KB // 2) as i:
                gemm_pair("kc", i, M, cols=MB * P)

            def turn_values(n):
                pe.wait_ge(tile_out[n % 2], TILE["vc"] // 2 + n // 2 + 1)
                for b in range(MB):
                    last = t_.transpose(acc[:, n % 2, (MB + b) * P:(MB + b + 1) * P],
                                        vcT[:, n % 2, b * P:(b + 1) * P], ident[:])
                last.then_inc(vcT_done, 1)

            pe.wait_ge(roped, 8)
            for step in range(DSA_STEPS):
                if step < len(DSA):
                    qb, h = DSA[step]
                    if step >= 2:
                        pe.wait_ge(logits_masked, step - 1)
                    w, rows = (qb + 1) * P, slice(h % 2 * HALF, h % 2 * HALF + HALF)
                    t_.matmul(aux[h % 2][:, 0:w], qT[rows, h // 2, qb * P:(qb + 1) * P], kT[rows, 0:w],
                              start=True, stop=True).then_inc(logits, 1)
                if step < KB:
                    n = step
                    m, s = CHUNK["vc"] // 2 + n // 2, n % 2
                    free(s, TILE["vc"] // 2 + n // 2)
                    if n >= 2:
                        pe.wait_ge(vc_out, n - 1)
                    chunk(m, s, KB, s, M, cols=MB * P)
                if 1 <= step <= KB:
                    turn_values(step - 1)
                j = step - 2
                if 0 <= j < len(DSA):
                    pe.wait_ge(prob_ready, j + 1)
                    if j >= 2:
                        pe.wait_ge(probT_ready, j - 1)
                    for b in range(DSA[j][0] + 1):
                        last = t_.transpose(aux[2 + j % 2][:, b * P:(b + 1) * P],
                                            prob[:, j % 3, b * P:(b + 1) * P], ident[:])
                    last.then_inc(probT_done, 1)
                j = step - 3
                if 0 <= j < len(DSA):
                    qb, h = DSA[j]
                    g = j // 2
                    pe.wait_ge(probT_ready, j + 1)
                    if g >= 2 and h % 2 == 0:
                        pe.wait_ge(operand_low, OP["a"] + g - 1)
                    for b in range(qb + 1):
                        last = t_.matmul(aux[4 + g % 2][:, 0:P], v_pad[:, b, h % 2],
                                         probT[:, j % 2, b * P:(b + 1) * P],
                                         start=h % 2 == 0 and b == 0, stop=h % 2 == 1 and b == qb)
                    last.then_inc(heads_done, 1)
                if step == LN_MEAN:
                    pe.wait_ge(vc_out, KB)
                    pe.wait_ge(conv_steps, len(CONV))
                    for n in range(4):
                        last = t_.matmul(acc[:, 0], ones[:], conv[:, n], start=n == 0, stop=n == 3)
                    last.then_inc(mean_ready, 1)
                if step == LN_VAR:
                    pe.wait_ge(tile_out[1], TILE["out"] // 2)
                    pe.wait_ge(centred_squared, 4)
                    for tt in range(QB):
                        for n in range(4):
                            last = t_.matmul(acc[:, 1, tt:tt + 1], gate[:, n, tt * P:(tt + 1) * P],
                                             ones[:, 0:1], start=n == 0, stop=n == 3)
                    last.then_inc(variance_ready, 1)
                if step == LN_VAR + 1:
                    pe.wait_ge(ln_factor, 1)
                    spread(tok_factor, acc[:, 1]).then_inc(ln_spread, 1)

            pe.wait_ge(b_low_ready, 4)
            pe.wait_ge(ln_scaled, 4)
            pe.wait_ge(operand_low, OP["out"])
            gemm("out", KB // 2, A)
            def cross_step(step):
                if step < len(CROSS):
                    h, qb = CROSS[step]
                    if qb == 0:
                        for s in range(2):
                            pe.wait_ge(tile_out[s], TILE["qc"] // 2 + h + 1)
                    if step >= 2:
                        pe.wait_ge(x_masked, step - 1)
                    for c in range(X_KB):
                        last = t_.matmul(aux[step % 2][:, 0:MB * P],
                                         qcT[:, X_KB * h + c, qb * P:(qb + 1) * P], kcT[:, X_KB * h + c],
                                         start=c == 0, stop=c == X_KB - 1)
                    last.then_inc(x_logits, 1)
                j = step - 2
                if 0 <= j < len(CROSS):
                    pe.wait_ge(x_prob_ready, j + 1)
                    if j >= 2:
                        pe.wait_ge(x_probT_ready, j - 1)
                    for b in range(MB):
                        last = t_.transpose(aux[2 + j % 2][:, b * P:(b + 1) * P],
                                            xprob[:, j % 3, b * P:(b + 1) * P], ident[:])
                    last.then_inc(x_probT_done, 1)
                j = step - 3
                if 0 <= j < len(CROSS) and j % QB == QB - 1:
                    h = CROSS[j][0]
                    pe.wait_ge(x_probT_ready, j + 1)
                    for d in range(2):
                        if h:
                            pe.wait_ge(operand_low, OP["oc"] + 2 * (h - 1) + d + 1)
                        col0 = h * X_KB * P + d * P
                        for b in range(MB):
                            last = t_.matmul(aux[4 + d][:], vc[:, b, col0:col0 + P], xprobT[:, h % 2, b],
                                             start=b == 0, stop=b == MB - 1)
                        last.then_inc(x_heads_done, 1)

            for what, n, *span in CROSS_PLAN:
                if what == "query":
                    if span[0] == 0:
                        free(n % 2, TILE["qc"] // 2 + n // 2)
                    chunk(CHUNK["qc"] // 2 + n // 2, n % 2, span[1], n % 2, B,
                          ready=OP["out"] if n == 0 else None, first=span[0])
                    if n == 0:
                        sum_features(SQ["out"] + KB, square_sum[:], aux[0])
                elif what == "factor":
                    spread_factor(RT["out"], aux[0])
                elif what == "step":
                    cross_step(n)
                else:
                    first_tile("oc", n, O, OP["oc"], *span)
            gemm_rest("oc", KB // 2, O)
            gemm("ffn", FB, A, OP["wo"],
                 sums=lambda: sum_features(SQ["wo"] + KB, square_sum[:], aux[0]),
                 spreads=lambda: spread_factor(RT["wo"], aux[0]))

            def down(name, n, t, s, ready=None, between=None):
                m = CHUNK[name] // 2 + n
                free(s, t)
                for half in range(2):
                    chunk(m, half, FH, s, H, k0=half * FH, start=half == 0, stop=half == 1,
                          ready=None if ready is None else ready + half * FH)
                    if between and half == 0:
                        between()

            def down_gemm(name, ready, after=None):
                for s in range(2):
                    down(name, s, TILE[name] // 2, s, ready=ready if s == 0 else None)
                with pe.Fori(1, KB // 2) as i:
                    for s in range(2):
                        down(name, 2 * i + s, TILE[name] // 2 + i, s)

            down_gemm("down", OP["h"])

            def two_sums():
                sum_features(SQ["down"] + 2 * KB, square_sum[:], aux[0])
                sum_features(SQ["down"] + 2 * KB, work[:, 1], aux[1])

            def two_factors():
                pe.wait_ge(factor_ready, RT["down"] + 2)
                spread(first_factor, aux[1]).then_inc(factor_spread, 1)
                spread(tok_factor, aux[0]).then_inc(factor_spread, 1)

            gemm("in2", 4, A, OP["down"], sums=two_sums, spreads=two_factors)

            def in2_tile(n, k, end):
                m, s = CHUNK["in2"] // 2 + n // 2, n % 2
                if k == 0:
                    free(s, TILE["in2"] // 2 + n // 2)
                chunk(m, s, end, s, A, first=k)

            pe.wait_ge(blockdiag_in, 16)
            def stick_step(step):
                if step < len(STICK):
                    p, qb, sub = STICK[step]
                    if qb == 0 and sub == 0:
                        pe.wait_ge(v2_out, 2 * (p + 1))
                        for n in (9 + 3 * p, 10 + 3 * p):
                            pe.wait_ge(tile_out[n % 2], TILE["in2"] // 2 + n // 2 + 1)
                    if step >= 2:
                        pe.wait_ge(breaks, 2 * (step - 1))
                    w, rows = (qb + 1) * P, slice(sub * HALF, (sub + 1) * HALF)
                    t_.matmul(aux[sub][:, 0:w], q2[rows, p, qb * P:(qb + 1) * P], k2[rows, p, 0:w],
                              start=True, stop=True).then_inc(sticks, 1)
                j = step - 2
                if 0 <= j < len(STICK):
                    pe.wait_ge(taken, j + 1)
                    if j >= 2:
                        pe.wait_ge(takenT_ready, j - 1)
                    for b in range(STICK[j][1] + 1):
                        last = t_.transpose(aux[2 + j % 2][:, b * P:(b + 1) * P],
                                            take[:, j % 3, b * P:(b + 1) * P], ident[:])
                    last.then_inc(takenT, 1)
                j = step - 3
                if 0 <= j < len(STICK):
                    p, qb, sub = STICK[j]
                    pe.wait_ge(takenT_ready, j + 1)
                    if p and qb == 0 and sub == 0:
                        pe.wait_ge(att_out, p)
                    for b in range(qb + 1):
                        last = t_.matmul(aux[4][:, qb * P:(qb + 1) * P], v2[:, b, 2 * p + sub],
                                         takeT[:, j % 2, b * P:(b + 1) * P],
                                         start=sub == 0 and b == 0, stop=sub == 1 and b == qb)
                    last.then_inc(stick_heads, 1)

            for what, *n in REC_PLAN:
                j = n[0] if n else 0
                if what == "tile":
                    in2_tile(*n)
                elif what == "gate":
                    r = n[1]
                    pe.wait_ge(lconv_ready, j + 1)
                    if r:
                        pe.wait_ge(lgates_ready, 2 * j + 1)
                    elif j:
                        pe.wait_ge(v2_out, 2 * j)
                    t_.matmul(aux[5][:], lru_weights[:, r, j], xc[:], start=True, stop=True
                              ).then_inc(lgates_done, 1)
                elif what == "turn":
                    pe.wait_ge(tile_out[j % 2], TILE["in2"] // 2 + (8 + 3 * j) // 2 + 1)
                    pe.wait_ge(lgates_ready, 2 * j + 2)
                    for b in range(QB):
                        last = t_.transpose(aux[5][:, b * P:(b + 1) * P], vT2[:, b * P:(b + 1) * P],
                                            ident[:])
                    last.then_inc(vT2_done, 1)
                elif what == "step":
                    stick_step(j)
                elif what == "lru_sum":
                    pe.wait_ge(v2_out, 8)
                    sum_features(SQ["ylru"] + 4, square_sum[:], aux[5])
                elif what == "lru_spread":
                    spread_factor(RT["ylru"], aux[5])
                elif what == "att_spread":
                    spread_factor(RT["yatt"], aux[5])
                elif what == "att_sum":
                    pe.wait_ge(y_scaled, 4)
                    sum_features(SQ["yatt"] + 4, square_sum[:], aux[5])
                elif what == "first":
                    first_tile("out2", j, Y, OP["ylru"], *n[1:])
            gemm_rest("out2", KB // 2, Y)
            gemm("ffn2", FB, A, OP["out2"],
                 sums=lambda: sum_features(SQ["out2"] + KB, square_sum[:], aux[0]),
                 spreads=lambda: spread_factor(RT["out2"], aux[0]))

            def turn_out(n):
                pe.wait_ge(out_scaled, n + 1)
                if n >= 2:
                    pe.wait_ge(outT_out, n - 1)
                for b in range(QB):
                    last = t_.transpose(aux[2 + n % 2][:, b * P:(b + 1) * P],
                                        work[:, n % 2, b * P:(b + 1) * P], ident[:])
                last.then_inc(outT_done, 1)

            for n in range(KB):
                down("down2", n, TILE["down2"] // 2 + n // 2, n % 2, ready=OP["h2"] if n == 0 else None,
                     between=(lambda: turn_out(n - 1)) if n else None)
            turn_out(KB - 1)
            pe.wait_ge(summed, SQ["down2"] + KB)
            for tt in range(QB):
                last = t_.matmul(aux[0][:, tt:tt + 1], square_sum[:, tt * P:(tt + 1) * P], ones[:, 0:1],
                                 start=True, stop=True)
            last.then_inc(out_sums, 1)


def _column_blocks(w, starts, width=P):
    rows = w.shape[0] // P
    cut = np.stack([w[:, s:s + width] for s in starts])
    return cut.reshape(len(starts), rows, P, width).transpose(0, 2, 1, 3).reshape(len(starts), P, -1)


def _columns(v):
    v = v.reshape(-1, v.shape[-1] // P, P)
    return v.transpose(2, 1, 0).reshape(P, -1)


def kernel(**a):
    from concourse import bacc
    from concourse.bass_utils import run_bass_kernel_spmd
    a = {k: np.asarray(v) for k, v in a.items()}
    every = [n * P for n in range(FB)]
    d = every[:KB]
    w_in, w_in2, ffn_in2 = a["w_in"][0], a["w_in_2"][0], a["w_ffn_in_2"][0]
    glu0 = 964
    starts = [512, 896, 640, 768] + every[:4]
    for n in range(4):
        starts += [glu0 + n * P, glu0 + 512 + n * P]
    starts2 = every[:8]
    for n in range(4):
        starts2 += [2048 + n * P, 1024 + n * P, 1536 + n * P]
    pairs = []
    for gate, up in ((a["w_gate"][0], a["w_up"][0]), (ffn_in2[:, :F], ffn_in2[:, F:])):
        both = np.stack([_column_blocks(gate, every), _column_blocks(up, every)], 1)
        pairs.append(both.reshape(2 * FB, P, -1))
    w8 = np.concatenate([
        _column_blocks(w_in, starts), _column_blocks(a["w_k_cross"][0], d),
        _column_blocks(a["w_v_cross"][0], d), _column_blocks(a["w_out"][0], d),
        _column_blocks(a["w_q_cross"][0], d), _column_blocks(a["w_o_cross"][0], d), pairs[0],
        _column_blocks(w_in2, starts2), _column_blocks(a["w_out_2"][0], d), pairs[1]])
    halves = []
    for w in (a["w_down"][0], a["w_ffn_out_2"][0]):
        halves.append(_column_blocks(w, d).reshape(KB, P, 2, FH * P).transpose(0, 2, 1, 3)
                      .reshape(2 * KB, P, FH * P))
    w11 = np.concatenate(halves)
    freq = np.float32(500000.0) ** (-np.arange(0, 16, 2, dtype=np.float32) / np.float32(16))
    head = np.concatenate([freq, freq, np.zeros(48, np.float32)]).astype(np.float32)
    given = {"g_mix": a["norm_mix_g"], "g_cross": a["norm_cross_g"], "g_mem": a["norm_mem_g"],
             "g_ffn": a["norm_ffn_g"], "g_final": a["norm_final_g"], "g_mix2": a["norm_mix_2"],
             "g_ffn2": a["norm_ffn_2"], "g_final2": a["norm_final_2"], "ln_g": a["ln_b_g"],
             "ln_b": a["ln_b_b"], "g_lru": a["norm_lru_out_2"], "g_att": a["norm_att_out_2"],
             "conv_w": a["conv_b_w"][0], "conv_b": a["conv_b_b"], "fconv_w": a["ffn_conv_w"][0],
             "fconv_b": a["ffn_conv_b"], "lconv_w": a["conv_w_2"][0], "lconv_b": a["conv_b_2"],
             "b_rg": a["b_rg_2"].reshape(-1), "b_ig": a["b_ig_2"].reshape(-1),
             "lam": a["lru_lambda_2"], "freq": np.concatenate([head, head])}
    params = np.ascontiguousarray(np.concatenate([_columns(given[k]) for k, _ in PARAMS], 1))
    blockdiag = np.zeros((P, 2, 4, P), np.float32)
    for r, name in enumerate(("w_rg_2", "w_ig_2")):
        for n in range(8):
            at = slice(n % 2 * HALF, n % 2 * HALF + HALF)
            blockdiag[at, r, n // 2, at] = a[name][0, n]
    arrays = {"w8": w8, "w11": w11, "x": a["x"][0], "mem": a["mem"][0],
              "positions": a["positions"][0].astype(np.int32), "params": params,
              "blockdiag": blockdiag}
    arrays = {k: np.ascontiguousarray(v) for k, v in arrays.items()}
    nc = bacc.Bacc("TRN2", target_bir_lowering=False, num_devices=1)
    aps = [nc.dram_tensor(k, v.shape, mybir.dt.from_np(v.dtype), kind="ExternalInput").ap()
           for k, v in arrays.items()]
    out = nc.dram_tensor("out", (T, D), F32, kind="ExternalOutput").ap()
    build(nc, *aps, out)
    r = run_bass_kernel_spmd(nc, [arrays], core_ids=[0])
    return r.results[0]["out"].reshape(1, T, D)
```

```python
import numpy as np
import concourse.bass as bass
from concourse import mybir
from contextlib import ExitStack

F32 = mybir.dt.float32
F32R = mybir.dt.float32r
I32 = mybir.dt.int32
ALU = mybir.AluOpType
ACT = mybir.ActivationFunctionType

P = 128
T = 512
QB = T // P
D = 1024
KB = D // P
F = 2816
FB = F // P
FH = FB // 2
HALF = 64
A_HEADS = 8
IDX_HEADS = 4
TOPK = 128
MB = 256 // P
X_HEADS = 4
X_KB = 256 // P
TAPS = 31
TAPS_FFN = 3
TAPS_LRU = 4
EPS = 1e-6
NEG = -1e30
CHOSEN = -3e38
ROUND = 1.5 * 2.0 ** 23
TWO_PI = (6.28125, 0.0019350051879882812, 3.0199159819567e-07)

GEMMS = (("in", 16), ("kc", 8), ("vc", 8), ("out", 8), ("qc", 8), ("oc", 8), ("ffn", 2 * FB),
         ("down", 16), ("in2", 20), ("out2", 8), ("ffn2", 2 * FB), ("down2", 16))
CHUNK, TILE = {}, {}
_c = _t = 0
for _name, _n in GEMMS:
    CHUNK[_name], TILE[_name] = _c, _t
    _c += _n
    _t += _n // 2 if _name.startswith("down") else _n
CHUNKS, TILES = _c, _t

PARAMS = (("g_mix", KB), ("g_cross", KB), ("g_mem", KB), ("g_ffn", KB), ("g_final", KB),
          ("g_mix2", KB), ("g_ffn2", KB), ("g_final2", KB), ("ln_g", 4), ("ln_b", 4),
          ("g_lru", 4), ("g_att", 4), ("conv_w", 4 * TAPS), ("conv_b", 4), ("fconv_w", FB * TAPS_FFN),
          ("fconv_b", FB), ("lconv_w", 4 * TAPS_LRU), ("lconv_b", 4), ("b_rg", 4), ("b_ig", 4),
          ("lam", 4), ("freq", 1))
PCOL = {}
_p = 0
for _name, _n in PARAMS:
    PCOL[_name] = _p
    _p += _n
PCOLS = _p


class Steps:

    def __init__(self, eng, sem):
        self.eng, self.sem, self.at = eng, sem, 0

    def step(self, ins):
        ins.then_inc(self.sem, 1)
        self.at = self.at + 1

    def settle(self, lag=0):
        self.eng.wait_ge(self.sem, self.at - lag)

    def then(self, ins):
        self.step(ins)
        self.settle()

    def run(self, first, end, each, body):
        start = self.at
        with self.eng.Fori(first, end) as i:
            self.at = start + (i - first) * each
            body(i)
        self.at = start + (end - first) * each


def build(nc, w8, w11, x, mem, positions, params, blockdiag, out):
    ctx = ExitStack()
    with ctx:
        def sb(name, shape, dt=F32, where=ctx):
            return where.enter_context(nc.sbuf_tensor(name, shape, dt))

        def sem(name):
            return ctx.enter_context(nc.semaphore(name))

        weights_raw = sb("weights_raw", [P, 2, FH * P])
        weights_high = sb("weights_high", [P, 2, FH * P], F32R)
        weights_low = sb("weights_low", [P, 2, FH * P], F32R)
        residual = sb("residual", [P, KB, T])
        a_high = sb("a_high", [P, KB, T], F32R)
        a_low = sb("a_low", [P, KB, T], F32R)
        par = sb("par", [P, PCOLS])
        small = sb("small", [P, 86])
        ident = sb("ident", [P, P])
        ones = sb("ones", [P, P])
        rotate = sb("rotate", [P, P])
        twice = sb("twice", [P, P])
        causal = sb("causal", [P, P])
        before = sb("before", [P, P])
        notbefore = sb("notbefore", [P, P])
        row_factor = sb("row_factor", [P, T])
        square = sb("square", [P, T])
        square_sum = sb("square_sum", [P, T])

        def col(name, n=0, width=1):
            c = PCOL[name]
            return par[:, c + n:c + n + width]

        def dcol(name, n):
            return par[:, bass.ds(PCOL[name] + n, 1)]

        eps = small[:, 0:1]
        tok_sum = small[:, 1:7]
        tok_root = small[:, 7:13]
        tok_factor = small[:, 13:19]
        best = [small[:, c:c + 8] for c in (19, 70, 78)]
        least = small[:, 27:29]
        total = small[:, 29:31]
        inverse = small[:, 31:33]
        decay = small[:, 33:37]
        both_gains = small[:, 37:45]
        first_factor = small[:, 62:66]
        scaled_sum = small[:, 66:70]
        half_pi = small[:, 45:46]
        sp = small[:, 46:62]

        s12 = ExitStack()
        kcT = sb("kcT", [P, KB, MB * P], where=s12)
        vc = sb("vc", [P, MB, D], where=s12)
        s1 = ExitStack()
        m_high = sb("m_high", [P, KB, MB * P], F32R, s1)
        m_low = sb("m_low", [P, KB, MB * P], F32R, s1)
        qT = sb("qT", [P, 4, T], where=s1)
        qiT = sb("qiT", [P, 2, T], where=s1)
        kv = sb("kv", [P, T], where=s1)
        kiwi = sb("kiwi", [P, T], where=s1)
        kT = sb("kT", [P, T], where=s1)
        kiT = sb("kiT", [P, T], where=s1)
        v_pad = sb("v_pad", [P, QB, 2, P], where=s1)
        wi = sb("wi", [P, QB, IDX_HEADS], where=s1)
        cosine = sb("cosine", [P, T], where=s1)
        turned = sb("turned", [P, T], where=s1)
        sine = sb("sine", [P, T], where=s1)
        s1a = ExitStack()
        x_tok = sb("x_tok", [P, 6, D], where=s1a)
        xn_tok = sb("xn_tok", [P, 6, D], where=s1a)
        s1a.close()
        s1b = ExitStack()
        glu = sb("glu", [P, 4, TAPS - 1 + T], where=s1b)
        gate = sb("gate", [P, 4, T], where=s1b)
        conv = sb("conv", [P, 4, T], where=s1b)
        score = sb("score", [P, 3, T], where=s1b)
        rel = sb("rel", [P, 2, T], where=s1b)
        product = rel
        masked = sb("masked", [P, 2, T], where=s1b)
        prob = sb("prob", [P, 3, T], where=s1b)
        probT = sb("probT", [P, 2, T], where=s1b)
        vcT = sb("vcT", [P, 2, MB * P], where=s1b)
        s1b.close()
        s1.close()
        s2 = ExitStack()
        b_high = sb("b_high", [P, KB, T], F32R, s2)
        b_low = sb("b_low", [P, KB, T], F32R, s2)
        qcT = sb("qcT", [P, KB, T], where=s2)
        zeros = sb("zeros", [P, MB * P], where=s2)
        o_high = sb("o_high", [P, KB, T], F32R, s2)
        o_low = sb("o_low", [P, KB, T], F32R, s2)
        xmasked = sb("xmasked", [P, 2, MB * P], where=s2)
        xprob = sb("xprob", [P, 3, MB * P], where=s2)
        xprobT = sb("xprobT", [P, 2, MB, T], where=s2)
        s2.close()
        s12.close()

        s3 = ExitStack()
        h_high = sb("h_high", [P, FB, T], F32R, s3)
        h_low = sb("h_low", [P, FB, T], F32R, s3)
        gated = sb("gated", [P, TAPS_FFN - 1 + T], where=s3)
        work = sb("work", [P, 2, T], where=s3)
        y_tok = sb("y_tok", [P, QB, D], where=s3)
        s3.close()

        s4 = ExitStack()
        y_high = sb("y_high", [P, KB, T], F32R, s4)
        y_low = sb("y_low", [P, KB, T], F32R, s4)
        lru_weights = sb("lru_weights", [P, 2, 4, P], where=s4)
        lru_in = sb("lru_in", [P, 4, TAPS_LRU - 1 + T], where=s4)
        lru_gate = sb("lru_gate", [P, 4, T], where=s4)
        q2 = sb("q2", [P, 4, T], where=s4)
        k2 = sb("k2", [P, 4, T], where=s4)
        vT2 = sb("vT2", [P, T], where=s4)
        v2 = sb("v2", [P, QB, A_HEADS, P], where=s4)
        xc = sb("xc", [P, T], where=s4)
        gates = sb("gates", [P, 2, T], where=s4)
        half_tanh = sb("half_tanh", [P, T], where=s4)
        gate_root = sb("gate_root", [P, T], where=s4)
        inverse_sum = sb("inverse_sum", [P, T], where=s4)
        stay = sb("stay", [P, 2, T], where=s4)
        take = sb("take", [P, 3, T], where=s4)
        left = sb("left", [P, T], where=s4)
        takeT = sb("takeT", [P, 2, T], where=s4)
        s4.close()

        acc = ctx.enter_context(nc.psum_tensor("acc", [P, 2, T], F32))
        aux = [ctx.enter_context(nc.psum_tensor(f"aux{i}", [P, T], F32)) for i in range(6)]
        chunk_landed = [sem("chunk_landed0"), sem("chunk_landed1")]
        weight_high = sem("weight_high")
        weight_low = sem("weight_low")
        chunk_done = sem("chunk_done")
        tile_out = [sem("tile_out0"), sem("tile_out1")]
        operand_high = sem("operand_high")
        operand_low = sem("operand_low")
        squared = sem("squared")
        summed = sem("summed")
        sums_ready = sem("sums_ready")
        root_ready = sem("root_ready")
        factor_ready = sem("factor_ready")
        factor_spread = sem("factor_spread")
        act_steps = sem("act_steps")
        dve_steps = sem("dve_steps")
        consts_ready = sem("consts_ready")
        params_in = sem("params_in")
        positions_in = sem("positions_in")
        blockdiag_in = sem("blockdiag_in")
        x_in = [sem(f"x_in{i}") for i in range(6)]
        angle_ready = sem("angle_ready")
        tables_ready = sem("tables_ready")
        softplus_exp = sem("softplus_exp")
        token_root = sem("token_root")
        token_scaled = sem("token_scaled")
        xT_done = sem("xT_done")
        residual_in = sem("residual_in")
        mT_done = sem("mT_done")
        rotated = sem("rotated")
        roped = sem("roped")
        doubled = sem("doubled")
        doubled_out = sem("doubled_out")
        vwi_done = sem("vwi_done")
        v_out = sem("v_out")
        v_pad_clear = sem("v_pad_clear")
        index_logits = sem("index_logits")
        rel_ready = sem("rel_ready")
        rel_used = sem("rel_used")
        vcT_done = sem("vcT_done")
        vc_out = sem("vc_out")
        conv_steps = sem("conv_steps")
        glu_scaled = sem("glu_scaled")
        glu_gate = sem("glu_gate")
        x_factor = sem("x_factor")
        x_spread = sem("x_spread")
        kv_scaled = sem("kv_scaled")
        glu_ready = sem("glu_ready")
        products = sem("products")
        last_conv_steps = sem("last_conv_steps")
        b_high_ready = sem("b_high_ready")
        b_low_ready = sem("b_low_ready")
        mean_ready = sem("mean_ready")
        centred = sem("centred")
        centred_squared = sem("centred_squared")
        variance_ready = sem("variance_ready")
        ln_root = sem("ln_root")
        ln_factor = sem("ln_factor")
        ln_spread = sem("ln_spread")
        ln_scaled = sem("ln_scaled")
        logits = sem("logits")
        logits_masked = sem("logits_masked")
        prob_raw = sem("prob_raw")
        prob_ready = sem("prob_ready")
        probT_done = sem("probT_done")
        probT_ready = sem("probT_ready")
        heads_done = sem("heads_done")
        x_logits = sem("x_logits")
        x_masked = sem("x_masked")
        x_prob_raw = sem("x_prob_raw")
        x_prob_ready = sem("x_prob_ready")
        x_probT_done = sem("x_probT_done")
        x_probT_ready = sem("x_probT_ready")
        x_heads_done = sem("x_heads_done")
        gate_ready = sem("gate_ready")
        silu_ready = sem("silu_ready")
        hidden_ready = sem("hidden_ready")
        rescaled = sem("rescaled")
        lconv_ready = sem("lconv_ready")
        lgates_done = sem("lgates_done")
        lgates_ready = sem("lgates_ready")
        tanh_ready = sem("tanh_ready")
        lroot_ready = sem("lroot_ready")
        lru_done = sem("lru_done")
        y_lru_done = sem("y_lru_done")
        gelu_ready = sem("gelu_ready")
        y_scaled = sem("y_scaled")
        vT2_done = sem("vT2_done")
        v2_out = sem("v2_out")
        v2_clear = sem("v2_clear")
        sticks = sem("sticks")
        breaks = sem("breaks")
        taken = sem("taken")
        takenT = sem("takenT")
        takenT_ready = sem("takenT_ready")
        stick_heads = sem("stick_heads")
        att_out = sem("att_out")
        out_scaled = sem("out_scaled")
        outT_done = sem("outT_done")
        outT_out = sem("outT_out")
        out_sums = sem("out_sums")
        out_ready = sem("out_ready")
        stored = sem("stored")

        OP = {"x": 0, "mem": 8, "a": 16, "out": 32, "oc": 40, "wo": 48, "h": 56,
              "down": 78, "ylru": 86, "yatt": 90, "out2": 94, "h2": 102}
        SQ = {"out": 0, "wo": 8, "down": 16, "ylru": 32, "yatt": 36, "out2": 40, "down2": 48}
        RT = {"out": 0, "wo": 1, "down": 2, "ylru": 4, "yatt": 5, "out2": 6, "down2": 7}
        DSA = [(qb, h) for qb in range(QB) for h in range(A_HEADS)]
        CROSS = [(h, qb) for h in range(X_HEADS) for qb in range(QB)]
        STICK = [(p, qb, sub) for p in range(4) for qb in range(QB) for sub in range(2)]
        PAIR_TAPS = 20
        CONV = [(n, k) for k in range(TAPS) for n in range(2)]
        third = [(2, k) for k in range(TAPS)]
        CONV, pair = CONV[:PAIR_TAPS], CONV[PAIR_TAPS:]
        while pair or third:
            CONV += pair[:1] + third[:1]
            pair, third = pair[1:], third[1:]
        CONV_STEPS = 25
        LN_MEAN, LN_VAR, LN_OUT, LN_LOW = 26, 28, 30, 31
        OUT_FIRST = 32
        DSA_STEPS = len(DSA) + 4
        EARLY_TAPS = PAIR_TAPS

        def taps_before(step):
            narrow, wide = min(step, KB), max(step - KB, 0)
            rest = len(CONV) - EARLY_TAPS - 3 * KB
            return min(EARLY_TAPS + 3 * narrow + wide * rest // (CONV_STEPS - KB), len(CONV))

        def products_before(step):
            return min(step + 1 if step <= 2 * KB else
                       2 * KB + 1 + (step - 2 * KB) * (TAPS - 2 * KB - 1) // (CONV_STEPS - 2 * KB), TAPS)

        CROSS_PLAN = [("query", 0, 0, 8), ("query", 1, 0, 4), ("factor", 0), ("query", 1, 4, 8)]
        for n in range(2, KB):
            for half in range(2):
                step = 2 * (n - 2) + half
                CROSS_PLAN += [("query", n, 4 * half, 4 * half + 3), ("step", step),
                               ("query", n, 4 * half + 3, 4 * half + 4)]
        CROSS_PLAN.append(CROSS_PLAN.pop(-2))
        for step, piece in enumerate(((0, 0, 2), (0, 2, 4), (1, 0, 2), (1, 2, 4), (0, 4, 5), (0, 5, 6),
                                      (1, 4, 5), (1, 5, 6), ()), 12):
            if step < 20:
                CROSS_PLAN += [("step", step)]
            if piece:
                CROSS_PLAN += [("first", *piece)]
        CROSS_PLAN += [("first", 0, 6, 8), ("first", 1, 6, 8)]
        REC_PLAN = []

        def piece(n, k):
            return [("tile", n, 2 * k, 2 * k + 2)]

        for j in range(4):
            steps = [[("step", 8 * (j - 1) + i)] if j else [] for i in range(8)]
            V, Q, K = ([piece(6 + 3 * j + i, k) for k in range(4)] for i in range(3))
            if j == 0:
                parts = (V[0], [("conv", j)], V[1], V[2], V[3], Q[0], [("gate", j, 0)], Q[1], Q[2],
                         [("gate", j, 1)], Q[3], [("turn", j)], K[0], [("late", j)], K[1],
                         [("hidden", j)], K[2], [("square", j)], K[3])
            else:
                parts = (V[0], [("conv", j)], V[1], steps[0], V[2], [("gate", j, 0)], V[3], steps[1],
                         Q[0], steps[2], [("gate", j, 1)], Q[1], steps[3], [("turn", j)], Q[2],
                         steps[4], [("late", j)], Q[3], K[0], steps[5], K[1],
                         [("hidden", j), ("square", j)] if j < 2 else [], steps[6],
                         K[2], steps[7], K[3])
            for part in parts:
                REC_PLAN += part
        G, H = ([piece(n, k) for k in range(4)] for n in (18, 19))
        for part in ([("step", 24)], G[0], [("step", 25)], G[1], G[2],
                     [("att_clear",), ("step", 26)], G[3], H[0],
                     [("att_square", 0), ("step", 27)], H[1], H[2],
                     [("gelu", 2), ("hidden", 2), ("att_square", 1), ("step", 28)], H[3],
                     [("square", 2), ("step", 29), ("gelu", 3), ("hidden", 3), ("step", 30), ("square", 3),
                      ("step", 31), ("lru_sum",), ("att_square", 2), ("step", 32), ("lru_spread",),
                      ("step", 33), ("lru_scale",), ("lru_low",), ("step", 34), ("first", 0, 0, 2),
                      ("step", 35), ("att_square", 3), ("first", 0, 2, 4), ("first", 1, 0, 1),
                      ("att_sum",), ("first", 1, 1, 2), ("att_spread",), ("first", 1, 2, 4),
                      ("att_scale",), ("first", 0, 4, 8), ("first", 1, 4, 8)]):
            REC_PLAN += part
        SQUARES = [item for item in REC_PLAN if item[0] in ("square", "att_square")]

        def squares_before(*item):
            return SQ["ylru"] + SQUARES.index(item)

        SPREAD = 4
        INDEX = [(qb, h) for qb in range(1, QB) for h in range(IDX_HEADS)]

        def w8_chunk(c):
            return w8[bass.ds(c, 1)].rearrange("a p n -> (a p) n")

        def w_of(step):
            return (DSA[step][0] + 1) * P

        block = ctx.enter_context(nc.Block())

        @block.sync
        def _(sp):
            def load(m, s, src, cols):
                sp.wait_ge(weight_low, 2 * m + s - 1)
                sp.dma_start(weights_raw[:, s, 0:cols], src).then_inc(chunk_landed[s], 16)

            sp.dma_start(weights_raw[:, 0, 0:KB * P], w8[0]).then_inc(chunk_landed[0], 16)
            for tt in range(QB):
                sp.dma_start(x_tok[:, tt], x[tt * P:(tt + 1) * P, :]).then_inc(x_in[tt], 16)
            sp.dma_start(weights_raw[:, 1, 0:KB * P], w8[1]).then_inc(chunk_landed[1], 16)
            for tt in range(2):
                sp.dma_start(x_tok[:, QB + tt], mem[tt * P:(tt + 1) * P, :]).then_inc(x_in[QB + tt], 16)
            with sp.Fori(1, CHUNK["down"] // 2) as m:
                for s in range(2):
                    load(m, s, w8_chunk(2 * m + s), KB * P)
            with sp.Fori(0, 8) as m:
                for s in range(2):
                    load(m + CHUNK["down"] // 2, s,
                         w11[bass.ds(2 * m + s, 1)].rearrange("a p n -> (a p) n"), FH * P)
            with sp.Fori(CHUNK["in2"] // 2, CHUNK["down2"] // 2) as m:
                for s in range(2):
                    load(m, s, w8_chunk(2 * m + s - 16), KB * P)
            with sp.Fori(0, 8) as m:
                for s in range(2):
                    load(m + CHUNK["down2"] // 2, s,
                         w11[bass.ds(2 * m + s + 16, 1)].rearrange("a p n -> (a p) n"), FH * P)
            for tt in range(QB):
                sp.wait_ge(out_ready, tt + 1)
                sp.dma_start(out[tt * P:(tt + 1) * P, :], y_tok[:, tt]).then_inc(stored, 16)
            sp.wait_ge(stored, 16 * QB)

        @block.gpsimd
        def _(pool):
            made = [0]

            def then(ins):
                made[0] += 1
                ins.then_inc(consts_ready, 1)
                pool.wait_ge(consts_ready, made[0])

            g = nc.gpsimd
            for t in (ident, rotate, twice, causal):
                then(g.memset(t[:], 0.0))
            for t in (ones, before):
                then(g.memset(t[:], 1.0))
            then(g.memset(notbefore[:], 0.0))
            then(g.memset(eps, EPS))
            then(g.memset(half_pi, float(np.pi / 2)))
            then(g.affine_select(out=ident[:], in_=ident[:], compare_op=ALU.not_equal, fill=1.0, base=0,
                                 pattern=[[-1, P]], channel_multiplier=1))
            heads = rotate[:].rearrange("p (a b) -> p a b", b=HALF)
            then(g.affine_select(out=heads[:, :, 0:8], in_=heads[:, :, 0:8], compare_op=ALU.not_equal,
                                 fill=-1.0, base=-8, pattern=[[-HALF, 2], [-1, 8]], channel_multiplier=1))
            then(g.affine_select(out=heads[:, :, 8:16], in_=heads[:, :, 8:16], compare_op=ALU.not_equal,
                                 fill=1.0, base=0, pattern=[[-HALF, 2], [-1, 8]], channel_multiplier=1))
            copies = twice[:].rearrange("p (a b) -> p a b", b=HALF)
            then(g.affine_select(out=copies, in_=copies, compare_op=ALU.not_equal, fill=1.0, base=0,
                                 pattern=[[0, 2], [-1, HALF]], channel_multiplier=1))
            then(g.affine_select(out=causal[:], in_=causal[:], compare_op=ALU.is_ge, fill=NEG, base=0,
                                 pattern=[[-1, P]], channel_multiplier=1))
            then(g.affine_select(out=before[:], in_=before[:], compare_op=ALU.is_gt, fill=0.0, base=0,
                                 pattern=[[-1, P]], channel_multiplier=1))
            then(g.affine_select(out=notbefore[:], in_=notbefore[:], compare_op=ALU.is_gt, fill=1.0,
                                 base=0, pattern=[[-1, P]], channel_multiplier=1))

            def low(m, s, cols):
                pool.wait_ge(weight_high, 2 * m + s + 1)
                g.tensor_tensor(weights_low[:, s, 0:cols], weights_raw[:, s, 0:cols],
                                weights_high[:, s, 0:cols].bitcast(F32), ALU.subtract
                                ).then_inc(weight_low, 1)

            def lows(first, end, cols):
                with pool.Fori(first // 2, end // 2) as m:
                    for s in range(2):
                        low(m, s, cols)

            def conv_tap(k):
                pool.wait_ge(products, k + 1)
                if k > 1:
                    pool.wait_ge(last_conv_steps, k - 1)
                g.tensor_tensor(conv[:, 3], conv[:, 3], product[:, k % 2], ALU.add
                                ).then_inc(last_conv_steps, 1)

            def scale_glu(i):
                n, s = i // 2, i % 2
                pool.wait_ge(tile_out[s], TILE["in"] // 2 + 4 + n + 1)
                t = gate[:, n] if s else glu[:, n, TAPS - 1:TAPS - 1 + T]
                g.tensor_tensor(t, t, row_factor[:], ALU.mult).then_inc(glu_scaled, 1)

            glu_tile = CHUNK["in"] + 8
            lows(0, glu_tile + 2, KB * P)
            for i in range(8):
                low((glu_tile + 2 + i) // 2, i % 2, KB * P)
                scale_glu(i)
            for c in range(CHUNK["kc"] + 2, CHUNK["out"] + 2):
                low(c // 2, c % 2, KB * P)
                conv_tap(c - CHUNK["kc"] - 1)
            for k in range(CHUNK["out"] - CHUNK["kc"] + 1, TAPS):
                conv_tap(k)
            for first, end, cols in ((CHUNK["out"] + 2, CHUNK["down"], KB * P),
                                     (CHUNK["down"], CHUNK["in2"], FH * P),
                                     (CHUNK["in2"], CHUNK["down2"], KB * P),
                                     (CHUNK["down2"], CHUNKS, FH * P)):
                lows(first, end, cols)
        NCONST = 16

        @block.scalar
        def _(act):
            a = nc.scalar
            own = Steps(act, act_steps)

            act.dma_start(par[:], params).then_inc(params_in, 16)
            act.dma_start(sine[:].bitcast(I32), positions.partition_broadcast(P)).then_inc(positions_in, 16)

            def high(m, s, cols=KB * P):
                act.wait_ge(chunk_landed[s], 16 * (m + 1))
                act.wait_ge(chunk_done, 2 * m + s - 1)
                a.copy(weights_high[:, s, 0:cols], weights_raw[:, s, 0:cols]).then_inc(weight_high, 1)

            def high_next(m, s, cols=KB * P):
                high(m + 1, s, cols)

            def tile_done(m, s):
                act.wait_ge(chunk_done, 2 * m + s + 1)

            def first_high(s):
                act.wait_ge(chunk_landed[s], 16)
                a.copy(weights_high[:, s, 0:KB * P], weights_raw[:, s, 0:KB * P]).then_inc(weight_high, 1)

            first_high(0)
            act.wait_ge(params_in, 16)
            for k in range(KB):
                act.wait_ge(xT_done, k + 1)
                a.activation(a_high[:, k], aux[k % 6][:], ACT.Copy, scale=col("g_mix", k)
                             ).then_inc(operand_high, 1)
                a.copy(residual[:, k], aux[k % 6][:]).then_inc(residual_in, 1)
                if k == 2:
                    first_high(1)

            def row_roots(first, end):
                for tt in range(first, end):
                    act.wait_ge(x_in[tt], 16)
                    own.step(a.activation(xn_tok[:, tt], x_tok[:, tt], ACT.Square,
                                          accum_out=tok_sum[:, tt:tt + 1]))
                own.settle()
                a.activation(tok_root[:, first:end], tok_sum[:, first:end], ACT.Sqrt, scale=1.0 / D,
                             bias=eps).then_inc(token_root, 1)

            def first_out(n, dst):
                high_next(n // 2, n % 2)
                tile_done(n // 2, n % 2)
                a.copy(dst, acc[:, n % 2]).then_inc(tile_out[n % 2], 1)

            first_out(0, kv[:])
            row_roots(0, QB + MB)
            first_out(1, kiwi[:])
            act.wait_ge(angle_ready, 2)
            own.step(a.activation(sine[:], sine[:], ACT.Sin))
            a.activation(cosine[:], cosine[:], ACT.Sin, bias=half_pi, scale=-1.0).then_inc(tables_ready, 1)
            first_out(2, qiT[:, 0])
            first_out(3, qiT[:, 1])
            act.wait_ge(doubled, 1)
            a.copy(kT[:], aux[4][:]).then_inc(doubled_out, 1)
            act.wait_ge(doubled, 2)
            a.copy(kiT[:], aux[5][:]).then_inc(doubled_out, 1)
            for k in range(KB):
                act.wait_ge(mT_done, k + 1)
                a.activation(m_high[:, k], aux[k % 2][:, 0:MB * P], ACT.Copy, scale=col("g_mem", k)
                             ).then_inc(operand_high, 1)
            act.wait_ge(vwi_done, 1)
            act.wait_ge(v_pad_clear, 1)
            v_tok = aux[4][:].rearrange("p (b f) -> p b f", f=P)[:, :, HALF:P]
            a.copy(v_pad[:, :, 0, 0:HALF], v_tok).then_inc(v_out, 1)
            a.copy(v_pad[:, :, 1, HALF:P], v_tok).then_inc(v_out, 1)
            act.wait_ge(vwi_done, 2)
            a.mul(wi[:], aux[5][:].rearrange("p (b f) -> p b f", f=P)[:, :, HALF:HALF + IDX_HEADS],
                  IDX_HEADS ** -0.5).then_inc(v_out, 1)
            for n, (qb, h) in enumerate(INDEX):
                act.wait_ge(index_logits, n + 1)
                if n >= 2:
                    act.wait_ge(rel_used, n - 1)
                bank = aux[2 + h % 2 + 2 * (n // 2 % 2)]
                a.activation(rel[:, n % 2, 0:(qb + 1) * P], bank[:, 0:(qb + 1) * P], ACT.Relu,
                             scale=HALF ** -0.5).then_inc(rel_ready, 1)
            act.wait_ge(angle_ready, 3)
            a.activation(sp[:, 0:4], sp[:, 0:4], ACT.Exp, scale=-1.0).then_inc(softplus_exp, 1)
            for n in range(4):
                m, s = 2 + n // 2, n % 2
                high_next(m, s)
                tile_done(m, s)
                a.copy(qT[:, n], acc[:, s]).then_inc(tile_out[s], 1)

            def glu_sigmoid(n):
                act.wait_ge(glu_scaled, 2 * n + 2)
                a.activation(gate[:, n], gate[:, n], ACT.Sigmoid).then_inc(glu_gate, 1)

            for n in range(4):
                m = 4 + n
                high_next(m, 0)
                tile_done(m, 0)
                a.copy(glu[:, n, TAPS - 1:TAPS - 1 + T], acc[:, 0]).then_inc(tile_out[0], 1)
                high_next(m, 1)
                tile_done(m, 1)
                a.copy(gate[:, n], acc[:, 1]).then_inc(tile_out[1], 1)
                if n:
                    glu_sigmoid(n - 1)
            glu_sigmoid(3)
            def vc_back(n):
                act.wait_ge(vcT_done, n + 1)
                a.copy(vc[:, :, n * P:(n + 1) * P],
                       acc[:, n % 2, MB * P:2 * MB * P].rearrange("p (b f) -> p b f", f=P)
                       ).then_inc(vc_out, 1)

            def kc_tile(n):
                m, s = CHUNK["kc"] // 2 + n // 2, n % 2
                high_next(m, s)
                a.copy(kcT[:, n], acc[:, s, 0:MB * P]).then_inc(tile_out[s], 1)

            def vc_tile(n):
                m, s = CHUNK["vc"] // 2 + n // 2, n % 2
                high_next(m, s)
                if n >= 2:
                    act.wait_ge(vcT_done, n - 1)
                a.copy(vcT[:, s], acc[:, s, 0:MB * P]).then_inc(tile_out[s], 1)

            def conv_product(k):
                src, weight = glu[:, 3, k:k + T], col("conv_w", 3 * TAPS + k)
                if k == 0:
                    act.wait_ge(glu_ready, 1)
                    ins = a.activation(conv[:, 3], src, ACT.Identity, scale=weight, bias=col("conv_b", 3))
                else:
                    if k >= 3:
                        act.wait_ge(last_conv_steps, k - 2)
                    ins = a.activation(product[:, k % 2], src, ACT.Copy, scale=weight)
                ins.then_inc(products, 1)

            conv_product(0)
            for step in range(DSA_STEPS):
                if step < len(DSA):
                    w = w_of(step)
                    act.wait_ge(logits_masked, step + 1)
                    if step >= 2:
                        act.wait_ge(prob_ready, step - 1)
                    if step >= 3:
                        act.wait_ge(probT_done, step - 2)
                    a.activation(prob[:, step % 3, 0:w], masked[:, step % 2, 0:w], ACT.Exp, scale=-1.0,
                                 bias=least[:, step % 2:step % 2 + 1],
                                 accum_out=total[:, step % 2:step % 2 + 1]).then_inc(prob_raw, 1)
                if 1 <= step - KB <= KB:
                    vc_back(step - KB - 1)
                j = step - 2
                if 0 <= j < len(DSA):
                    w = w_of(j)
                    act.wait_ge(probT_done, j + 1)
                    if j >= 2:
                        act.wait_ge(heads_done, j - 1)
                    a.copy(probT[:, j % 2, 0:w], aux[2 + j % 2][:, 0:w]).then_inc(probT_ready, 1)
                if step < KB:
                    kc_tile(step)
                elif step < 2 * KB:
                    vc_tile(step - KB)
                j = step - 4
                if j >= 0 and j % 2:
                    qb, h = DSA[j]
                    act.wait_ge(heads_done, j + 1)
                    a.copy(a_high[:, h // 2, qb * P:(qb + 1) * P], aux[4 + j // 2 % 2][:, 0:P]
                           ).then_inc(operand_high, 1)
                for k in range(products_before(step), products_before(step + 1)):
                    conv_product(k)
                if step == LN_MEAN:
                    for n in range(4):
                        act.wait_ge(centred, n + 1)
                        a.activation(gate[:, n], conv[:, n], ACT.Square).then_inc(centred_squared, 1)
                if step == LN_VAR:
                    act.wait_ge(variance_ready, 1)
                    a.activation(tok_root[:, 0:QB], acc[:, 1, 0:QB], ACT.Sqrt, scale=1.0 / (4 * P), bias=eps
                                 ).then_inc(ln_root, 1)
                if step in (LN_OUT, LN_OUT + 1):
                    for n in (0, 1) if step == LN_OUT else (2, 3):
                        act.wait_ge(ln_scaled, n + 1)
                        own.then(a.activation(conv[:, n], conv[:, n], ACT.Silu, scale=col("ln_g", n),
                                              bias=col("ln_b", n)))
                        a.copy(a_high[:, 4 + n], conv[:, n]).then_inc(b_high_ready, 1)

            def take_root(rt, bank, width):
                act.wait_ge(sums_ready, rt + 1)
                a.activation(tok_root[:, 0:QB], bank[:, 0:QB], ACT.Sqrt, scale=1.0 / width, bias=eps
                             ).then_inc(root_ready, 1)

            def residual_tile(m, s, n, sq, op, gain, dst):
                act.wait_ge(tile_out[s], m + 1)
                if sq is not None:
                    act.wait_ge(summed, sq + n)
                    a.activation(square[:], residual[:, bass.ds(n, 1)], ACT.Square
                                 ).then_inc(squared, 1)
                a.activation(dst[:, bass.ds(n, 1)], residual[:, bass.ds(n, 1)], ACT.Copy,
                             scale=dcol(gain, n)).then_inc(operand_high, 1)

            def residual_gemm(name, sq, op, gain, dst):
                first = CHUNK[name] // 2
                tile = TILE[name] // 2
                with act.Fori(0, KB // 2) as i:
                    for s in range(2):
                        high_next(first + i, s)
                        residual_tile(tile + i, s, 2 * i + s, sq, op, gain, dst)

            residual_gemm("out", SQ["out"], OP["out"], "g_cross", b_high)
            def cross_step(step):
                if step < len(CROSS):
                    act.wait_ge(x_masked, step + 1)
                    if step >= 3:
                        act.wait_ge(x_probT_done, step - 2)
                    a.activation(xprob[:, step % 3], xmasked[:, step % 2], ACT.Exp, scale=-1.0,
                                 bias=least[:, step % 2:step % 2 + 1],
                                 accum_out=total[:, step % 2:step % 2 + 1]).then_inc(x_prob_raw, 1)
                j = step - 2
                if 0 <= j < len(CROSS):
                    h, qb = CROSS[j]
                    act.wait_ge(x_probT_done, j + 1)
                    if h >= 2:
                        act.wait_ge(x_heads_done, 2 * (h - 1))
                    a.copy(xprobT[:, h % 2, :, qb * P:(qb + 1) * P],
                           aux[2 + j % 2][:, 0:MB * P].rearrange("p (b f) -> p b f", f=P)
                           ).then_inc(x_probT_ready, 1)
                j = step - 4
                if j >= 0 and j % QB == QB - 1:
                    h = CROSS[j][0]
                    for d in range(2):
                        act.wait_ge(x_heads_done, 2 * h + d + 1)
                        a.copy(o_high[:, 2 * h + d], aux[4 + d][:]).then_inc(operand_high, 1)

            for what, n, *span in CROSS_PLAN:
                if what == "query" and span[1] == KB:
                    high_next(CHUNK["qc"] // 2 + n // 2, n % 2)
                    if n == 0:
                        take_root(RT["out"], aux[0], D)
                elif what == "step":
                    cross_step(n)
            residual_gemm("oc", SQ["wo"], OP["wo"], "g_ffn", a_high)

            def ffn(name, dst, last_cols, rt, base_):
                def pair(m, n, first=False, cols=KB * P):
                    high_next(m, 0, cols)
                    if first:
                        take_root(rt, aux[0], D)
                    if name == "ffn":
                        act.wait_ge(gate_ready, n + 1)
                    else:
                        act.wait_ge(tile_out[0], TILE[name] // 2 + n + 1)
                    a.activation(work[:, 0], work[:, 0], ACT.Silu).then_inc(silu_ready, 1)
                    high_next(m, 1, cols)
                    act.wait_ge(hidden_ready, base_ + n + 1)
                    a.copy(dst[:, bass.ds(n, 1)], work[:, bass.ds(1, 1)]).then_inc(operand_high, 1)

                base = CHUNK[name] // 2
                pair(base, 0, first=True)
                with act.Fori(1, FB - 1) as i:
                    pair(base + i, i)
                pair(base + FB - 1, FB - 1, cols=last_cols)

            ffn("ffn", h_high, FH * P, RT["wo"], 0)
            def down_tile(m, t, s, n, next_cols):
                high(m + 1, 0, next_cols)
                high(m + 1, 1, next_cols)
                act.wait_ge(tile_out[s], t + 1)
                act.wait_ge(summed, SQ["down"] + 2 * n)
                a.activation(square[:], residual[:, bass.ds(n, 1)], ACT.Square).then_inc(squared, 1)
                a.activation(work[:, bass.ds(0, 1)], residual[:, bass.ds(n, 1)], ACT.Square,
                             scale=dcol("g_final", n)).then_inc(squared, 1)
                a.activation(a_high[:, bass.ds(n, 1)], residual[:, bass.ds(n, 1)], ACT.Copy,
                             scale=both_gains[:, bass.ds(n, 1)]).then_inc(operand_high, 1)

            with act.Fori(0, 3) as i:
                for s in range(2):
                    down_tile(CHUNK["down"] // 2 + 2 * i + s, TILE["down"] // 2 + i, s, 2 * i + s, FH * P)
            for s in range(2):
                down_tile(CHUNK["down"] // 2 + 6 + s, TILE["down"] // 2 + 3, s, 6 + s,
                          FH * P if s == 0 else KB * P)

            c0, t0 = CHUNK["in2"] // 2, TILE["in2"] // 2
            act.dma_start(lru_weights[:], blockdiag).then_inc(blockdiag_in, 16)
            high_next(c0, 0)
            take_root(RT["down"], aux[0], D)
            act.wait_ge(rescaled, 1)
            a.activation(tok_root[:, 0:QB], scaled_sum, ACT.Sqrt, scale=1.0 / D, bias=eps
                         ).then_inc(root_ready, 1)
            high_next(c0, 1)
            with act.Fori(1, 3) as i:
                for s in range(2):
                    high_next(c0 + i, s)

            def gelu(n):
                act.wait_ge(tile_out[n % 2], t0 + (2 if n < 2 else 9) + 1)
                a.activation(lru_gate[:, n], lru_gate[:, n], ACT.Gelu_apprx_tanh).then_inc(gelu_ready, 1)

            gelu(0)
            gelu(1)

            def squares(src, n, before_, count, sem_):
                act.wait_ge(sem_, count)
                act.wait_ge(summed, before_)
                a.activation(square[:], src[:, n], ACT.Square).then_inc(squared, 1)

            def high_parts(src, block0):
                for n in range(4):
                    act.wait_ge(y_scaled, block0 + n + 1)
                    a.copy(y_high[:, block0 + n], src[:, n]).then_inc(operand_high, 1)

            def stick_step(step):
                if step % 8 == 3 and step > 3:
                    p = step // 8 - 1
                    act.wait_ge(stick_heads, 8 * (p + 1))
                    a.copy(q2[:, p], aux[4][:]).then_inc(att_out, 1)
                if step < len(STICK):
                    p, qb, sub = STICK[step]
                    w = (qb + 1) * P
                    act.wait_ge(sticks, step + 1)
                    if step >= 3:
                        act.wait_ge(takenT, step - 2)
                    a.activation(take[:, step % 3, 0:w], aux[sub][:, 0:w], ACT.Sigmoid,
                                 scale=HALF ** -0.5).then_inc(breaks, 1)
                    if step >= 2:
                        act.wait_ge(taken, step - 1)
                    a.activation(stay[:, step % 2, 0:w], aux[sub][:, 0:w], ACT.Sigmoid,
                                 scale=-HALF ** -0.5).then_inc(breaks, 1)
                j = step - 2
                if 0 <= j < len(STICK):
                    w = (STICK[j][1] + 1) * P
                    act.wait_ge(takenT, j + 1)
                    if j >= 2:
                        act.wait_ge(stick_heads, j - 1)
                    a.copy(takeT[:, j % 2, 0:w], aux[2 + j % 2][:, 0:w]).then_inc(takenT_ready, 1)

            for what, *n in REC_PLAN:
                j = n[0] if n else 0
                if what == "tile":
                    if n[2] == KB:
                        high_next(c0 + j // 2, j % 2)
                elif what == "gate":
                    r = n[1]
                    act.wait_ge(lgates_done, 2 * j + r + 1)
                    if r and j:
                        act.wait_ge(lru_done, j)
                    a.activation(gates[:, r], aux[5][:], ACT.Sigmoid, bias=col(("b_rg", "b_ig")[r], j)
                                 ).then_inc(lgates_ready, 1)
                    if r == 0:
                        act.wait_ge(lgates_ready, 2 * j + 1)
                        if j:
                            act.wait_ge(lru_done, j)
                        a.activation(half_tanh[:], gates[:, 0], ACT.Tanh, scale=decay[:, j:j + 1]
                                     ).then_inc(tanh_ready, 1)
                elif what == "turn":
                    act.wait_ge(vT2_done, j + 1)
                    act.wait_ge(v2_clear, QB)
                    blocks = aux[5][:].rearrange("p (b f) -> p b f", f=P)
                    for sub in range(2):
                        a.copy(v2[:, :, 2 * j + sub, sub * HALF:(sub + 1) * HALF],
                               blocks[:, :, sub * HALF:(sub + 1) * HALF]).then_inc(v2_out, 1)
                elif what == "late":
                    act.wait_ge(tanh_ready, j + 1)
                    a.activation(gate_root[:], half_tanh[:], ACT.Sqrt).then_inc(lroot_ready, 1)
                elif what == "square":
                    squares(lru_gate, j, squares_before(what, j), j + 1, y_lru_done)
                elif what == "gelu":
                    gelu(j)
                elif what == "step":
                    stick_step(j)
                elif what == "lru_sum":
                    take_root(RT["ylru"], aux[5], 4 * P)
                elif what == "lru_low":
                    high_parts(lru_gate, 0)
                elif what == "att_square":
                    squares(q2, j, squares_before(what, j), j + 1, att_out)
                elif what == "att_sum":
                    take_root(RT["yatt"], aux[5], 4 * P)
                elif what == "att_scale":
                    high_parts(q2, 4)
            residual_gemm("out2", SQ["out2"], OP["out2"], "g_ffn2", a_high)
            ffn("ffn2", h_high, FH * P, RT["out2"], FB)

            def back(n):
                act.wait_ge(outT_done, n + 1)
                a.copy(y_tok[:, :, n * P:(n + 1) * P],
                       aux[2 + n % 2][:].rearrange("p (b f) -> p b f", f=P)).then_inc(outT_out, 1)

            def last_tile(m, t, s, n, more=True):
                if more:
                    high(m + 1, 0, FH * P)
                if n:
                    back(n - 1)
                if more:
                    high(m + 1, 1, FH * P)
                act.wait_ge(tile_out[s], t + 1)
                act.wait_ge(summed, SQ["down2"] + n)
                a.activation(square[:], residual[:, bass.ds(n, 1)], ACT.Square).then_inc(squared, 1)
                if n >= 2:
                    act.wait_ge(outT_done, n - 1)
                a.activation(work[:, s], residual[:, bass.ds(n, 1)], ACT.Copy,
                             scale=dcol("g_final2", n)).then_inc(out_scaled, 1)

            own.then(a.activation(tok_root[:, QB:QB + 1], eps, ACT.Sqrt))
            for n in range(KB):
                last_tile(CHUNK["down2"] // 2 + n, TILE["down2"] // 2 + n // 2, n % 2, n, n < KB - 1)
            back(KB - 1)
            act.wait_ge(out_sums, 1)
            a.activation(tok_root[:, 0:QB], aux[0][:, 0:QB], ACT.Sqrt, scale=1.0 / D, bias=eps
                         ).then_inc(root_ready, 1)

        @block.vector
        def _(dve):
            v = nc.vector
            own = Steps(dve, dve_steps)

            def scale_rows(tt):
                dve.wait_ge(token_root, 1)
                own.then(v.reciprocal(tok_factor[:, tt:tt + 1], tok_root[:, tt:tt + 1]))
                v.tensor_scalar(xn_tok[:, tt], x_tok[:, tt], tok_factor[:, tt:tt + 1], None, ALU.mult
                                ).then_inc(token_scaled, 1)

            for k in range(KB):
                dve.wait_ge(operand_high, OP["x"] + k + 1)
                dve.wait_ge(residual_in, k + 1)
                v.scalar_tensor_tensor(a_low[:, k], residual[:, k], col("g_mix", k),
                                       a_high[:, k].bitcast(F32), ALU.mult, ALU.subtract
                                       ).then_inc(operand_low, 1)
            dve.wait_ge(params_in, 16)
            dve.wait_ge(positions_in, 16)
            own.then(v.tensor_copy(cosine[:], sine[:].bitcast(I32)))
            own.then(v.tensor_scalar(sine[:], cosine[:], col("freq"), None, ALU.mult))
            own.then(v.tensor_scalar(cosine[:], sine[:], float(1 / (2 * np.pi)), ROUND, ALU.mult, ALU.add))
            own.then(v.tensor_scalar(cosine[:], cosine[:], -ROUND, None, ALU.add))
            for piece in TWO_PI:
                own.then(v.scalar_tensor_tensor(sine[:], cosine[:], -piece, sine[:], ALU.mult, ALU.add))
            v.tensor_scalar(sine[:], sine[:], 3.1415925, -3.1415925, ALU.min, ALU.max
                            ).then_inc(angle_ready, 1)
            dve.wait_ge(angle_ready, 1)
            v.scalar_tensor_tensor(cosine[:], sine[:], -1.0, sine[:], ALU.mult, ALU.max
                                   ).then_inc(angle_ready, 1)
            v.scalar_tensor_tensor(sp[:, 0:4], col("lam", 0, 4), -1.0, col("lam", 0, 4), ALU.mult, ALU.max
                                   ).then_inc(angle_ready, 1)
            own.step(v.tensor_tensor(both_gains, col("g_final", 0, KB), col("g_mix2", 0, KB), ALU.mult))
            v.memset(v_pad[:], 0.0).then_inc(v_pad_clear, 1)

            dve.wait_ge(token_root, 1)
            v.reciprocal(tok_factor[:, 0:QB], tok_root[:, 0:QB]).then_inc(x_factor, 1)
            dve.wait_ge(x_spread, 1)
            own.then(v.tensor_copy(row_factor[:], aux[4][:]))
            dve.wait_ge(tables_ready, 1)
            own.step(v.tensor_tensor(cosine[:], cosine[:], row_factor[:], ALU.mult))
            own.then(v.tensor_tensor(sine[:], sine[:], row_factor[:], ALU.mult))

            def rope(n, t, rows, bank):
                dve.wait_ge(rotated, n + 1)
                own.step(v.tensor_tensor(t, t, cosine[0:rows], ALU.mult))
                own.then(v.tensor_tensor(turned[0:rows], bank[0:rows], sine[0:rows], ALU.mult))
                v.tensor_tensor(t, t, turned[0:rows], ALU.add).then_inc(roped, 1)
                dve.wait_ge(roped, n + 1)

            rope(0, kv[0:HALF], HALF, aux[2])
            rope(1, kiwi[0:HALF], HALF, aux[3])
            for t in (kv, kiwi):
                v.tensor_tensor(t[HALF:P], t[HALF:P], row_factor[HALF:P], ALU.mult).then_inc(kv_scaled, 1)
            for tt in (4, 5):
                scale_rows(tt)
            rope(2, qiT[:, 0], P, aux[2])
            rope(3, qiT[:, 1], P, aux[3])
            for k in range(KB):
                dve.wait_ge(operand_high, OP["mem"] + k + 1)
                v.scalar_tensor_tensor(m_low[:, k], aux[k % 2][:, 0:MB * P], col("g_mem", k),
                                       m_high[:, k].bitcast(F32), ALU.mult, ALU.subtract
                                       ).then_inc(operand_low, 1)
            dve.wait_ge(v_out, 3)
            for n, (qb, h) in enumerate(INDEX):
                dve.wait_ge(rel_ready, n + 1)
                w = (qb + 1) * P
                dst, src, weight = score[:, qb - 1, 0:w], rel[:, n % 2, 0:w], wi[:, qb, h:h + 1]
                if h == 0:
                    v.tensor_scalar(dst, src, weight, None, ALU.mult).then_inc(rel_used, 1)
                else:
                    v.scalar_tensor_tensor(dst, src, weight, dst, ALU.mult, ALU.add
                                           ).then_inc(rel_used, 1)
                dve.wait_ge(rel_used, n + 1)
            rows = [score[:, qb - 1, 0:(qb + 1) * P] for qb in range(1, QB)]
            for qb in range(1, QB):
                diag = score[:, qb - 1, qb * P:(qb + 1) * P]
                own.step(v.tensor_tensor(diag, diag, causal[:], ALU.add))
            for _ in range(TOPK // 8):
                for n, row in enumerate(rows):
                    own.settle(lag=2)
                    own.step(v.max(best[n], row))
                for n, row in enumerate(rows):
                    own.settle(lag=2)
                    own.step(v.match_replace(out=row, in_to_replace=best[n], in_values=row,
                                             imm_value=CHOSEN))
            for row in rows:
                own.settle(lag=2)
                own.step(v.tensor_scalar(row, row, CHOSEN, NEG, ALU.not_equal, ALU.mult))
            own.settle()
            for n in range(4):
                rope(4 + n, qT[:, n], P, aux[n])
            def conv_tap(i):
                n, k = CONV[i]
                src, weight = glu[:, n, k:k + T], col("conv_w", n * TAPS + k)
                if k == 0:
                    ins = v.tensor_scalar(conv[:, n], src, weight, col("conv_b", n), ALU.mult, ALU.add)
                else:
                    dve.wait_ge(conv_steps, i - 1)
                    ins = v.scalar_tensor_tensor(conv[:, n], src, weight, conv[:, n], ALU.mult, ALU.add)
                ins.then_inc(conv_steps, 1)

            own.then(v.memset(glu[:, :, 0:TAPS - 1], 0.0))
            for n in range(4):
                if n == 2:
                    own.settle()
                    for i in range(EARLY_TAPS):
                        conv_tap(i)
                dve.wait_ge(glu_gate, n + 1)
                body = glu[:, n, TAPS - 1:TAPS - 1 + T]
                if n < 3:
                    own.step(v.tensor_tensor(body, body, gate[:, n], ALU.mult))
                else:
                    v.tensor_tensor(body, body, gate[:, n], ALU.mult).then_inc(glu_ready, 1)
            own.settle()

            for step in range(DSA_STEPS):
                if step < len(DSA):
                    qb, h = DSA[step]
                    w = (qb + 1) * P
                    dve.wait_ge(logits, step + 1)
                    if step >= 2:
                        dve.wait_ge(prob_raw, step - 1)
                    mask = causal[:] if qb == 0 else score[:, qb - 1, 0:w]
                    v.tensor_tensor_reduce(out=masked[:, step % 2, 0:w], in0=aux[h % 2][:, 0:w], in1=mask,
                                           scale=-HALF ** -0.5, scalar=3e38, op0=ALU.add, op1=ALU.min,
                                           accum_out=least[:, step % 2:step % 2 + 1]
                                           ).then_inc(logits_masked, 1)
                taps = range(taps_before(step), taps_before(step + 1))
                j = step - 1
                if 0 <= j < len(DSA):
                    dve.wait_ge(prob_raw, j + 1)
                    own.then(v.reciprocal(inverse[:, j % 2:j % 2 + 1], total[:, j % 2:j % 2 + 1]))
                    v.tensor_scalar(prob[:, j % 3, 0:w_of(j)], prob[:, j % 3, 0:w_of(j)],
                                    inverse[:, j % 2:j % 2 + 1], None, ALU.mult).then_inc(prob_ready, 1)
                for i in taps:
                    conv_tap(i)
                j = step - 4
                if j >= 0 and j % 2:
                    qb, h = DSA[j]
                    dve.wait_ge(operand_high, OP["a"] + j // 2 + 1)
                    span = slice(qb * P, (qb + 1) * P)
                    v.tensor_tensor(a_low[:, h // 2, span], aux[4 + j // 2 % 2][:, 0:P],
                                    a_high[:, h // 2, span].bitcast(F32), ALU.subtract
                                    ).then_inc(operand_low, 1)
                if step == LN_MEAN:
                    dve.wait_ge(mean_ready, 1)
                    for n in range(4):
                        v.scalar_tensor_tensor(conv[:, n], acc[:, 0], -1.0 / (4 * P), conv[:, n], ALU.mult,
                                               ALU.add).then_inc(centred, 1)
                if step == LN_VAR:
                    dve.wait_ge(ln_root, 1)
                    v.reciprocal(tok_factor[:, 0:QB], tok_root[:, 0:QB]).then_inc(ln_factor, 1)
                if step == LN_OUT:
                    dve.wait_ge(centred, 4)
                    dve.wait_ge(ln_spread, 1)
                    for n in range(4):
                        v.tensor_tensor(conv[:, n], conv[:, n], acc[:, 1], ALU.mult).then_inc(ln_scaled, 1)
                if step in (LN_LOW, LN_LOW + 1):
                    for n in (0, 1) if step == LN_LOW else (2, 3):
                        dve.wait_ge(b_high_ready, n + 1)
                        v.tensor_tensor(a_low[:, 4 + n], conv[:, n], a_high[:, 4 + n].bitcast(F32),
                                        ALU.subtract).then_inc(b_low_ready, 1)

            def token_factor(rt):
                dve.wait_ge(root_ready, rt + 1)
                v.reciprocal(tok_factor[:, 0:QB], tok_root[:, 0:QB]).then_inc(factor_ready, 1)

            def new_factor(rt):
                token_factor(rt)
                dve.wait_ge(factor_spread, rt + 1)
                own.then(v.tensor_copy(row_factor[:], aux[0][:]))

            def residual_tile(c, t, s, n):
                dve.wait_ge(chunk_done, c)
                v.tensor_tensor(residual[:, bass.ds(n, 1)].rearrange("p a n -> p (a n)"), acc[:, s],
                                residual[:, bass.ds(n, 1)].rearrange("p a n -> p (a n)"), ALU.add
                                ).then_inc(tile_out[s], 1)
                dve.wait_ge(tile_out[s], t + 1)

            def at(x, n):
                return x[:, bass.ds(n, 1)].rearrange("p a n -> p (a n)")

            def add_squares(count, total_, squares):
                dve.wait_ge(squared, count)
                v.tensor_tensor(total_, total_, squares, ALU.add).then_inc(summed, 1)

            def low_part(dst, src_high, n, gain, count):
                dve.wait_ge(operand_high, count)
                v.scalar_tensor_tensor(at(dst, n), at(residual, n), gain, at(src_high, n).bitcast(F32),
                                       ALU.mult, ALU.subtract).then_inc(operand_low, 1)

            def residual_gemm(name, sq, op, gain, dst_high, dst_low):
                own.then(v.memset(square_sum[:], 0.0))

                def body(i):
                    for s in range(2):
                        n = 2 * i + s
                        residual_tile(CHUNK[name] + n + 1, TILE[name] // 2 + i, s, n)
                        add_squares(sq + n + 1, square_sum[:], square[:])
                        low_part(dst_low, dst_high, n, dcol(gain, n), op + n + 1)
                        dve.wait_ge(summed, sq + n + 1)
                own.run(0, KB // 2, 0, body)

            residual_gemm("out", SQ["out"], OP["out"], "g_cross", b_high, b_low)
            own.then(v.memset(zeros[:], 0.0))
            new_factor(RT["out"])

            def cross_step(step):
                if step < len(CROSS):
                    dve.wait_ge(x_logits, step + 1)
                    if step >= 2:
                        dve.wait_ge(x_prob_raw, step - 1)
                    v.tensor_tensor_reduce(out=xmasked[:, step % 2], in0=aux[step % 2][:, 0:MB * P],
                                           in1=zeros[:], scale=-(X_KB * P) ** -0.5, scalar=3e38,
                                           op0=ALU.add, op1=ALU.min,
                                           accum_out=least[:, step % 2:step % 2 + 1]).then_inc(x_masked, 1)
                j = step - 1
                if 0 <= j < len(CROSS):
                    dve.wait_ge(x_prob_raw, j + 1)
                    own.then(v.reciprocal(inverse[:, j % 2:j % 2 + 1], total[:, j % 2:j % 2 + 1]))
                    v.tensor_scalar(xprob[:, j % 3], xprob[:, j % 3], inverse[:, j % 2:j % 2 + 1], None,
                                    ALU.mult).then_inc(x_prob_ready, 1)
                j = step - 4
                if j >= 0 and j % QB == QB - 1:
                    for d in range(2):
                        n = 2 * CROSS[j][0] + d
                        dve.wait_ge(operand_high, OP["oc"] + n + 1)
                        v.tensor_tensor(o_low[:, n], aux[4 + d][:], o_high[:, n].bitcast(F32),
                                        ALU.subtract).then_inc(operand_low, 1)

            for what, n, *span in CROSS_PLAN:
                if what == "query" and span[1] == KB:
                    dve.wait_ge(chunk_done, CHUNK["qc"] + n + 1)
                    v.tensor_tensor(qcT[:, n], acc[:, n % 2], row_factor[:], ALU.mult
                                    ).then_inc(tile_out[n % 2], 1)
                elif what == "step":
                    cross_step(n)
            residual_gemm("oc", SQ["wo"], OP["wo"], "g_ffn", a_high, a_low)

            def ffn(name, dst_high, dst_low, op, base, taps):
                def pair(i):
                    t = TILE[name] // 2 + i
                    dve.wait_ge(chunk_done, CHUNK[name] + 2 * i + 1)
                    dst = gated[:, TAPS_FFN - 1:TAPS_FFN - 1 + T] if taps else work[:, 0]
                    ins = v.tensor_tensor(dst, acc[:, 0], row_factor[:], ALU.mult)
                    ins.then_inc(tile_out[0], 1)
                    if taps:
                        dve.wait_ge(tile_out[0], t + 1)
                        c = i * TAPS_FFN
                        own.then(v.tensor_scalar(work[:, 0], gated[:, 2:2 + T], dcol("fconv_w", c + 2),
                                                 dcol("fconv_b", i), ALU.mult, ALU.add))
                        own.then(v.scalar_tensor_tensor(work[:, 0], gated[:, 1:1 + T], dcol("fconv_w", c + 1),
                                                        work[:, 0], ALU.mult, ALU.add))
                        v.scalar_tensor_tensor(work[:, 0], gated[:, 0:T], dcol("fconv_w", c), work[:, 0],
                                               ALU.mult, ALU.add).then_inc(gate_ready, 1)
                    dve.wait_ge(chunk_done, CHUNK[name] + 2 * i + 2)
                    v.tensor_tensor(work[:, 1], acc[:, 1], row_factor[:], ALU.mult).then_inc(tile_out[1], 1)
                    dve.wait_ge(tile_out[1], t + 1)
                    dve.wait_ge(silu_ready, base + i + 1)
                    v.tensor_tensor(work[:, 1], work[:, 1], work[:, 0], ALU.mult).then_inc(hidden_ready, 1)
                    dve.wait_ge(hidden_ready, base + i + 1)
                    dve.wait_ge(operand_high, op + i + 1)
                    v.tensor_tensor(at(dst_low, i), work[:, 1], at(dst_high, i).bitcast(F32), ALU.subtract
                                    ).then_inc(operand_low, 1)
                    dve.wait_ge(operand_low, op + i + 1)
                own.run(0, FB, 2 if taps else 0, pair)

            own.then(v.memset(gated[:, 0:TAPS_FFN - 1], 0.0))
            new_factor(RT["wo"])
            ffn("ffn", h_high, h_low, OP["h"], 0, True)

            own.step(v.memset(square_sum[:], 0.0))
            own.then(v.memset(work[:, 1], 0.0))
            dve.wait_ge(softplus_exp, 1)
            e, s1_, s2_, po = sp[:, 0:4], sp[:, 4:8], sp[:, 8:12], sp[:, 12:16]
            own.then(v.tensor_scalar(s1_, e, 2.0, None, ALU.add))
            own.then(v.reciprocal(s1_, s1_))
            own.then(v.tensor_tensor(s1_, s1_, e, ALU.mult))
            own.then(v.tensor_tensor(s2_, s1_, s1_, ALU.mult))
            own.then(v.tensor_scalar(po, s2_, 1.0 / 15, 1.0 / 13, ALU.mult, ALU.add))
            for n in (11, 9, 7, 5, 3, 1):
                own.then(v.tensor_tensor(po, po, s2_, ALU.mult))
                own.then(v.tensor_scalar(po, po, 1.0 / n, None, ALU.add))
            own.then(v.tensor_tensor(po, po, s1_, ALU.mult))
            own.then(v.tensor_scalar(s2_, col("lam", 0, 4), -4.0, 0.0, ALU.mult, ALU.max))
            own.then(v.scalar_tensor_tensor(decay, po, 8.0, s2_, ALU.mult, ALU.add))

            def down(i):
                for s in range(2):
                    n = 2 * i + s
                    residual_tile(CHUNK["down"] + 2 * n + 2, TILE["down"] // 2 + i, s, n)
                    add_squares(SQ["down"] + 2 * n + 1, square_sum[:], square[:])
                    add_squares(SQ["down"] + 2 * n + 2, work[:, 1], work[:, 0])
                    low_part(a_low, a_high, n, both_gains[:, bass.ds(n, 1)], OP["down"] + n + 1)
                    dve.wait_ge(summed, SQ["down"] + 2 * n + 2)
            own.run(0, KB // 2, 0, down)

            dve.wait_ge(root_ready, RT["down"] + 1)
            v.reciprocal(first_factor, tok_root[:, 0:QB]).then_inc(factor_ready, 1)
            dve.wait_ge(factor_ready, RT["down"] + 1)
            dve.wait_ge(sums_ready, RT["down"] + 2)
            own.then(v.tensor_tensor(scaled_sum, aux[1][:, 0:QB], first_factor, ALU.mult))
            v.tensor_tensor(scaled_sum, scaled_sum, first_factor, ALU.mult).then_inc(rescaled, 1)
            dve.wait_ge(root_ready, RT["down"] + 2)
            own.then(v.reciprocal(tok_factor[:, 0:QB], tok_root[:, 0:QB]))
            v.tensor_tensor(tok_factor[:, 0:QB], tok_factor[:, 0:QB], first_factor, ALU.mult
                            ).then_inc(factor_ready, 1)
            dve.wait_ge(factor_spread, RT["down"] + 2)
            own.step(v.tensor_copy(row_factor[:], aux[0][:]))
            own.then(v.tensor_copy(square_sum[:], aux[1][:]))

            own.step(v.memset(lru_in[:, :, 0:TAPS_LRU - 1], 0.0))

            def out_of(n, dst):
                dve.wait_ge(chunk_done, CHUNK["in2"] + n + 1)
                v.tensor_tensor(dst, acc[:, n % 2], row_factor[:], ALU.mult).then_inc(tile_out[n % 2], 1)
                dve.wait_ge(tile_out[n % 2], TILE["in2"] // 2 + n // 2 + 1)

            for n in range(6):
                out_of(n, lru_in[:, n, TAPS_LRU - 1:TAPS_LRU - 1 + T] if n < 4 else lru_gate[:, n - 4])
                for k in range(n * KB // 6, (n + 1) * KB // 6):
                    own.step(v.scalar_tensor_tensor(residual[:, k], residual[:, k], col("g_final", k),
                                                    square_sum[:], ALU.mult, ALU.mult))
                if n >= 2:
                    v.memset(v2[:, n - 2], 0.0).then_inc(v2_clear, 1)
            own.settle()
            own.then(v.memset(square_sum[:], 0.0))
            dve.wait_ge(blockdiag_in, 16)
            def scale_parts(rt, src, gain):
                dve.wait_ge(factor_spread, rt + 1)
                for n in range(4):
                    v.scalar_tensor_tensor(src[:, n], src[:, n], col(gain, n), aux[5][:], ALU.mult, ALU.mult
                                           ).then_inc(y_scaled, 1)

            def low_parts(src, op, block0):
                for n in range(4):
                    dve.wait_ge(operand_high, op + n + 1)
                    v.tensor_tensor(y_low[:, block0 + n], src[:, n], y_high[:, block0 + n].bitcast(F32),
                                    ALU.subtract).then_inc(operand_low, 1)

            def stick_step(step):
                if step >= len(STICK):
                    return
                p, qb, sub = STICK[step]
                w = (qb + 1) * P
                i, to = step % 2, step % 3
                dve.wait_ge(breaks, 2 * step + 2)
                own.step(v.tensor_tensor(stay[:, i, w - P:w], stay[:, i, w - P:w], notbefore[:], ALU.max))
                own.then(v.tensor_tensor(take[:, to, w - P:w], take[:, to, w - P:w], before[:], ALU.mult))
                back = stay[:, i, 0:w][:, ::-1]
                own.then(v.tensor_tensor_scan(left[:, 0:w][:, ::-1], back, back, 1.0, ALU.mult, ALU.min))
                v.tensor_tensor(take[:, to, 0:w - 1], take[:, to, 0:w - 1], left[:, 1:w], ALU.mult
                                ).then_inc(taken, 1)

            for what, *n in REC_PLAN:
                j = n[0] if n else 0
                if what == "conv":
                    if j:
                        dve.wait_ge(lgates_done, 2 * j)
                    for k in range(TAPS_LRU - 1, -1, -1):
                        src, weight = lru_in[:, j, k:k + T], col("lconv_w", j * TAPS_LRU + k)
                        if k == TAPS_LRU - 1:
                            own.then(v.tensor_scalar(xc[:], src, weight, col("lconv_b", j), ALU.mult,
                                                     ALU.add))
                        elif k:
                            own.then(v.scalar_tensor_tensor(xc[:], src, weight, xc[:], ALU.mult, ALU.add))
                        else:
                            v.scalar_tensor_tensor(xc[:], src, weight, xc[:], ALU.mult, ALU.add
                                                   ).then_inc(lconv_ready, 1)
                elif what == "tile" and n[2] == KB:
                    if j >= 18:
                        out_of(j, lru_gate[:, j - 16])
                        continue
                    p, kind = (j - 6) // 3, (j - 6) % 3
                    if kind == 0 and p:
                        dve.wait_ge(vT2_done, p)
                    out_of(j, (vT2[:], q2[:, p], k2[:, p])[kind])
                elif what == "gate" and n[1] == 1:
                    dve.wait_ge(tanh_ready, j + 1)
                    own.then(v.tensor_scalar(inverse_sum[:], half_tanh[:], 1.0, None, ALU.add))
                    own.then(v.reciprocal(inverse_sum[:], inverse_sum[:]))
                    dve.wait_ge(lgates_ready, 2 * j + 2)
                    own.then(v.tensor_tensor(gates[:, 1], gates[:, 1], xc[:], ALU.mult))
                elif what == "late":
                    dve.wait_ge(lroot_ready, j + 1)
                    own.then(v.scalar_tensor_tensor(gate_root[:], gate_root[:], 2.0, inverse_sum[:],
                                                    ALU.mult, ALU.mult))
                    own.step(v.tensor_tensor(gate_root[:], gate_root[:], gates[:, 1], ALU.mult))
                    own.then(v.tensor_scalar(inverse_sum[:], inverse_sum[:], 2.0, -1.0, ALU.mult, ALU.add))
                    v.tensor_tensor_scan(lru_in[:, j, TAPS_LRU - 1:TAPS_LRU - 1 + T], inverse_sum[:],
                                         gate_root[:], 0.0, ALU.mult, ALU.add).then_inc(lru_done, 1)
                elif what == "hidden":
                    dve.wait_ge(gelu_ready, j + 1)
                    dve.wait_ge(lru_done, j + 1)
                    v.tensor_tensor(lru_gate[:, j], lru_gate[:, j],
                                    lru_in[:, j, TAPS_LRU - 1:TAPS_LRU - 1 + T], ALU.mult
                                    ).then_inc(y_lru_done, 1)
                elif what == "square":
                    at_ = squares_before(what, j) + 1
                    add_squares(at_, square_sum[:], square[:])
                    dve.wait_ge(summed, at_)
                elif what == "att_clear":
                    dve.wait_ge(lgates_done, 8)
                    own.then(v.memset(xc[:], 0.0))
                elif what == "step":
                    stick_step(j)
                elif what == "lru_spread":
                    token_factor(RT["ylru"])
                elif what == "att_spread":
                    token_factor(RT["yatt"])
                elif what == "lru_scale":
                    scale_parts(RT["ylru"], lru_gate, "g_lru")
                elif what == "lru_low":
                    low_parts(lru_gate, OP["ylru"], 0)
                elif what == "att_square":
                    at_ = squares_before(what, j) + 1
                    add_squares(at_, xc[:], square[:])
                    dve.wait_ge(summed, at_)
                elif what == "att_scale":
                    scale_parts(RT["yatt"], q2, "g_att")
                    low_parts(q2, OP["yatt"], 4)
            residual_gemm("out2", SQ["out2"], OP["out2"], "g_ffn2", a_high, a_low)
            new_factor(RT["out2"])
            ffn("ffn2", h_high, h_low, OP["h2"], FB, False)

            own.then(v.memset(square_sum[:], 0.0))
            for n in range(KB):
                residual_tile(CHUNK["down2"] + 2 * n + 2, TILE["down2"] // 2 + n // 2, n % 2, n)
                add_squares(SQ["down2"] + n + 1, square_sum[:], square[:])
                dve.wait_ge(summed, SQ["down2"] + n + 1)
            dve.wait_ge(root_ready, RT["down2"] + 1)
            own.then(v.reciprocal(tok_factor[:, 0:QB], tok_root[:, 0:QB]))
            dve.wait_ge(outT_out, KB)
            for tt in range(QB):
                v.tensor_scalar(y_tok[:, tt], y_tok[:, tt], tok_factor[:, tt:tt + 1], None, ALU.mult
                                ).then_inc(out_ready, 1)

        @block.tensor
        def _(pe):
            t_ = nc.tensor
            A = (a_high, a_low)
            B = (b_high, b_low)
            M = (m_high, m_low)
            O = (o_high, o_low)
            Y = (y_high, y_low)
            H = (h_high, h_low)

            def chunk(m, s, blocks, bank, operand, k0=0, start=True, stop=True, ready=None, cols=T,
                      before_block=None, first=0, opens=0, closes=None):
                pe.wait_ge(weight_low, 2 * m + s + 1)
                high, low = operand
                closes = (FH if blocks == FH else KB) - 1 if closes is None else closes
                for k in range(first, blocks):
                    if before_block:
                        before_block(k)
                    if ready is not None:
                        pe.wait_ge(operand_low, ready + k + 1)
                    wide = slice(k * P, (k + 1) * P)
                    passes = ((weights_high, high), (weights_high, low), (weights_low, high))
                    for n, (w, x_) in enumerate(passes):
                        last = t_.matmul(acc[:, bank, 0:cols], w[:, s, wide], x_[:, k0 + k, 0:cols],
                                         start=start and k == opens and n == 0,
                                         stop=stop and k == closes and n == 2)
                if blocks == closes + 1:
                    last.then_inc(chunk_done, 1)

            def free(bank, t):
                pe.wait_ge(tile_out[bank], t)

            def gemm_pair(name, i, operand, cols=T):
                m, t = CHUNK[name] // 2 + i, TILE[name] // 2 + i
                for s in range(2):
                    free(s, t)
                    chunk(m, s, KB, s, operand, cols=cols)

            def gemm(name, pairs, operand, ready=None, sums=None, spreads=None, cols=T):
                m, t = CHUNK[name] // 2, TILE[name] // 2
                free(0, t)
                chunk(m, 0, KB, 0, operand, ready=ready, cols=cols)
                if sums:
                    sums()
                free(1, t)
                chunk(m, 1, SPREAD, 1, operand, cols=cols)
                if spreads:
                    spreads()
                chunk(m, 1, KB, 1, operand, cols=cols, first=SPREAD)
                with pe.Fori(1, pairs) as i:
                    gemm_pair(name, i, operand, cols=cols)

            def gemm_rest(name, pairs, operand):
                with pe.Fori(1, pairs) as i:
                    gemm_pair(name, i, operand)

            def first_tile(name, n, operand, ready, k, end):
                if k == 0:
                    free(n, TILE[name] // 2)
                chunk(CHUNK[name] // 2, n, end, n, operand, ready=ready, first=k)

            def sum_features(count, src, bank):
                pe.wait_ge(summed, count)
                for tt in range(QB):
                    last = t_.matmul(bank[:, tt:tt + 1], src[:, tt * P:(tt + 1) * P],
                                     ones[:, 0:1], start=True, stop=True)
                last.then_inc(sums_ready, 1)

            def spread(factor, bank):
                for tt in range(QB):
                    last = t_.matmul(bank[:, tt * P:(tt + 1) * P],
                                     factor[:, tt:tt + 1].broadcast_to([P, P]), ident[:],
                                     start=True, stop=True)
                return last

            def spread_factor(rt, bank):
                pe.wait_ge(factor_ready, rt + 1)
                spread(tok_factor, bank).then_inc(factor_spread, 1)

            pe.wait_ge(consts_ready, NCONST)

            def turn_x(k):
                if k >= 6:
                    pe.wait_ge(operand_low, k - 5)
                    pe.wait_ge(residual_in, k - 5)
                for tt in range(QB):
                    if k == 0:
                        pe.wait_ge(x_in[tt], 16)
                    last = t_.transpose(aux[k % 6][:, tt * P:(tt + 1) * P],
                                        x_tok[:, tt, k * P:(k + 1) * P], ident[:])
                last.then_inc(xT_done, 1)

            for k in range(3):
                turn_x(k)

            def in_tile(n):
                m, s = n // 2, n % 2
                if m:
                    free(s, m)
                chunk(m, s, KB, s, A, ready=0 if n == 0 else None,
                      before_block=(lambda k: turn_x(k + 3) if k + 3 < KB else None) if n == 0 else None)

            def rotation(src, rows, bank):
                t_.matmul(bank[0:rows], rotate[0:rows, 0:rows], src, start=True, stop=True
                          ).then_inc(rotated, 1)

            in_tile(0)
            in_tile(1)
            pe.wait_ge(tile_out[0], 1)
            rotation(kv[0:HALF], HALF, aux[2])
            in_tile(2)
            pe.wait_ge(operand_low, KB)
            pe.wait_ge(residual_in, KB)
            pe.wait_ge(x_factor, 1)
            spread(tok_factor, aux[4]).then_inc(x_spread, 1)
            pe.wait_ge(tile_out[1], 1)
            rotation(kiwi[0:HALF], HALF, aux[3])
            in_tile(3)
            pe.wait_ge(roped, 1)
            t_.matmul(aux[4][:], twice[0:HALF], kv[0:HALF], start=True, stop=True).then_inc(doubled, 1)
            pe.wait_ge(tile_out[0], 2)
            rotation(qiT[:, 0], P, aux[2])
            pe.wait_ge(roped, 2)
            t_.matmul(aux[5][:], twice[0:HALF], kiwi[0:HALF], start=True, stop=True).then_inc(doubled, 1)
            pe.wait_ge(tile_out[1], 2)
            rotation(qiT[:, 1], P, aux[3])
            pe.wait_ge(token_scaled, MB)
            for k in range(KB):
                if k >= 2:
                    pe.wait_ge(operand_low, OP["mem"] + k - 1)
                for tt in range(MB):
                    last = t_.transpose(aux[k % 2][:, tt * P:(tt + 1) * P],
                                        xn_tok[:, QB + tt, k * P:(k + 1) * P], ident[:])
                last.then_inc(mT_done, 1)
            for n, src in enumerate((kv, kiwi)):
                pe.wait_ge(doubled_out, n + 1)
                pe.wait_ge(kv_scaled, n + 1)
                for b in range(QB):
                    last = t_.transpose(aux[4 + n][:, b * P:(b + 1) * P], src[:, b * P:(b + 1) * P],
                                        ident[:])
                last.then_inc(vwi_done, 1)
            pe.wait_ge(roped, 4)
            pe.wait_ge(v_out, 3)
            for n, (qb, h) in enumerate(INDEX):
                if n >= 4:
                    pe.wait_ge(rel_ready, n - 3)
                w, rows = (qb + 1) * P, slice(h % 2 * HALF, h % 2 * HALF + HALF)
                t_.matmul(aux[2 + h % 2 + 2 * (n // 2 % 2)][:, 0:w],
                          qiT[rows, h // 2, qb * P:(qb + 1) * P], kiT[rows, 0:w], start=True, stop=True
                          ).then_inc(index_logits, 1)
            in_tile(4)
            for n in range(4):
                in_tile(5 + n)
                pe.wait_ge(tile_out[n % 2], 3 + n // 2)
                if n == 0:
                    pe.wait_ge(operand_low, OP["mem"] + KB)
                if n == 2:
                    pe.wait_ge(rel_ready, len(INDEX))
                rotation(qT[:, n], P, aux[n])
            for n in range(9, 16):
                in_tile(n)
            def turn_values(n):
                pe.wait_ge(tile_out[n % 2], TILE["vc"] // 2 + n // 2 + 1)
                for b in range(MB):
                    last = t_.transpose(acc[:, n % 2, (MB + b) * P:(MB + b + 1) * P],
                                        vcT[:, n % 2, b * P:(b + 1) * P], ident[:])
                last.then_inc(vcT_done, 1)

            pe.wait_ge(roped, 8)
            for step in range(DSA_STEPS):
                if step < len(DSA):
                    qb, h = DSA[step]
                    if step >= 2:
                        pe.wait_ge(logits_masked, step - 1)
                    w, rows = (qb + 1) * P, slice(h % 2 * HALF, h % 2 * HALF + HALF)
                    t_.matmul(aux[h % 2][:, 0:w], qT[rows, h // 2, qb * P:(qb + 1) * P], kT[rows, 0:w],
                              start=True, stop=True).then_inc(logits, 1)
                j = step - 2
                if 0 <= j < len(DSA):
                    pe.wait_ge(prob_ready, j + 1)
                    if j >= 2:
                        pe.wait_ge(probT_ready, j - 1)
                    for b in range(DSA[j][0] + 1):
                        last = t_.transpose(aux[2 + j % 2][:, b * P:(b + 1) * P],
                                            prob[:, j % 3, b * P:(b + 1) * P], ident[:])
                    last.then_inc(probT_done, 1)
                if 1 <= step - KB <= KB:
                    turn_values(step - KB - 1)
                if step < KB:
                    m, s = CHUNK["kc"] // 2 + step // 2, step % 2
                    free(s, TILE["kc"] // 2 + step // 2)
                    chunk(m, s, KB, s, M, cols=MB * P)
                elif step < 2 * KB:
                    n = step - KB
                    m, s = CHUNK["vc"] // 2 + n // 2, n % 2
                    free(s, TILE["vc"] // 2 + n // 2)
                    if n >= 2:
                        pe.wait_ge(vc_out, n - 1)
                    chunk(m, s, KB, s, M, cols=MB * P)
                j = step - 3
                if 0 <= j < len(DSA):
                    qb, h = DSA[j]
                    g = j // 2
                    pe.wait_ge(probT_ready, j + 1)
                    if g >= 2 and h % 2 == 0:
                        pe.wait_ge(operand_low, OP["a"] + g - 1)
                    for b in range(qb + 1):
                        last = t_.matmul(aux[4 + g % 2][:, 0:P], v_pad[:, b, h % 2],
                                         probT[:, j % 2, b * P:(b + 1) * P],
                                         start=h % 2 == 0 and b == 0, stop=h % 2 == 1 and b == qb)
                    last.then_inc(heads_done, 1)
                if step == LN_MEAN:
                    pe.wait_ge(vc_out, KB)
                    pe.wait_ge(conv_steps, len(CONV))
                    pe.wait_ge(last_conv_steps, TAPS - 1)
                    for n in range(4):
                        last = t_.matmul(acc[:, 0], ones[:], conv[:, n], start=n == 0, stop=n == 3)
                    last.then_inc(mean_ready, 1)
                if step == LN_VAR:
                    pe.wait_ge(tile_out[1], TILE["out"] // 2)
                    pe.wait_ge(centred_squared, 4)
                    for tt in range(QB):
                        for n in range(4):
                            last = t_.matmul(acc[:, 1, tt:tt + 1], gate[:, n, tt * P:(tt + 1) * P],
                                             ones[:, 0:1], start=n == 0, stop=n == 3)
                    last.then_inc(variance_ready, 1)
                if step >= OUT_FIRST and step - OUT_FIRST < 4:
                    s, part = divmod(step - OUT_FIRST, 2)
                    if step == OUT_FIRST:
                        pe.wait_ge(ln_scaled, 4)
                    pe.wait_ge(b_low_ready, 2 * part + 2)
                    chunk(CHUNK["out"] // 2, s, 6 + 2 * part, s, A, first=4 + 2 * part, opens=4, closes=3)
                if step == LN_VAR + 1:
                    pe.wait_ge(ln_factor, 1)
                    spread(tok_factor, acc[:, 1]).then_inc(ln_spread, 1)

            pe.wait_ge(operand_low, OP["out"])
            for s in range(2):
                chunk(CHUNK["out"] // 2, s, 4, s, A, opens=4, closes=3)
            gemm_rest("out", KB // 2, A)
            def cross_step(step):
                if step < len(CROSS):
                    h, qb = CROSS[step]
                    if qb == 0:
                        for s in range(2):
                            pe.wait_ge(tile_out[s], TILE["qc"] // 2 + h + 1)
                    if step >= 2:
                        pe.wait_ge(x_masked, step - 1)
                    for c in range(X_KB):
                        last = t_.matmul(aux[step % 2][:, 0:MB * P],
                                         qcT[:, X_KB * h + c, qb * P:(qb + 1) * P], kcT[:, X_KB * h + c],
                                         start=c == 0, stop=c == X_KB - 1)
                    last.then_inc(x_logits, 1)
                j = step - 2
                if 0 <= j < len(CROSS):
                    pe.wait_ge(x_prob_ready, j + 1)
                    if j >= 2:
                        pe.wait_ge(x_probT_ready, j - 1)
                    for b in range(MB):
                        last = t_.transpose(aux[2 + j % 2][:, b * P:(b + 1) * P],
                                            xprob[:, j % 3, b * P:(b + 1) * P], ident[:])
                    last.then_inc(x_probT_done, 1)
                j = step - 3
                if 0 <= j < len(CROSS) and j % QB == QB - 1:
                    h = CROSS[j][0]
                    pe.wait_ge(x_probT_ready, j + 1)
                    for d in range(2):
                        if h:
                            pe.wait_ge(operand_low, OP["oc"] + 2 * (h - 1) + d + 1)
                        col0 = h * X_KB * P + d * P
                        for b in range(MB):
                            last = t_.matmul(aux[4 + d][:], vc[:, b, col0:col0 + P], xprobT[:, h % 2, b],
                                             start=b == 0, stop=b == MB - 1)
                        last.then_inc(x_heads_done, 1)

            for what, n, *span in CROSS_PLAN:
                if what == "query":
                    if span[0] == 0:
                        free(n % 2, TILE["qc"] // 2 + n // 2)
                    chunk(CHUNK["qc"] // 2 + n // 2, n % 2, span[1], n % 2, B,
                          ready=OP["out"] if n == 0 else None, first=span[0])
                    if n == 0:
                        sum_features(SQ["out"] + KB, square_sum[:], aux[0])
                elif what == "factor":
                    spread_factor(RT["out"], aux[0])
                elif what == "step":
                    cross_step(n)
                else:
                    first_tile("oc", n, O, OP["oc"], *span)
            gemm_rest("oc", KB // 2, O)
            gemm("ffn", FB, A, OP["wo"],
                 sums=lambda: sum_features(SQ["wo"] + KB, square_sum[:], aux[0]),
                 spreads=lambda: spread_factor(RT["wo"], aux[0]))

            def down(name, n, t, s, ready=None, between=None):
                m = CHUNK[name] // 2 + n
                free(s, t)
                for half in range(2):
                    chunk(m, half, FH, s, H, k0=half * FH, start=half == 0, stop=half == 1,
                          ready=None if ready is None else ready + half * FH)
                    if between and half == 0:
                        between()

            def down_gemm(name, ready, after=None):
                for s in range(2):
                    down(name, s, TILE[name] // 2, s, ready=ready if s == 0 else None)
                with pe.Fori(1, KB // 2) as i:
                    for s in range(2):
                        down(name, 2 * i + s, TILE[name] // 2 + i, s)

            down_gemm("down", OP["h"])

            def two_sums():
                sum_features(SQ["down"] + 2 * KB, square_sum[:], aux[0])
                sum_features(SQ["down"] + 2 * KB, work[:, 1], aux[1])

            def two_factors():
                pe.wait_ge(factor_ready, RT["down"] + 2)
                spread(first_factor, aux[1]).then_inc(factor_spread, 1)
                spread(tok_factor, aux[0]).then_inc(factor_spread, 1)

            gemm("in2", 3, A, OP["down"], sums=two_sums, spreads=two_factors)

            def in2_tile(n, k, end):
                m, s = CHUNK["in2"] // 2 + n // 2, n % 2
                if k == 0:
                    free(s, TILE["in2"] // 2 + n // 2)
                chunk(m, s, end, s, A, first=k)

            pe.wait_ge(blockdiag_in, 16)
            def stick_step(step):
                if step < len(STICK):
                    p, qb, sub = STICK[step]
                    if step % 8 == 0:
                        pe.wait_ge(v2_out, 2 * (p + 1))
                        for n in (7 + 3 * p, 8 + 3 * p):
                            pe.wait_ge(tile_out[n % 2], TILE["in2"] // 2 + n // 2 + 1)
                    if step >= 2:
                        pe.wait_ge(breaks, 2 * (step - 1))
                    w, rows = (qb + 1) * P, slice(sub * HALF, (sub + 1) * HALF)
                    t_.matmul(aux[sub][:, 0:w], q2[rows, p, qb * P:(qb + 1) * P], k2[rows, p, 0:w],
                              start=True, stop=True).then_inc(sticks, 1)
                j = step - 2
                if 0 <= j < len(STICK):
                    pe.wait_ge(taken, j + 1)
                    if j >= 2:
                        pe.wait_ge(takenT_ready, j - 1)
                    for b in range(STICK[j][1] + 1):
                        last = t_.transpose(aux[2 + j % 2][:, b * P:(b + 1) * P],
                                            take[:, j % 3, b * P:(b + 1) * P], ident[:])
                    last.then_inc(takenT, 1)
                j = step - 3
                if 0 <= j < len(STICK):
                    p, qb, sub = STICK[j]
                    pe.wait_ge(takenT_ready, j + 1)
                    if p and j % 8 == 0:
                        pe.wait_ge(att_out, p)
                    for b in range(qb + 1):
                        last = t_.matmul(aux[4][:, qb * P:(qb + 1) * P], v2[:, b, 2 * p + sub],
                                         takeT[:, j % 2, b * P:(b + 1) * P],
                                         start=sub == 0 and b == 0, stop=sub == 1 and b == qb)
                    last.then_inc(stick_heads, 1)

            for what, *n in REC_PLAN:
                j = n[0] if n else 0
                if what == "tile":
                    in2_tile(*n)
                elif what == "gate":
                    r = n[1]
                    pe.wait_ge(lconv_ready, j + 1)
                    if r:
                        pe.wait_ge(lgates_ready, 2 * j + 1)
                    elif j:
                        pe.wait_ge(v2_out, 2 * j)
                    t_.matmul(aux[5][:], lru_weights[:, r, j], xc[:], start=True, stop=True
                              ).then_inc(lgates_done, 1)
                elif what == "turn":
                    pe.wait_ge(tile_out[j % 2], TILE["in2"] // 2 + (6 + 3 * j) // 2 + 1)
                    pe.wait_ge(lgates_ready, 2 * j + 2)
                    for b in range(QB):
                        last = t_.transpose(aux[5][:, b * P:(b + 1) * P], vT2[:, b * P:(b + 1) * P],
                                            ident[:])
                    last.then_inc(vT2_done, 1)
                elif what == "step":
                    stick_step(j)
                elif what == "lru_sum":
                    pe.wait_ge(v2_out, 8)
                    sum_features(squares_before("square", 3) + 1, square_sum[:], aux[5])
                elif what == "lru_spread":
                    spread_factor(RT["ylru"], aux[5])
                elif what == "att_spread":
                    spread_factor(RT["yatt"], aux[5])
                elif what == "att_sum":
                    pe.wait_ge(y_scaled, 4)
                    sum_features(squares_before("att_square", 3) + 1, xc[:], aux[5])
                elif what == "first":
                    first_tile("out2", j, Y, OP["ylru"], *n[1:])
            gemm_rest("out2", KB // 2, Y)
            gemm("ffn2", FB, A, OP["out2"],
                 sums=lambda: sum_features(SQ["out2"] + KB, square_sum[:], aux[0]),
                 spreads=lambda: spread_factor(RT["out2"], aux[0]))

            def turn_out(n):
                pe.wait_ge(out_scaled, n + 1)
                if n >= 2:
                    pe.wait_ge(outT_out, n - 1)
                for b in range(QB):
                    last = t_.transpose(aux[2 + n % 2][:, b * P:(b + 1) * P],
                                        work[:, n % 2, b * P:(b + 1) * P], ident[:])
                last.then_inc(outT_done, 1)

            for n in range(KB):
                down("down2", n, TILE["down2"] // 2 + n // 2, n % 2, ready=OP["h2"] if n == 0 else None,
                     between=(lambda: turn_out(n - 1)) if n else None)
            turn_out(KB - 1)
            pe.wait_ge(summed, SQ["down2"] + KB)
            for tt in range(QB):
                last = t_.matmul(aux[0][:, tt:tt + 1], square_sum[:, tt * P:(tt + 1) * P], ones[:, 0:1],
                                 start=True, stop=True)
            last.then_inc(out_sums, 1)


def _column_blocks(w, starts, width=P):
    rows = w.shape[0] // P
    cut = np.stack([w[:, s:s + width] for s in starts])
    return cut.reshape(len(starts), rows, P, width).transpose(0, 2, 1, 3).reshape(len(starts), P, -1)


def _columns(v):
    v = v.reshape(-1, v.shape[-1] // P, P)
    return v.transpose(2, 1, 0).reshape(P, -1)


def kernel(**a):
    from concourse import bacc
    from concourse.bass_utils import run_bass_kernel_spmd
    a = {k: np.asarray(v) for k, v in a.items()}
    every = [n * P for n in range(FB)]
    d = every[:KB]
    w_in, w_in2, ffn_in2 = a["w_in"][0], a["w_in_2"][0], a["w_ffn_in_2"][0]
    glu0 = 964
    starts = [512, 896, 640, 768] + every[:4]
    for n in range(4):
        starts += [glu0 + n * P, glu0 + 512 + n * P]
    starts2 = every[:6]
    for n in range(4):
        starts2 += [2048 + n * P, 1024 + n * P, 1536 + n * P]
    starts2 += every[6:8]
    pairs = []
    for gate, up in ((a["w_gate"][0], a["w_up"][0]), (ffn_in2[:, :F], ffn_in2[:, F:])):
        both = np.stack([_column_blocks(gate, every), _column_blocks(up, every)], 1)
        pairs.append(both.reshape(2 * FB, P, -1))
    w8 = np.concatenate([
        _column_blocks(w_in, starts), _column_blocks(a["w_k_cross"][0], d),
        _column_blocks(a["w_v_cross"][0], d), _column_blocks(a["w_out"][0], d),
        _column_blocks(a["w_q_cross"][0], d), _column_blocks(a["w_o_cross"][0], d), pairs[0],
        _column_blocks(w_in2, starts2), _column_blocks(a["w_out_2"][0], d), pairs[1]])
    halves = []
    for w in (a["w_down"][0], a["w_ffn_out_2"][0]):
        halves.append(_column_blocks(w, d).reshape(KB, P, 2, FH * P).transpose(0, 2, 1, 3)
                      .reshape(2 * KB, P, FH * P))
    w11 = np.concatenate(halves)
    freq = np.float32(500000.0) ** (-np.arange(0, 16, 2, dtype=np.float32) / np.float32(16))
    head = np.concatenate([freq, freq, np.zeros(48, np.float32)]).astype(np.float32)
    given = {"g_mix": a["norm_mix_g"], "g_cross": a["norm_cross_g"], "g_mem": a["norm_mem_g"],
             "g_ffn": a["norm_ffn_g"], "g_final": a["norm_final_g"], "g_mix2": a["norm_mix_2"],
             "g_ffn2": a["norm_ffn_2"], "g_final2": a["norm_final_2"], "ln_g": a["ln_b_g"],
             "ln_b": a["ln_b_b"], "g_lru": a["norm_lru_out_2"], "g_att": a["norm_att_out_2"],
             "conv_w": a["conv_b_w"][0], "conv_b": a["conv_b_b"], "fconv_w": a["ffn_conv_w"][0],
             "fconv_b": a["ffn_conv_b"], "lconv_w": a["conv_w_2"][0], "lconv_b": a["conv_b_2"],
             "b_rg": a["b_rg_2"].reshape(-1), "b_ig": a["b_ig_2"].reshape(-1),
             "lam": a["lru_lambda_2"], "freq": np.concatenate([head, head])}
    params = np.ascontiguousarray(np.concatenate([_columns(given[k]) for k, _ in PARAMS], 1))
    blockdiag = np.zeros((P, 2, 4, P), np.float32)
    for r, name in enumerate(("w_rg_2", "w_ig_2")):
        for n in range(8):
            at = slice(n % 2 * HALF, n % 2 * HALF + HALF)
            blockdiag[at, r, n // 2, at] = a[name][0, n]
    arrays = {"w8": w8, "w11": w11, "x": a["x"][0], "mem": a["mem"][0],
              "positions": a["positions"][0].astype(np.int32), "params": params,
              "blockdiag": blockdiag}
    arrays = {k: np.ascontiguousarray(v) for k, v in arrays.items()}
    nc = bacc.Bacc("TRN2", target_bir_lowering=False, num_devices=1)
    aps = [nc.dram_tensor(k, v.shape, mybir.dt.from_np(v.dtype), kind="ExternalInput").ap()
           for k, v in arrays.items()]
    out = nc.dram_tensor("out", (T, D), F32, kind="ExternalOutput").ap()
    build(nc, *aps, out)
    r = run_bass_kernel_spmd(nc, [arrays], core_ids=[0])
    return r.results[0]["out"].reshape(1, T, D)
```
